# Optimizing a Trainium2 kernel written in Bass

```python
import jax, jax.numpy as jnp
from jax import lax
import numpy as np

D_MODEL = 1024
BATCH = 1
SEQ = 1024
DEPTH = 1

CHUNK = 64
Q_BLOCK = 128
MEM_LEN = 256
NORM_EPS = 1e-6

MIX_WIDTH = D_MODEL
MLA_WIDTH = MIX_WIDTH // 2
RWKV_WIDTH = MIX_WIDTH - MLA_WIDTH

MLA_HEADS = 8
MLA_V_DIM = MLA_WIDTH // MLA_HEADS
MLA_NOPE_DIM = MLA_V_DIM
MLA_ROPE_DIM = MLA_NOPE_DIM // 2
MLA_Q_RANK = 3 * D_MODEL // 16
MLA_KV_RANK = D_MODEL // 8
ROPE_THETA = 10000.0

RWKV_HEAD = 64
RWKV_HEADS = RWKV_WIDTH // RWKV_HEAD
DECAY_RANK = 32
ICL_RANK = 32
GATE_RANK = 96
VRES_RANK = 32
GN_EPS = 64e-5

CA_HEADS = 4
CA_HEAD_DIM = D_MODEL // CA_HEADS
D_FF = 4 * D_MODEL

MLA_COLS = MLA_Q_RANK + MLA_KV_RANK + MLA_ROPE_DIM
RWKV_COLS0 = 3 * RWKV_WIDTH + DECAY_RANK + ICL_RANK + GATE_RANK
RWKV_COLS = RWKV_COLS0 + VRES_RANK
IN_COLS0 = MLA_COLS + RWKV_COLS0
IN_COLS = MLA_COLS + RWKV_COLS

kernel_name = "hybrid_mla_rwkv7_stream_encoder"

def rms_norm(x, g, eps=NORM_EPS):
    xf = x.astype(jnp.float32)
    y = xf * lax.rsqrt(jnp.mean(xf * xf, axis=-1, keepdims=True) + eps)
    return (y * g.astype(jnp.float32)).astype(x.dtype)

def rope_tables(positions):
    inv = ROPE_THETA ** (-jnp.arange(0, MLA_ROPE_DIM, 2, dtype=jnp.float32) / MLA_ROPE_DIM)
    ang = positions.astype(jnp.float32)[..., None] * inv
    return jnp.cos(ang), jnp.sin(ang)

def apply_rope(x, cos, sin):
    x1, x2 = jnp.split(x.astype(jnp.float32), 2, axis=-1)
    return jnp.concatenate([x1 * cos - x2 * sin, x1 * sin + x2 * cos], axis=-1).astype(x.dtype)

def token_shift(z, mu):
    prev = jnp.pad(z, ((0, 0), (1, 0), (0, 0)))[:, :-1]
    return z + (prev - z) * mu

def chunk_causal_mla_attention(q_nope, q_rope, k_nope, k_rope, v):
    B_, S_, H, _ = q_nope.shape
    nb = S_ // Q_BLOCK
    scale = (MLA_NOPE_DIM + MLA_ROPE_DIM) ** -0.5
    key_chunk = jnp.arange(S_) // CHUNK

    def to_blocks(t):
        return jnp.moveaxis(t.reshape(B_, nb, Q_BLOCK, *t.shape[2:]), 1, 0)

    def block(args):
        qn, qr, start = args
        s = (jnp.einsum('bqhd,bkhd->bhqk', qn, k_nope, preferred_element_type=jnp.float32)
             + jnp.einsum('bqhr,bkr->bhqk', qr, k_rope, preferred_element_type=jnp.float32)) * scale
        q_chunk = (start + jnp.arange(Q_BLOCK)) // CHUNK
        s = jnp.where(key_chunk[None, :] <= q_chunk[:, None], s, -jnp.inf)
        p = jax.nn.softmax(s, axis=-1).astype(v.dtype)
        return jnp.einsum('bhqk,bkhd->bqhd', p, v)

    out = lax.map(block, (to_blocks(q_nope), to_blocks(q_rope), jnp.arange(nb) * Q_BLOCK))
    return jnp.moveaxis(out, 0, 1).reshape(B_, S_, H, v.shape[-1])

def mla_group(cols, cos, sin, q_norm, w_uq, kv_norm, w_ukv, out_norm):
    B_, S_, _ = cols.shape
    c_q = cols[..., :MLA_Q_RANK]
    c_kv = cols[..., MLA_Q_RANK:MLA_Q_RANK + MLA_KV_RANK]
    k_rope = cols[..., MLA_Q_RANK + MLA_KV_RANK:]
    q = (rms_norm(c_q, q_norm) @ w_uq).reshape(B_, S_, MLA_HEADS, MLA_NOPE_DIM + MLA_ROPE_DIM)
    q_nope = q[..., :MLA_NOPE_DIM]
    q_rope = apply_rope(q[..., MLA_NOPE_DIM:], cos[:, :, None], sin[:, :, None])
    k_rope = apply_rope(k_rope, cos, sin)
    kv = (rms_norm(c_kv, kv_norm) @ w_ukv).reshape(B_, S_, MLA_HEADS, MLA_NOPE_DIM + MLA_V_DIM)
    k_nope, v = kv[..., :MLA_NOPE_DIM], kv[..., MLA_NOPE_DIM:]
    o = chunk_causal_mla_attention(q_nope, q_rope, k_nope, k_rope, v)
    o = rms_norm(o, out_norm.reshape(MLA_HEADS, MLA_V_DIM))
    return o.reshape(B_, S_, MLA_WIDTH)

def wkv7(r, decay, k, v, a, b):
    B_, S_, H, N = r.shape
    xs = tuple(jnp.swapaxes(t.astype(jnp.float32), 0, 1) for t in (r, decay, k, v, a, b))

    def step(state, inp):
        rt, wt, kt, vt, at, bt = inp
        sa = jnp.einsum('bhvk,bhk->bhv', state, at)
        state = state * wt[:, :, None, :] + sa[..., None] * bt[:, :, None, :] + vt[..., None] * kt[:, :, None, :]
        return state, jnp.einsum('bhvk,bhk->bhv', state, rt)

    s0 = jnp.zeros((B_, H, N, N), jnp.float32)
    _, ys = lax.scan(step, s0, xs)
    return jnp.swapaxes(ys, 0, 1)

def rwkv7_group(cols, w0, w2, a0, a2, g2, k_k, k_a, r_k, ln_w, ln_b, v_first, v0, v2):
    B_, S_, _ = cols.shape
    RW, H, N = RWKV_WIDTH, RWKV_HEADS, RWKV_HEAD
    r = cols[..., :RW]
    k = cols[..., RW:2 * RW]
    v = cols[..., 2 * RW:3 * RW]
    o = 3 * RW
    w_l = cols[..., o:o + DECAY_RANK]
    o += DECAY_RANK
    a_l = cols[..., o:o + ICL_RANK]
    o += ICL_RANK
    g_l = cols[..., o:o + GATE_RANK]
    o += GATE_RANK

    w_log = -jax.nn.softplus(-(w0 + jnp.tanh(w_l) @ w2)) - 0.5
    decay = jnp.exp(-jnp.exp(w_log.astype(jnp.float32)))
    a = jax.nn.sigmoid(a0 + a_l @ a2)
    g = jax.nn.sigmoid(g_l) @ g2
    if v0 is None:
        v_first = v
    else:
        v_l = cols[..., o:o + VRES_RANK]
        v = v + (v_first - v) * jax.nn.sigmoid(v0 + v_l @ v2)

    heads = lambda t: t.reshape(B_, S_, H, N)
    kk = heads(k * k_k).astype(jnp.float32)
    kk = kk / jnp.maximum(jnp.sqrt(jnp.sum(kk * kk, axis=-1, keepdims=True)), 1e-12)
    k = k * (1.0 + (a - 1.0) * k_a)
    rh, kh, vh, ah = heads(r), heads(k), heads(v), heads(a)
    y = wkv7(rh, heads(decay), kh, vh, -kk, kk * ah)

    mu = jnp.mean(y, axis=-1, keepdims=True)
    var = jnp.mean(jnp.square(y - mu), axis=-1, keepdims=True)
    y = (y - mu) * lax.rsqrt(var + GN_EPS) * ln_w.reshape(H, N) + ln_b.reshape(H, N)
    y = y + jnp.sum(rh * kh * r_k, axis=-1, keepdims=True) * vh
    out = (y.reshape(B_, S_, RW) * g).astype(cols.dtype)
    return out, v_first

def mem_cross_attention(hn, mem_n, wq, wkv, wo):
    B_, S_, _ = hn.shape
    M = mem_n.shape[1]
    q = (hn @ wq).reshape(B_, S_, CA_HEADS, CA_HEAD_DIM)
    kv = (mem_n @ wkv).reshape(B_, M, 2, CA_HEADS, CA_HEAD_DIM)
    k, v = kv[:, :, 0], kv[:, :, 1]
    s = jnp.einsum('bshd,bmhd->bhsm', q, k, preferred_element_type=jnp.float32) * (CA_HEAD_DIM ** -0.5)
    p = jax.nn.softmax(s, axis=-1).astype(v.dtype)
    o = jnp.einsum('bhsm,bmhd->bshd', p, v).reshape(B_, S_, D_MODEL)
    return o @ wo

def squared_relu_mlp(hn, w_up, w_down):
    return jnp.square(jax.nn.relu(hn @ w_up)) @ w_down

def setup_inputs(seed: int = 0) -> dict:
    key = jax.random.key(seed)
    keys = iter(jax.random.split(key, 64))
    f32 = jnp.float32

    def nrm(shape, scale):
        return scale * jax.random.normal(next(keys), shape, f32)

    def gain(shape):
        return 1.0 + nrm(shape, 0.02)

    L, L1 = DEPTH, DEPTH - 1
    RW = RWKV_WIDTH
    x = jax.random.normal(next(keys), (BATCH, SEQ, D_MODEL), f32)
    mem = jax.random.normal(next(keys), (BATCH, MEM_LEN, D_MODEL), f32)
    start = jax.random.randint(next(keys), (BATCH, 1), 0, 64) * CHUNK
    positions = (start + jnp.arange(SEQ)[None, :]).astype(jnp.int32)

    n = jnp.arange(RW, dtype=f32) / (RW - 1)
    decay_speed = -7.0 + 5.0 * n ** 0.85 + 0.5
    w0 = decay_speed[None, :] + nrm((L, RW), 0.1)

    return {
        "x": x,
        "mem": mem,
        "positions": positions,
        "mix_norm": gain((L, D_MODEL)),
        "w_in_first": nrm((D_MODEL, IN_COLS0), D_MODEL ** -0.5),
        "w_in_rest": nrm((L1, D_MODEL, IN_COLS), D_MODEL ** -0.5),
        "shift_mu_first": jax.random.uniform(next(keys), (RWKV_COLS0,), f32, 0.2, 0.8),
        "shift_mu_rest": jax.random.uniform(next(keys), (L1, RWKV_COLS), f32, 0.2, 0.8),
        "mla_q_norm": gain((L, MLA_Q_RANK)),
        "mla_w_uq": nrm((L, MLA_Q_RANK, MLA_HEADS * (MLA_NOPE_DIM + MLA_ROPE_DIM)), MLA_Q_RANK ** -0.5),
        "mla_kv_norm": gain((L, MLA_KV_RANK)),
        "mla_w_ukv": nrm((L, MLA_KV_RANK, MLA_HEADS * (MLA_NOPE_DIM + MLA_V_DIM)), MLA_KV_RANK ** -0.5),
        "mla_out_norm": gain((L, MLA_WIDTH)),
        "rwkv_w0": w0,
        "rwkv_w2": nrm((L, DECAY_RANK, RW), 0.1 * DECAY_RANK ** -0.5),
        "rwkv_a0": nrm((L, RW), 0.1),
        "rwkv_a2": nrm((L, ICL_RANK, RW), 0.5 * ICL_RANK ** -0.5),
        "rwkv_g2": nrm((L, GATE_RANK, RW), GATE_RANK ** -0.5),
        "rwkv_v0": 1.0 + nrm((L1, RW), 0.1),
        "rwkv_v2": nrm((L1, VRES_RANK, RW), 0.5 * VRES_RANK ** -0.5),
        "rwkv_k_k": 0.85 + nrm((L, RW), 0.02),
        "rwkv_k_a": 1.0 + nrm((L, RW), 0.02),
        "rwkv_r_k": nrm((L, RWKV_HEADS, RWKV_HEAD), 0.1),
        "rwkv_ln_w": gain((L, RW)),
        "rwkv_ln_b": nrm((L, RW), 0.02),
        "w_out": nrm((L, MIX_WIDTH, D_MODEL), MIX_WIDTH ** -0.5),
        "ca_norm": gain((L, D_MODEL)),
        "mem_norm": gain((D_MODEL,)),
        "ca_wq": nrm((L, D_MODEL, D_MODEL), D_MODEL ** -0.5),
        "ca_wkv": nrm((L, D_MODEL, 2 * D_MODEL), D_MODEL ** -0.5),
        "ca_wo": nrm((L, D_MODEL, D_MODEL), D_MODEL ** -0.5),
        "mlp_norm": gain((L, D_MODEL)),
        "mlp_w_up": nrm((L, D_MODEL, D_FF), D_MODEL ** -0.5),
        "mlp_w_down": nrm((L, D_FF, D_MODEL), D_FF ** -0.5),
        "final_norm": gain((D_MODEL,)),
    }

def reference(x, mem, positions, mix_norm, w_in_first, w_in_rest, shift_mu_first, shift_mu_rest,
              mla_q_norm, mla_w_uq, mla_kv_norm, mla_w_ukv, mla_out_norm,
              rwkv_w0, rwkv_w2, rwkv_a0, rwkv_a2, rwkv_g2, rwkv_v0, rwkv_v2,
              rwkv_k_k, rwkv_k_a, rwkv_r_k, rwkv_ln_w, rwkv_ln_b, w_out,
              ca_norm, mem_norm, ca_wq, ca_wkv, ca_wo,
              mlp_norm, mlp_w_up, mlp_w_down, final_norm):
    cos, sin = rope_tables(positions)
    mem_n = rms_norm(mem, mem_norm)
    h = x
    v_first = None
    for l in range(DEPTH):
        if l == 0:
            w_in, mu, v0, v2 = w_in_first, shift_mu_first, None, None
        else:
            w_in, mu, v0, v2 = w_in_rest[l - 1], shift_mu_rest[l - 1], rwkv_v0[l - 1], rwkv_v2[l - 1]
        proj = rms_norm(h, mix_norm[l]) @ w_in
        att = mla_group(proj[..., :MLA_COLS], cos, sin, mla_q_norm[l], mla_w_uq[l],
                        mla_kv_norm[l], mla_w_ukv[l], mla_out_norm[l])
        rw, v_first = rwkv7_group(token_shift(proj[..., MLA_COLS:], mu),
                                  rwkv_w0[l], rwkv_w2[l], rwkv_a0[l], rwkv_a2[l], rwkv_g2[l],
                                  rwkv_k_k[l], rwkv_k_a[l], rwkv_r_k[l], rwkv_ln_w[l], rwkv_ln_b[l],
                                  v_first, v0, v2)
        h = h + jnp.concatenate([att, rw], axis=-1) @ w_out[l]
        h = h + mem_cross_attention(rms_norm(h, ca_norm[l]), mem_n, ca_wq[l], ca_wkv[l], ca_wo[l])
        h = h + squared_relu_mlp(rms_norm(h, mlp_norm[l]), mlp_w_up[l], mlp_w_down[l])
    return rms_norm(h, final_norm)


_drawn_inputs = setup_inputs


def setup_inputs(seed=0):
    import zlib

    import numpy as np

    out = dict(_drawn_inputs(seed))
    spreads = {}
    factors = {'mix_norm': 2.684,
     'mla_q_norm': 4.763,
     'mla_kv_norm': 2.709,
     'mla_out_norm': 4.824,
     'rwkv_w2': 8.0,
     'rwkv_a0': 4.03,
     'rwkv_k_k': 8.0,
     'rwkv_k_a': 7.968,
     'rwkv_ln_w': 8.0,
     'rwkv_ln_b': 8.0,
     'ca_norm': 8.0,
     'mem_norm': 8.0,
     'mlp_norm': 11.729,
     'final_norm': 8.114}
    for name, (base, spread) in spreads.items():
        noise = np.random.default_rng([zlib.crc32(name.encode()), seed]).standard_normal(out[name].shape)
        drawn = base * np.exp(spread * noise) if base else spread * noise
        out[name] = __import__('jax').numpy.asarray(drawn.astype(out[name].dtype))
    for name, factor in factors.items():
        out[name] = (out[name] * factor).astype(out[name].dtype)
    return out
```

```python
from contextlib import ExitStack
import math

import numpy as np

import concourse.bass as bass
from concourse import mybir

F32 = mybir.dt.float32
F32R = mybir.dt.float32r
I32 = mybir.dt.int32
ACT = mybir.ActivationFunctionType
ALU = mybir.AluOpType
AX_X = mybir.AxisListType.X

P = 128
D = 1024
S = 1024
KT = D // P
NW = S // P
HALF = 512
MEM = 256
CH = 64
NC = S // CH
HD = 64
MLA_HEADS = 8
PAIRS = 4
CA_HEADS = 4
QR, KVR, ROPE = 192, 128, 32
EPS = 1e-6
GN_EPS = 64e-5
EXPM05 = math.exp(-0.5)
MLA_SCALE = (HD + ROPE) ** -0.5
CA_SCALE = 256 ** -0.5
MAGIC = 12582912.0

T_CQ, T_CQWA, T_CKV, T_GK, T_R, T_K, T_V = 0, 1, 2, 3, 4, 8, 12

V_MIX, V_CA, V_MLP, V_FIN, V_MEM, V_MU = 0, 8, 16, 24, 32, 40
V_QN, V_KVN, V_ON = 56, 58, 59
V_W0, V_A0, V_KK, V_KA, V_RK, V_LW, V_LB = 63, 67, 71, 75, 79, 83, 87
NV = 91

C_ID, C_MS, C_ML, C_BQ, C_B0, C_B0T, C_SEL, C_E1, C_E2, C_BO, C_BM = (
    0, 128, 640, 768, 1408, 1536, 1664, 1920, 2048, 2176, 2304)
C_HO, C_ONE, C_INV, C_SGN, C_RA, C_RB, C_NH = 2432, 2434, 2435, 2436, 2437, 2565, 2693
C_PI2, C_EM, C_EP = 2709, 2710, 2711
NCON = 2712

U_IN, U_OUT, U_MK, U_MV, U_Q, U_O, U_MLP = 0, 16, 24, 32, 40, 48, 56
UNITS = U_MLP + 64


def constants():
    c = np.zeros((P, NCON), np.float32)
    i = np.arange(P)
    part, free = i[:, None], i[None, :]
    same = part // CH == free // CH
    c[:, C_ID:C_ID + P] = np.eye(P)
    for n in range(2):
        c[:, C_MS + 256 * n:C_MS + 256 * n + P] = same & (part < free)
        c[:, C_MS + 256 * n + P:C_MS + 256 * n + 2 * P] = same & (part <= free)
    c[:, C_ML:C_ML + P] = same & (free < part)
    for n in range(5):
        m = 2 << n
        c[:, C_BQ + P * n:C_BQ + P * n + P] = (
            (part // (2 * m) == free // (2 * m)) & (part % (2 * m) < m) & (free % (2 * m) >= m))
    c[:, C_B0:C_B0 + P] = (part % 2 == 1) & (free == part - 1)
    c[:, C_B0T:C_B0T + P] = (free % 2 == 1) & (part == free - 1)
    for h in range(2):
        c[:, C_SEL + P * h:C_SEL + P * h + P] = (free < HD) & (part == free + HD * h)
    r = np.arange(ROPE)
    half = ROPE // 2
    for base in (64, 96):
        c[96 + r, C_E1 + base + r] = 1.0
        c[96 + half + r[:half], C_E2 + base + r[:half]] = -1.0
        c[96 + r[:half], C_E2 + base + half + r[:half]] = 1.0
    c[:, C_BO:C_BO + P] = same
    c[:, C_BM:C_BM + P] = same / HD
    c[:, C_HO:C_HO + 2] = part // HD == free[:, :2]
    c[:, C_ONE] = 1.0
    inv = (10000.0 ** (-np.arange(0, ROPE, 2) / ROPE)).astype(np.float32)
    c[:, C_INV] = inv[i % half]
    c[:, C_SGN] = np.where(i % ROPE < half, -1.0, 1.0)
    c[0, C_RA:C_RA + P] = i < CH
    c[0, C_RB:C_RB + P] = np.where(i >= CH, -1e30, 0.0)
    c[:, C_NH:C_NH + 16] = -0.5
    c[:, C_PI2] = math.pi / 2
    c[:, C_EM] = -0.5 * EXPM05
    c[:, C_EP] = 0.5 * EXPM05
    return c


class Steps:

    def __init__(self, semaphore, names):
        self.sem, self.names, self.n = semaphore, names, len(names)
        self.pos = {name: i + 1 for i, name in enumerate(names)}
        assert len(self.pos) == self.n
        self.next = 0

    def at(self, name, turn=0):
        return (turn + 1) * self.n + self.pos[name]

    def one(self, name):
        assert self.names[self.next % self.n] == name, (self.names[self.next % self.n], name)
        self.next += 1
        return 1


def build(nc, x_t, mem_t, pos, wall, vecs, con_d, headw, wv_d, lora_d, out_t):
    with ExitStack() as ctx:
        def sb(name, shape, dt=F32):
            return ctx.enter_context(nc.sbuf_tensor(name, shape, dt))

        def overlay(*specs):
            made, size = [], 0
            for name, shape, dt in specs:
                with nc.sbuf_tensor(name, shape, dt) as t:
                    made.append(t)
                size = max(size, int(np.prod(shape[1:])))
            sb(specs[0][0] + "_place", [P, size])
            return made

        def sem(name):
            return ctx.enter_context(nc.semaphore(name))

        xn, sa = overlay(("xn", [P, KT, 2, S], F32R), ("sa", [P, 16384], F32))
        proj, hid, sbx, memr = overlay(("proj", [P, 16, S], F32), ("hid", [P, KT, 2, S], F32R),
                                       ("sbx", [P, 16384], F32), ("memr", [P, 16384], F32R))
        H = sb("H", [P, KT, S])
        wraw, sc_w = overlay(("wraw", [P, 2, KT * P], F32), ("sc_w", [P, 2048], F32))
        wsp, sc_s = overlay(("wsp", [P, 2, KT, 2, P], F32R), ("sc_s", [P, 4096], F32))
        con = sb("con", [P, NCON])
        vec = sb("vec", [P, NV])
        omu = sb("omu", [P, 16])
        vech = sb("vech", [P, 12])
        small = sb("small", [P, 64])
        tmp = sb("tmp", [P, 2, S])
        ssum = sb("ssum", [P, S])

        ident = con[:, C_ID:C_ID + P]
        PS = ctx.enter_context(nc.psum_tensor("PS", [P, 8, HALF], F32))

        def two(b):
            return PS[:, b:b + 2, :].rearrange("p a n -> p (a n)")

        def win(w):
            return slice(P * w, P * w + P)

        mV = sa[:, 0:4096].rearrange("p (w n) -> p w n", w=NW)
        mO = sa[:, 4096:8192].rearrange("p (w n) -> p w n", w=NW)
        mQ = sa[:, 8192:9216]
        mK = sa[:, 9216:10240]
        mP = [sa[:, 10240:11264], sa[:, 11264:12288]]
        mPT = [sa[:, 12288:13312], ssum[:, :]]
        mCS = sa[:, 13312:14336]
        mCos = sa[:, 14336:15360]
        mSin = sa[:, 15360:16384]
        mT = [tmp[:, 0, :], tmp[:, 1, :]]
        mOsq = sa[:, 8192:12288]
        mSt = sa[:, 12288:12352]
        headw_sb = sc_s[:, 0:320]
        wv_sb = sc_s[:, 512:1024]
        posi = sc_w[:, 0:1024].bitcast(I32)

        rAR = sa[:, 0:2048].rearrange("p (w a t) -> p w a t", w=NW, a=2)
        rB = sa[:, 2048:3072]
        rK = sa[:, 3072:4096]
        rBh = sa[:, 4096:5120]
        rKh = sa[:, 5120:6144]
        rW = sa[:, 6144:7168]
        rWi = sa[:, 7168:8192]
        rT1, rT2, rT3 = (sa[:, 8192 + 1024 * n:9216 + 1024 * n] for n in range(3))
        rG = sa[:, 11264:12288]
        rBV = sa[:, 12288:13312]
        rY = sa[:, 13312:14336]
        rMT = sa[:, 14336:16384].rearrange("p (c h n) -> p c h n", c=NC, h=2)
        rSC = [proj[:, t, :].rearrange("p (h k n) -> p h k n", h=2, k=4) for t in (T_CQ, T_CKV)]
        rXX = [sc_w[:, 1024 * n:1024 * n + 512].rearrange("p (a h n) -> p a h n", a=2, h=2) for n in range(2)]
        rAL = [sc_w[:, 1024 * n + 512:1024 * n + 768].rearrange("p (h n) -> p h n", h=2) for n in range(2)]
        rQ = [sc_w[:, 1024 * n + 768:1024 * n + 1024].rearrange("p (h n) -> p h n", h=2) for n in range(2)]

        def wbuf(n, k):
            return sc_s[:, 1536 * n + 256 * k:1536 * n + 256 * k + 256]

        rAG, rBK, rVZ, rPG, rRY = ([wbuf(n, k).rearrange("p (h n) -> p h n", h=2) for n in range(2)]
                                   for k in range(5))
        lora = sc_s[:, 3072:3456]
        rST = tmp[:, :, :].rearrange("p a (c h n) -> p (a c) h n", h=2, n=HD)
        rWT = small[0:HD, 32:64].rearrange("p (c h) -> p c h", h=2)

        cQ = sbx[:, 0:8192].rearrange("p (k t) -> p k t", k=KT)
        cMem = sbx[:, 0:2048].rearrange("p (k t) -> p k t", k=KT)
        cMt = sbx[:, 2048:4096].rearrange("p (k t) -> p k t", k=KT)
        cMs = sbx[:, 4096:4352]
        cK = sbx[:, 8192:10240].rearrange("p (k t) -> p k t", k=KT)
        cV = sbx[:, 10240:12288].rearrange("p (k t) -> p k t", k=2)
        memn = memr[:, 12288:16384].rearrange("p (k a t) -> p k a t", k=KT, a=2)
        cVh = sbx[:, 12288:12800].rearrange("p (k n) -> p k n", k=2)
        cP = [sbx[:, 12800 + 256 * n:13056 + 256 * n] for n in range(2)]
        cPT = [sbx[:, 13312 + 1024 * n:14336 + 1024 * n].rearrange("p (k q) -> p k q", k=2) for n in range(2)]
        cQh = tmp[:, :, :]

        con_loaded, vec_loaded = sem("con_loaded"), sem("vec_loaded")
        x_loaded = [sem(f"x_loaded{k}") for k in range(KT)]
        raw_loaded = [sem("raw_loaded0"), sem("raw_loaded1")]
        pos_loaded, wv_loaded, headw_loaded = sem("pos_loaded"), sem("wv_loaded"), sem("headw_loaded")
        lora_loaded, mem_loaded = sem("lora_loaded"), sem("mem_loaded")
        stored = sem("stored")
        vec_made = sem("vec_made")
        w_split = sem("w_split")
        w_head = sem("w_head")
        acc_ready = sem("acc_ready")
        acc_free = sem("acc_free")
        proj_part = sem("proj_part")
        sq_ready = sem("sq_ready")
        sq_added = sem("sq_added")
        nsum_ready, var_ready, std_ready, rstd_ready, nb_ready = (
            sem("nsum_ready"), sem("var_ready"), sem("std_ready"), sem("rstd_ready"), sem("nb_ready"))
        scaled = sem("scaled")
        head_ready = sem("head_ready")
        xn_ready = sem("xn_ready")
        h_added = sem("h_added")
        ssum_zero = sem("ssum_zero")
        pool_turn = sem("pool_turn")
        relu_ready, hsq_ready, hhead_ready, hid_ready = (
            sem("relu_ready"), sem("hsq_ready"), sem("hhead_ready"), sem("hid_ready"))
        ca_hi, ca_lo = sem("ca_hi"), sem("ca_lo")
        out_scaled = sem("out_scaled")

        MP_ACT = Steps(sem("mla_pre_act"), ["sq1", "sq2", "sq3", "sin", "cos", "std"] + [f"v{w}" for w in range(NW)])
        MP_DVE = Steps(sem("mla_pre_dve"), ["posf", "ang", "turns", "m1", "r1", "m2", "r2", "clamp", "abs",
                                            "var1", "var", "rstd", "one", "csc", "css", "kr1", "kr2", "kr",
                                            "cq0", "cq1", "ckv"])
        MP_PE = Steps(sem("mla_pre_pe"), ["e12", "sums", "bq", "bkv"] + [f"v{w}" for w in range(NW)])
        qn = range(NW)
        M_PE = Steps(sem("mla_pe"), ["q", "k", "s0", "s1", "t0"]
                     + [x for q in range(2, NW) for x in (f"s{q}", f"t{q - 1}", f"o{q - 2}")]
                     + ["t7", "o6", "o7"])
        M_ACT = Steps(sem("mla_act"), ["k"] + [f"e{q}" for q in qn])
        M_DVE = Steps(sem("mla_dve"), ["q", "m0", "b0", "m1", "b1", "t0"]
                      + [x for q in range(2, NW) for x in (f"m{q}", f"b{q}", f"t{q - 1}", f"r{q - 2}", f"o{q - 2}")]
                      + ["t7", "r6", "o6", "r7", "o7"])
        mo_dve, mo_act, mo_pe = sem("mla_out_dve"), sem("mla_out_act"), sem("mla_out_pe")
        rp_act, rp_dve = sem("rwkv_set_act"), sem("rwkv_set_dve")

        pe_names = ["lw", "la", "lg", "kks", "kkb", "rk"]
        act_names = ["tw", "dec", "dnv", "ta", "g", "kksq", "afirst", "wt0", "wt1", "vc"]
        dve_names = ["kk", "zb", "zk", "zm", "nw", "dinv", "f1", "f2", "z1", "z2", "W", "Wi", "kkm", "nkk", "at", "na", "b", "bt",
                     "am", "k2", "kt", "rt", "rk", "bv"]
        pool_names = ["pow", "bh", "kh", "dg"]
        for g in range(NW // 2):
            ab = (2 * g, 2 * g + 1)
            for w in ab:
                pe_names += [f"sc{w}", f"al{w}"]
                dve_names += [f"sc0_{w}", f"sc1_{w}", f"al0_{w}", f"al1_{w}"]
                pool_names += [f"x_{w}", f"xt_{w}", f"xi_{w}"]
            for w in ab:
                pe_names += [f"tok{w}"]
                act_names += [f"ag{w}", f"bk{w}", f"vz{w}"]
            for w in ab:
                pe_names += [f"akv{w}"]
                act_names += [f"akv{w}"]
            for lv in range(5):
                pe_names += [f"q{lv}_{w}" for w in ab] + [f"z{lv}_{w}" for w in ab]
                dve_names += [f"q{lv}_{w}" for w in ab] + [f"z{lv}_{w}" for w in ab]
            for st in ("pg", "ry"):
                pe_names += [f"{st}{w}" for w in ab]
                act_names += [f"{st}{w}" for w in ab]
            pe_names += [f"mn{w}" for w in ab]
            for w in ab:
                dve_names += [f"mt0_{w}", f"mt1_{w}"]
            for w in ab:
                for c in (2 * w, 2 * w + 1):
                    if c < NC - 1:
                        pe_names += [f"st{c}"]
                        dve_names += [f"st{c}"]
                    pe_names += [f"y{c}"]
                act_names += [f"y{w}"]
        pe_names += ["mean", "vs", "vb"]
        act_names += ["ysq"]
        dve_names += ["yc", "var", "yn", "yl", "yb", "out"]
        pool_names += ["gpow"]
        R_PE, R_ACT, R_DVE, R_POOL = (Steps(sem("rwkv_pe"), pe_names), Steps(sem("rwkv_act"), act_names),
                                      Steps(sem("rwkv_dve"), dve_names), Steps(sem("rwkv_pool"), pool_names))

        mm_act, mm_dve, mm_pe = sem("mem_act"), sem("mem_dve"), sem("mem_pe")
        ca_stage = sem("ca_stage")
        C_PE = Steps(sem("ca_pe"), ["s0"] + [x for q in range(1, NW) for x in
                                             ([f"s{q}", f"t{q - 1}"] + (["o0"] if q == 5 else []))] + ["t7", "o1"])
        C_ACT = Steps(sem("ca_act"), [x for q in range(NW) for x in
                                      ([f"e{q}"] + (["h00", "h01"] if q == 6 else []))] + ["h10", "h11"])
        C_DVE = Steps(sem("ca_dve"), ["m0", "b0"]
                      + [x for q in range(1, NW) for x in
                         ([f"m{q}", f"b{q}", f"r{q - 1}", f"p{q - 1}", f"t{q - 1}"] + (["l00", "l01"] if q == 6 else []))]
                      + ["r7", "p7", "t7", "l10", "l11"])
        STEPS = (MP_ACT, MP_DVE, MP_PE, M_PE, M_ACT, M_DVE, R_PE, R_ACT, R_DVE, R_POOL, C_PE, C_ACT, C_DVE)

        block = ctx.enter_context(nc.Block())

        @block.sync
        def _(sp):
            def weights(u0, n):
                with sp.Fori(0, n // 2) as i:
                    for k in range(2):
                        sp.wait_ge(w_split, 2 * i + (u0 + k + 1))
                        sp.dma_start(wraw[:, k, :], wall[bass.ds(2 * i + (u0 + k), 1)].rearrange(
                            "a p n -> (a p) n")).then_inc(raw_loaded[k], 16)

            for kt in range(KT):
                sp.dma_start(H[:, kt, :], x_t[kt]).then_inc(x_loaded[kt], 16)
            sp.dma_start(vec[:, :], vecs).then_inc(vec_loaded, 16)
            sp.dma_start(con[:, :], con_d).then_inc(con_loaded, 16)
            weights(U_IN, 16)

            sp.wait_ge(acc_ready, U_OUT + 2)
            sp.dma_start(posi, pos.broadcast_to([P, S])).then_inc(pos_loaded, 16)
            sp.dma_start(wv_sb, wv_d).then_inc(wv_loaded, 16)
            with sp.Fori(0, MLA_HEADS) as h:
                sp.wait_ge(M_PE.sem, M_PE.at("k", h - 1))
                sp.dma_start(headw_sb, headw[bass.ds(h, 1)].rearrange("a p n -> (a p) n")).then_inc(headw_loaded, 16)

            with sp.Fori(0, PAIRS) as p:
                sp.wait_ge(R_PE.sem, R_PE.at("lg", p - 1))
                sp.dma_start(lora, lora_d[bass.ds(p, 1)].rearrange("a p n -> (a p) n")).then_inc(lora_loaded, 16)

            sp.wait_ge(R_DVE.sem, R_DVE.at("out", PAIRS - 1))
            sp.dma_start(cMem, mem_t.rearrange("k p t -> p k t")).then_inc(mem_loaded, 16)
            weights(U_OUT, 2)
            for kt in range(KT):
                sp.wait_ge(xn_ready, KT + kt + 1)
                sp.dma_start(H[:, kt, :], x_t[kt]).then_inc(x_loaded[kt], 16)
            weights(U_OUT + 2, UNITS - U_OUT - 2)

            for kt in range(KT):
                sp.wait_ge(out_scaled, kt + 1)
                sp.dma_start(out_t[kt], proj[:, kt, :]).then_inc(stored, 16)
            sp.wait_ge(stored, 16 * KT)

        @block.gpsimd
        def _(pool):
            def split_weights(u0, n):
                with pool.Fori(0, n // 2) as i:
                    for k in range(2):
                        raw = wraw[:, k, :].rearrange("p (k n) -> p k n", k=KT)
                        pool.wait_ge(raw_loaded[k], 16 * (i + (u0 // 2 + 1)))
                        pool.wait_ge(acc_ready, 2 * i + (u0 + k + 1))
                        nc.gpsimd.sem_inc(pool_turn, 1)
                        nc.gpsimd.tensor_copy(wsp[:, k, :, 0, :], raw).then_inc(w_head, 1)
                        pool.wait_ge(w_head, 2 * i + (u0 + k + 1))
                        nc.gpsimd.tensor_tensor(wsp[:, k, :, 1, :], raw, wsp[:, k, :, 0, :].bitcast(F32),
                                                ALU.subtract).then_inc(w_split, 1)

            nc.gpsimd.sem_inc(w_split, 2)
            nc.gpsimd.sem_inc(R_POOL.sem, R_POOL.n)
            split_weights(U_IN, 16)

            with pool.Fori(0, PAIRS) as p:
                pool.wait_ge(R_DVE.sem, R_DVE.at("kkm", p))
                nc.gpsimd.tensor_tensor(small[:, 16:32], small[:, 0:16], con[:, C_NH:C_NH + 16],
                                        ALU.pow).then_inc(R_POOL.sem, R_POOL.one("pow"))
                wt = rW.rearrange("p (c t) -> p c t", c=NC)[:, :, CH - 1:CH].broadcast_to([P, NC, CH])
                pool.wait_ge(R_DVE.sem, R_DVE.at("bt", p))
                nc.gpsimd.tensor_tensor(rBh.rearrange("p (c t) -> p c t", c=NC),
                                        rB.rearrange("p (c t) -> p c t", c=NC), wt,
                                        ALU.mult).then_inc(R_POOL.sem, R_POOL.one("bh"))
                pool.wait_ge(R_DVE.sem, R_DVE.at("kt", p))
                nc.gpsimd.tensor_tensor(rKh.rearrange("p (c t) -> p c t", c=NC),
                                        rK.rearrange("p (c t) -> p c t", c=NC), wt,
                                        ALU.mult).then_inc(R_POOL.sem, R_POOL.one("kh"))
                pool.wait_ge(R_ACT.sem, R_ACT.at("wt1", p))
                nc.gpsimd.tensor_tensor(
                    rMT[0:HD], ident[0:HD, 0:HD].rearrange("p (a b n) -> p a b n", a=1, b=1).broadcast_to([HD, NC, 2, HD]),
                    rWT.rearrange("p c (h n) -> p c h n", n=1).broadcast_to([HD, NC, 2, HD]),
                    ALU.mult).then_inc(R_POOL.sem, R_POOL.one("dg"))
                for w in range(NW):
                    s = w % 2
                    b0 = con[:, C_B0:C_B0 + P].rearrange("p (a n) -> p a n", a=1).broadcast_to([P, 2, P])
                    b0t = con[:, C_B0T:C_B0T + P].rearrange("p (a n) -> p a n", a=1).broadcast_to([P, 2, P])
                    idb = ident.rearrange("p (a n) -> p a n", a=1).broadcast_to([P, 4, P])
                    if w >= 2:
                        pool.wait_ge(R_PE.sem, R_PE.at(f"pg{w - 2}", p))
                    pool.wait_ge(R_DVE.sem, R_DVE.at(f"al1_{w}", p))
                    nc.gpsimd.tensor_tensor(rXX[s][:, 0], rAL[s], b0, ALU.mult).then_inc(
                        R_POOL.sem, R_POOL.one(f"x_{w}"))
                    nc.gpsimd.tensor_tensor(rXX[s][:, 1], rSC[s][:, :, 0, :], b0t, ALU.mult).then_inc(
                        R_POOL.sem, R_POOL.one(f"xt_{w}"))
                    pool.wait_ge(R_POOL.sem, R_POOL.at(f"xt_{w}", p))
                    xx = rXX[s].rearrange("p a h n -> p (a h) n")
                    nc.gpsimd.tensor_tensor(xx, xx, idb, ALU.add).then_inc(R_POOL.sem, R_POOL.one(f"xi_{w}"))
                pool.wait_ge(R_DVE.sem, R_DVE.at("var", p))
                nc.gpsimd.tensor_tensor(small[:, 16:32], small[:, 0:16], con[:, C_NH:C_NH + 16],
                                        ALU.pow).then_inc(R_POOL.sem, R_POOL.one("gpow"))

            pool.wait_ge(R_PE.sem, R_PE.at("vb", PAIRS - 1))
            split_weights(U_OUT, U_O - U_OUT)

            with pool.Fori(0, CA_HEADS) as h:
                pool.wait_ge(C_PE.sem, C_PE.at("o1", h - 1))
                pool.wait_ge(acc_free, U_O + 2)
                pool.wait_ge(xn_ready, 3 * KT)
                nc.gpsimd.sem_inc(pool_turn, 1)
                for k in range(2):
                    nc.gpsimd.tensor_copy(cQh[:, k, :], cQ[:, bass.ds(2 * h + k, 1), :].rearrange(
                        "p a t -> p (a t)")).then_inc(ca_stage, 1)
                    nc.gpsimd.tensor_copy(cVh[:, k, :], cV[:, k, bass.ds(256 * h, 256)]).then_inc(ca_stage, 1)
            split_weights(U_O, UNITS - U_O)

        @block.tensor
        def _(pe):
            nc.tensor.sem_inc(acc_ready, 2)
            for st in (M_PE, R_PE, C_PE):
                nc.tensor.sem_inc(st.sem, st.n)

            def gemm(u0, n, src, ready):
                with pe.Fori(0, n // 2) as i:
                    for k in range(2):
                        unit(2 * i + (u0 + k), k, src, ready)

            def unit(u, k, src, ready):
                pe.wait_ge(w_split, u + 3)
                pe.wait_ge(acc_free, u + 1)
                for kt in range(KT):
                    ready(kt)
                    for a, b in ((0, 0), (0, 1), (1, 0)):
                        for half in range(2):
                            last = nc.tensor.matmul(
                                PS[:, 2 * k + half, :], wsp[:, k, kt, a, :],
                                src[:, kt, b, HALF * half:HALF * half + HALF],
                                start=(kt == 0 and (a, b) == (0, 0)), stop=(kt == KT - 1 and a == 1))
                last.then_inc(acc_ready, 1)

            def norm(n):
                pe.wait_ge(sq_added, KT * (n + 1))
                for w in range(NW):
                    last = nc.tensor.matmul(PS[:, 4, w:w + 1], ssum[:, win(w)], con[:, C_ONE:C_ONE + 1],
                                            start=True, stop=True)
                last.then_inc(nsum_ready, 1)
                pe.wait_ge(rstd_ready, n + 1)
                for w in range(NW):
                    last = nc.tensor.matmul(PS[:, 5 + w // 4, P * (w % 4):P * (w % 4) + P],
                                            small[:, 16 + w:17 + w].broadcast_to([P, P]), ident,
                                            start=True, stop=True)
                last.then_inc(nb_ready, 1)

            def split_ready(n):
                return lambda kt: pe.wait_ge(xn_ready, KT * n + kt + 1)

            pe.wait_ge(con_loaded, 16)
            norm(0)
            gemm(U_IN, 16, xn, split_ready(0))

            pe.wait_ge(acc_free, U_OUT + 2)
            for half in range(2):
                hs = slice(HALF * half, HALF * half + HALF)
                nc.tensor.matmul(PS[:, half, :], con[96:P, C_E1:C_E1 + P], proj[96:P, T_GK, hs], start=True, stop=True)
                last = nc.tensor.matmul(PS[:, 2 + half, :], con[96:P, C_E2:C_E2 + P], proj[96:P, T_GK, hs],
                                        start=True, stop=True)
            last.then_inc(MP_PE.sem, MP_PE.one("e12"))
            pe.wait_ge(MP_ACT.sem, MP_ACT.at("sq3", -1))
            for w in range(NW):
                nc.tensor.matmul(PS[:, 4, w:w + 1], mQ[:, win(w)], con[:, C_ONE:C_ONE + 1], start=True, stop=False)
                nc.tensor.matmul(PS[:, 4, w:w + 1], mK[0:HD, win(w)], con[0:HD, C_ONE:C_ONE + 1], start=False, stop=True)
            for w in range(NW):
                last = nc.tensor.matmul(PS[:, 4, NW + w:NW + w + 1], mPT[0][:, win(w)], con[:, C_ONE:C_ONE + 1],
                                        start=True, stop=True)
            last.then_inc(MP_PE.sem, MP_PE.one("sums"))
            pe.wait_ge(MP_DVE.sem, MP_DVE.at("rstd", -1))
            for w in range(NW):
                last = nc.tensor.matmul(PS[:, 5 + w // 4, P * (w % 4):P * (w % 4) + P],
                                        small[:, 32 + w:33 + w].broadcast_to([P, P]), ident, start=True, stop=True)
            last.then_inc(MP_PE.sem, MP_PE.one("bq"))
            pe.wait_ge(MP_DVE.sem, MP_DVE.at("kr2", -1))
            for w in range(NW):
                last = nc.tensor.matmul(PS[:, w // 4, P * (w % 4):P * (w % 4) + P],
                                        small[:, 40 + w:41 + w].broadcast_to([P, P]), ident, start=True, stop=True)
            last.then_inc(MP_PE.sem, MP_PE.one("bkv"))
            pe.wait_ge(wv_loaded, 16)
            pe.wait_ge(MP_DVE.sem, MP_DVE.at("ckv", -1))
            for w in range(NW):
                if w >= 2:
                    pe.wait_ge(MP_ACT.sem, MP_ACT.at(f"v{w - 2}", -1))
                nc.tensor.matmul(PS[:, 4 + w % 2, :], proj[:, T_CKV, win(w)], wv_sb, start=True, stop=True).then_inc(
                    MP_PE.sem, MP_PE.one(f"v{w}"))

            with pe.Fori(0, MLA_HEADS) as h:
                pe.wait_ge(headw_loaded, 16 * (h + 1))
                pe.wait_ge(MP_ACT.sem, MP_ACT.at("v7", -1))
                pe.wait_ge(M_ACT.sem, M_ACT.at("e7", h - 1))
                pe.wait_ge(M_DVE.sem, M_DVE.at("o7", h - 1))
                for half in range(2):
                    hs = slice(HALF * half, HALF * half + HALF)
                    nc.tensor.matmul(PS[:, half, :], headw_sb[:, 0:P], proj[:, T_CQ, hs], start=True, stop=False)
                    last = nc.tensor.matmul(PS[:, half, :], headw_sb[0:HD, P:2 * P], proj[0:HD, T_CQWA, hs],
                                            start=False, stop=True)
                last.then_inc(M_PE.sem, M_PE.one("q"))
                for half in range(2):
                    hs = slice(HALF * half, HALF * half + HALF)
                    last = nc.tensor.matmul(PS[0:HD, 2 + half, :], headw_sb[:, 2 * P:2 * P + HD], proj[:, T_CKV, hs],
                                            start=True, stop=True)
                last.then_inc(M_PE.sem, M_PE.one("k"))

                def scores(q):
                    if q == 0:
                        pe.wait_ge(M_DVE.sem, M_DVE.at("q", h))
                        pe.wait_ge(M_ACT.sem, M_ACT.at("k", h))
                    if q >= 2:
                        pe.wait_ge(M_ACT.sem, M_ACT.at(f"e{q - 2}", h))
                    b = 2 * (q % 2)
                    for part in range(q // 4 + 1):
                        n = min(HALF, P * (q + 1) - HALF * part)
                        nc.tensor.matmul(PS[:, b + part, 0:n], mQ[:, win(q)], mK[:, HALF * part:HALF * part + n],
                                         start=True, stop=(part < q // 4))
                    nc.tensor.matmul(PS[:, b + q // 4, P * (q % 4):P * (q % 4) + P], con[0:1, C_RA:C_RA + P],
                                     con[0:1, C_RB:C_RB + P], start=False, stop=True).then_inc(
                        M_PE.sem, M_PE.one(f"s{q}"))

                def turn(q):
                    pe.wait_ge(M_ACT.sem, M_ACT.at(f"e{q}", h))
                    if q >= 1:
                        pe.wait_ge(M_DVE.sem, M_DVE.at(f"t{q - 1}", h))
                    for k in range(q + 1):
                        last = nc.tensor.transpose(PS[:, 4 + k // 4, P * (k % 4):P * (k % 4) + P],
                                                   mP[q % 2][:, win(k)], ident)
                    last.then_inc(M_PE.sem, M_PE.one(f"t{q}"))

                def values(q):
                    pe.wait_ge(M_DVE.sem, M_DVE.at(f"t{q}", h))
                    if q >= 2:
                        pe.wait_ge(M_DVE.sem, M_DVE.at(f"o{q - 2}", h))
                    for k in range(q + 1):
                        last = nc.tensor.matmul(PS[:, 6 + q % 2, 0:HD], mPT[q % 2][:, win(k)],
                                                mV[:, k, bass.ds(HD * h, HD)], start=(k == 0), stop=(k == q))
                    last.then_inc(M_PE.sem, M_PE.one(f"o{q}"))

                scores(0)
                for q in range(1, NW):
                    scores(q)
                    turn(q - 1)
                    if q >= 2:
                        values(q - 2)
                turn(NW - 1)
                values(NW - 2)
                values(NW - 1)

            pe.wait_ge(mo_dve, 5)
            for t in range(4):
                if t >= 2:
                    pe.wait_ge(mo_dve, 6 + t - 2)
                for w in range(NW):
                    last = nc.tensor.transpose(PS[:, 2 * (t % 2) + w // 4, P * (w % 4):P * (w % 4) + P],
                                               mO[:, w, win(t)], ident)
                last.then_inc(mo_pe, 1)

            pe.wait_ge(rp_act, 2)
            pe.wait_ge(rp_dve, 5)
            pe.wait_ge(mo_dve, 9)
            with pe.Fori(0, PAIRS) as p:
                pe.wait_ge(lora_loaded, 16 * (p + 1))
                pe.wait_ge(R_DVE.sem, R_DVE.at("out", p - 1))
                pe.wait_ge(R_ACT.sem, R_ACT.at("ysq", p - 1))
                for name, b, rows, col, t in (("lw", 0, slice(64, P), 0, T_CQWA), ("la", 2, slice(64, P), P, T_CQWA),
                                              ("lg", 4, slice(0, 96), 2 * P, T_GK)):
                    for half in range(2):
                        last = nc.tensor.matmul(PS[:, b + half, :], lora[rows, col:col + P],
                                                proj[rows, t, HALF * half:HALF * half + HALF], start=True, stop=True)
                    last.then_inc(R_PE.sem, R_PE.one(name))

                def head_sums(bank, src):
                    for w in range(NW):
                        last = nc.tensor.matmul(PS[:, bank, 2 * w:2 * w + 2], src[:, win(w)],
                                                con[:, C_HO:C_HO + 2], start=True, stop=True)
                    return last

                def spread(bank, col):
                    for w in range(NW):
                        for h in range(2):
                            last = nc.tensor.matmul(PS[HD * h:HD * h + HD, bank + w // 4, P * (w % 4):P * (w % 4) + P],
                                                    small[:, col + 2 * w + h:col + 2 * w + h + 1].broadcast_to([P, HD]),
                                                    ident, start=True, stop=True)
                    return last

                pe.wait_ge(R_ACT.sem, R_ACT.at("kksq", p))
                head_sums(6, rBV).then_inc(R_PE.sem, R_PE.one("kks"))
                pe.wait_ge(R_POOL.sem, R_POOL.at("pow", p))
                pe.wait_ge(R_ACT.sem, R_ACT.at("tw", p))
                spread(0, 16).then_inc(R_PE.sem, R_PE.one("kkb"))
                pe.wait_ge(R_DVE.sem, R_DVE.at("rk", p))
                pe.wait_ge(R_ACT.sem, R_ACT.at("ta", p))
                for half in range(2):
                    last = nc.tensor.matmul(PS[:, 2 + half, :], con[:, C_BO:C_BO + P],
                                            rT2[:, HALF * half:HALF * half + HALF], start=True, stop=True)
                last.then_inc(R_PE.sem, R_PE.one("rk"))

                def scores(w):
                    s, bb = w % 2, 4 * (w % 2)
                    if w == 0:
                        pe.wait_ge(R_DVE.sem, R_DVE.at("bv", p))
                        pe.wait_ge(R_ACT.sem, R_ACT.at("afirst", p))
                        pe.wait_ge(R_ACT.sem, R_ACT.at("g", p))
                    if w >= 2:
                        pe.wait_ge(R_DVE.sem, R_DVE.at(f"mt1_{w - 2}", p))
                        pe.wait_ge(R_DVE.sem, R_DVE.at(f"st{2 * (w - 2) + 1}", p))
                        pe.wait_ge(R_ACT.sem, R_ACT.at(f"y{w - 2}", p))
                    for h in range(2):
                        rows = slice(HD * h, HD * h + HD)
                        nc.tensor.matmul(PS[:, bb + h, 0:256], rB[rows, win(w)], rAR[rows, w, :, :],
                                         start=True, stop=True)
                        last = nc.tensor.matmul(PS[:, bb + h, 256:512], rK[rows, win(w)], rAR[rows, w, :, :],
                                                start=True, stop=True)
                    last.then_inc(R_PE.sem, R_PE.one(f"sc{w}"))
                    for h in range(2):
                        rows = slice(HD * h, HD * h + HD)
                        last = nc.tensor.matmul(PS[:, bb + 2 + h, 0:P], rAR[rows, w, 0, :], rB[rows, win(w)],
                                                start=True, stop=True)
                    last.then_inc(R_PE.sem, R_PE.one(f"al{w}"))

                def tokens(w):
                    bb = 4 * (w % 2)
                    if w == 0:
                        pe.wait_ge(R_POOL.sem, R_POOL.at("kh", p))
                        pe.wait_ge(R_ACT.sem, R_ACT.at("vc", p))
                    pe.wait_ge(R_DVE.sem, R_DVE.at(f"sc0_{w}", p))
                    nc.tensor.transpose(PS[:, bb, 0:P], rAR[:, w, 0, :], ident)
                    nc.tensor.transpose(PS[:, bb, P:2 * P], rBh[:, win(w)], ident)
                    nc.tensor.transpose(PS[:, bb, 2 * P:3 * P], rKh[:, win(w)], ident)
                    nc.tensor.transpose(PS[:, bb, 3 * P:4 * P], rT3[:, win(w)], ident).then_inc(
                        R_PE.sem, R_PE.one(f"tok{w}"))

                def a_v(w):
                    s, bb = w % 2, 4 * (w % 2)
                    pe.wait_ge(R_DVE.sem, R_DVE.at(f"sc1_{w}", p))
                    pe.wait_ge(R_ACT.sem, R_ACT.at(f"vz{w}", p))
                    for h in range(2):
                        last = nc.tensor.matmul(PS[:, bb + 1, HD * h:HD * h + HD], rSC[s][:, h, 2, :],
                                                rVZ[s][:, h, HD:P], start=True, stop=True)
                    last.then_inc(R_PE.sem, R_PE.one(f"akv{w}"))

                def double_q(lv, w):
                    s, bb = w % 2, 4 * (w % 2)
                    if lv == 0:
                        pe.wait_ge(R_POOL.sem, R_POOL.at(f"xi_{w}", p))
                    else:
                        pe.wait_ge(R_DVE.sem, R_DVE.at(f"z{lv - 1}_{w}", p))
                    for h in range(2):
                        last = nc.tensor.matmul(PS[:, bb + 2, win(h)], rAL[s][:, h, :], rXX[s][:, 1, h, :],
                                                start=True, stop=True)
                    last.then_inc(R_PE.sem, R_PE.one(f"q{lv}_{w}"))

                def double_z(lv, w):
                    s, bb = w % 2, 4 * (w % 2)
                    pe.wait_ge(R_DVE.sem, R_DVE.at(f"q{lv}_{w}", p))
                    for h in range(2):
                        if lv < 4:
                            nc.tensor.matmul(PS[:, bb + 3, win(h)], rQ[s][:, h, :], rXX[s][:, 0, h, :],
                                             start=True, stop=True)
                        last = nc.tensor.matmul(PS[:, bb + 3, win(2 + h)], rXX[s][:, 0, h, :], rQ[s][:, h, :],
                                                start=True, stop=True)
                    last.then_inc(R_PE.sem, R_PE.one(f"z{lv}_{w}"))

                def solve(w):
                    s, bb = w % 2, 4 * (w % 2)
                    pe.wait_ge(R_ACT.sem, R_ACT.at(f"akv{w}", p))
                    pe.wait_ge(R_DVE.sem, R_DVE.at(f"z4_{w}", p))
                    for h in range(2):
                        last = nc.tensor.matmul(PS[:, bb + 2, win(h)], rXX[s][:, 1, h, :], rAG[s][:, h, :],
                                                start=True, stop=True)
                    last.then_inc(R_PE.sem, R_PE.one(f"pg{w}"))

                def local(w):
                    s, bb = w % 2, 4 * (w % 2)
                    pe.wait_ge(R_ACT.sem, R_ACT.at(f"pg{w}", p))
                    for h in range(2):
                        nc.tensor.matmul(PS[:, bb + 3, win(h)], rPG[s][:, h, :], rSC[s][:, h, 1, :],
                                         start=True, stop=False)
                        nc.tensor.matmul(PS[:, bb + 3, win(h)], rVZ[s][:, h, :], rSC[s][:, h, 3, :],
                                         start=False, stop=False)
                        last = nc.tensor.matmul(PS[:, bb + 3, win(h)], con[:, C_SEL + P * h:C_SEL + P * h + P],
                                                rAR[:, w, 1, :], start=False, stop=True)
                    last.then_inc(R_PE.sem, R_PE.one(f"ry{w}"))

                def carry(w):
                    s, bb = w % 2, 4 * (w % 2)
                    for c in range(2):
                        rows = slice(CH * c, CH * c + CH)
                        for h in range(2):
                            hc = slice(HD * h, HD * h + HD)
                            nc.tensor.matmul(PS[:, bb + c, hc], rPG[s][rows, h, :], rBK[s][rows, 0, hc],
                                             start=True, stop=False)
                            last = nc.tensor.matmul(PS[:, bb + c, hc], rVZ[s][rows, h, :], rBK[s][rows, 1, hc],
                                                    start=False, stop=True)
                    last.then_inc(R_PE.sem, R_PE.one(f"mn{w}"))

                def state(c):
                    w = c // 2
                    bb = 4 * (w % 2)
                    pe.wait_ge(R_DVE.sem, R_DVE.at(f"mt1_{w}", p))
                    if c >= 1:
                        pe.wait_ge(R_DVE.sem, R_DVE.at(f"st{c - 1}", p))
                    for h in range(2):
                        last = nc.tensor.matmul(PS[0:HD, bb + 2, HD * h:HD * h + HD], rMT[:, c, h, :],
                                                rST[:, c, h, :], start=True, stop=True)
                    last.then_inc(R_PE.sem, R_PE.one(f"st{c}"))

                def outputs(c):
                    w = c // 2
                    s, bb = w % 2, 4 * (w % 2)
                    pe.wait_ge(R_ACT.sem, R_ACT.at(f"ry{w}", p))
                    if c >= 1:
                        pe.wait_ge(R_DVE.sem, R_DVE.at(f"st{c - 1}", p))
                    cc = slice(CH * (c % 2), CH * (c % 2) + CH)
                    for h in range(2):
                        last = nc.tensor.matmul(PS[HD * h:HD * h + HD, bb + 3, cc], rST[:, c, h, :],
                                                rRY[s][:, h, cc], start=True, stop=True)
                    last.then_inc(R_PE.sem, R_PE.one(f"y{c}"))

                for g in range(NW // 2):
                    ab = (2 * g, 2 * g + 1)
                    for stage in (scores, tokens, a_v):
                        for w in ab:
                            stage(w)
                    for lv in range(5):
                        for w in ab:
                            double_q(lv, w)
                        for w in ab:
                            double_z(lv, w)
                    for stage in (solve, local, carry):
                        for w in ab:
                            stage(w)
                    for c in range(4 * g, 4 * g + 4):
                        if c < NC - 1:
                            state(c)
                        outputs(c)

                pe.wait_ge(R_ACT.sem, R_ACT.at("y7", p))
                pe.wait_ge(R_DVE.sem, R_DVE.at("st14", p))
                for half in range(2):
                    last = nc.tensor.matmul(PS[:, half, :], con[:, C_BM:C_BM + P], rY[:, HALF * half:HALF * half + HALF],
                                            start=True, stop=True)
                last.then_inc(R_PE.sem, R_PE.one("mean"))
                pe.wait_ge(R_ACT.sem, R_ACT.at("ysq", p))
                head_sums(4, rT1).then_inc(R_PE.sem, R_PE.one("vs"))
                pe.wait_ge(R_POOL.sem, R_POOL.at("gpow", p))
                spread(2, 16).then_inc(R_PE.sem, R_PE.one("vb"))

            gemm(U_OUT, 8, xn, split_ready(1))

            pe.wait_ge(mm_dve, 8)
            for w in range(2):
                last = nc.tensor.matmul(PS[:, 4, w:w + 1], cMs[:, win(w)], con[:, C_ONE:C_ONE + 1], start=True, stop=True)
            last.then_inc(mm_pe, 1)
            pe.wait_ge(mm_dve, 10)
            for w in range(2):
                last = nc.tensor.matmul(PS[:, 7, P * w + 64:P * w + 64 + P], small[:, 36 + w:37 + w].broadcast_to([P, P]),
                                        ident, start=True, stop=True)
            last.then_inc(mm_pe, 1)
            with pe.Fori(0, 4) as i:
                for k in range(2):
                    pe.wait_ge(w_split, 2 * i + (U_MK + k + 3))
                    pe.wait_ge(acc_free, 2 * i + (U_MK + k + 1))
                    pe.wait_ge(mm_dve, 10 + 2 * KT)
                    for kt in range(KT):
                        for a, b in ((0, 0), (0, 1), (1, 0)):
                            last = nc.tensor.matmul(PS[:, 2 * k, 0:MEM], wsp[:, k, kt, a, :], memn[:, kt, b, :],
                                                    start=(kt == 0 and (a, b) == (0, 0)), stop=(kt == KT - 1 and a == 1))
                    last.then_inc(acc_ready, 1)
            norm(1)
            with pe.Fori(0, 4) as i:
                for k in range(2):
                    pe.wait_ge(w_split, 2 * i + (U_MV + k + 3))
                    pe.wait_ge(acc_free, 2 * i + (U_MV + k + 1))
                    for t in range(2):
                        for kt in range(KT):
                            for a, b in ((0, 0), (0, 1), (1, 0)):
                                last = nc.tensor.matmul(PS[:, 2 * k + t, 0:P], memn[:, kt, b, win(t)],
                                                        wsp[:, k, kt, a, :], start=(kt == 0 and (a, b) == (0, 0)),
                                                        stop=(kt == KT - 1 and a == 1))
                    last.then_inc(acc_ready, 1)
            gemm(U_Q, 8, xn, split_ready(2))

            with pe.Fori(0, CA_HEADS) as h:
                pe.wait_ge(ca_stage, 4 * h + 4)
                pe.wait_ge(acc_free, U_O + 2)

                def cscores(q):
                    if q >= 2:
                        pe.wait_ge(C_ACT.sem, C_ACT.at(f"e{q - 2}", h))
                    else:
                        pe.wait_ge(C_ACT.sem, C_ACT.at(f"e{q + 6}", h - 1))
                    for k in range(2):
                        last = nc.tensor.matmul(PS[:, 4 + q % 2, 0:MEM], cQh[:, k, win(q)],
                                                cK[:, bass.ds(2 * h + k, 1), :].rearrange("p a t -> p (a t)"),
                                                start=(k == 0), stop=(k == 1))
                    last.then_inc(C_PE.sem, C_PE.one(f"s{q}"))

                def cturn(q):
                    pe.wait_ge(C_DVE.sem, C_DVE.at(f"p{q}", h))
                    if q >= 2:
                        pe.wait_ge(C_DVE.sem, C_DVE.at(f"t{q - 2}", h))
                    else:
                        pe.wait_ge(C_DVE.sem, C_DVE.at(f"t{q + 6}", h - 1))
                    for k in range(2):
                        last = nc.tensor.transpose(PS[:, 6 + q % 2, P * k:P * k + P], cP[q % 2][:, win(k)], ident)
                    last.then_inc(C_PE.sem, C_PE.one(f"t{q}"))

                def cvalues(half):
                    pe.wait_ge(C_DVE.sem, C_DVE.at(f"t{4 * half + 3}", h))
                    pe.wait_ge(C_DVE.sem, C_DVE.at(f"l{half}1", h - 1))
                    for m in range(2):
                        for k in range(2):
                            last = nc.tensor.matmul(PS[:, 2 * half + m, :], cVh[:, k, win(m)], cPT[half][:, k, :],
                                                    start=(k == 0), stop=(k == 1))
                    last.then_inc(C_PE.sem, C_PE.one(f"o{half}"))

                cscores(0)
                for q in range(1, NW):
                    cscores(q)
                    cturn(q - 1)
                    if q == 5:
                        cvalues(0)
                cturn(NW - 1)
                cvalues(1)

            def ca_ready(kt):
                pe.wait_ge(C_DVE.sem, C_DVE.at("l11", CA_HEADS - 1))

            gemm(U_O, 8, xn, ca_ready)
            norm(2)

            with pe.Fori(0, 4) as c:
                with pe.Fori(0, 4) as i:
                    for k in range(2):
                        unit(16 * c + 2 * i + (U_MLP + k), k, xn, split_ready(3))
                with pe.Fori(0, 4) as i:
                    for k in range(2):
                        unit(16 * c + 2 * i + (U_MLP + 8 + k), k, hid,
                             lambda kt: pe.wait_ge(hid_ready, 8 * c + kt + 3))
            norm(3)

        @block.scalar
        def _(act):
            for st in (M_ACT, R_ACT, C_ACT):
                nc.scalar.sem_inc(st.sem, st.n)

            def square(i, src):
                nc.scalar.activation(tmp[:, i % 2, :], src, ACT.Square).then_inc(sq_ready, 1)

            def norm(n):
                act.wait_ge(var_ready, n + 1)
                nc.scalar.activation(small[:, 8:16], small[:, 0:8], ACT.Sqrt).then_inc(std_ready, 1)

            def heads(n):
                for kt in range(KT):
                    act.wait_ge(scaled, KT * n + kt + 1)
                    nc.scalar.copy(xn[:, kt, 0, :], tmp[:, kt % 2, :]).then_inc(head_ready, 1)

            for kt in range(KT):
                act.wait_ge(x_loaded[kt], 16)
                if kt >= 2:
                    act.wait_ge(sq_added, kt - 1)
                square(kt, H[:, kt, :])
            norm(0)
            heads(0)

            act.wait_ge(acc_free, U_OUT + 2)
            act.wait_ge(acc_ready, U_OUT + 2)
            nc.scalar.activation(mQ, proj[:, T_CQ, :], ACT.Square).then_inc(MP_ACT.sem, MP_ACT.one("sq1"))
            nc.scalar.activation(mK[0:HD], proj[0:HD, T_CQWA, :], ACT.Square).then_inc(MP_ACT.sem, MP_ACT.one("sq2"))
            nc.scalar.activation(mPT[0], proj[:, T_CKV, :], ACT.Square).then_inc(MP_ACT.sem, MP_ACT.one("sq3"))
            act.wait_ge(MP_DVE.sem, MP_DVE.at("clamp", -1))
            nc.scalar.activation(mSin, mT[0], ACT.Sin).then_inc(MP_ACT.sem, MP_ACT.one("sin"))
            act.wait_ge(MP_DVE.sem, MP_DVE.at("abs", -1))
            nc.scalar.activation(mCos, mT[1], ACT.Sin, bias=con[:, C_PI2:C_PI2 + 1], scale=-1.0).then_inc(
                MP_ACT.sem, MP_ACT.one("cos"))
            act.wait_ge(MP_DVE.sem, MP_DVE.at("var", -1))
            nc.scalar.activation(small[:, 16:32], small[:, 0:16], ACT.Sqrt).then_inc(MP_ACT.sem, MP_ACT.one("std"))
            for w in range(NW):
                act.wait_ge(MP_PE.sem, MP_PE.at(f"v{w}", -1))
                nc.scalar.copy(mV[:, w, :], PS[:, 4 + w % 2, :]).then_inc(MP_ACT.sem, MP_ACT.one(f"v{w}"))

            with act.Fori(0, MLA_HEADS) as h:
                act.wait_ge(M_PE.sem, M_PE.at("k", h))
                act.wait_ge(MP_DVE.sem, MP_DVE.at("kr", -1))
                nc.scalar.copy(mK[0:HD], two(2)[0:HD]).then_inc(M_ACT.sem, M_ACT.one("k"))
                for q in range(NW):
                    n = P * (q + 1)
                    act.wait_ge(M_DVE.sem, M_DVE.at(f"b{q}", h))
                    if q >= 2:
                        act.wait_ge(M_PE.sem, M_PE.at(f"t{q - 2}", h))
                    else:
                        act.wait_ge(M_PE.sem, M_PE.at(f"t{q + 6}", h - 1))
                    nc.scalar.activation(mP[q % 2][:, 0:n], two(2 * (q % 2))[:, 0:n], ACT.Exp,
                                         bias=small[:, 8 + q:9 + q], scale=MLA_SCALE,
                                         accum_out=small[:, 16 + q:17 + q]).then_inc(M_ACT.sem, M_ACT.one(f"e{q}"))
            act.wait_ge(mo_dve, 3)
            nc.scalar.activation(mSt, mSt, ACT.Sqrt).then_inc(mo_act, 1)

            nc.scalar.activation(proj[64:96, T_CQWA, :], proj[64:96, T_CQWA, :], ACT.Tanh).then_inc(rp_act, 1)
            nc.scalar.activation(proj[0:96, T_GK, :], proj[0:96, T_GK, :], ACT.Tanh, scale=0.5).then_inc(rp_act, 1)
            with act.Fori(0, PAIRS) as p:
                half_e = 0.5 * EXPM05

                def par(base):
                    return vech[:, bass.ds(p + base, 1)]

                act.wait_ge(R_PE.sem, R_PE.at("lw", p))
                nc.scalar.activation(rT1, two(0), ACT.Tanh, bias=par(0), scale=0.5).then_inc(
                    R_ACT.sem, R_ACT.one("tw"))
                act.wait_ge(R_ACT.sem, R_ACT.at("tw", p))
                act.wait_ge(R_DVE.sem, R_DVE.at("out", p - 1))
                nc.scalar.activation(rT2, rT1, ACT.Exp, bias=con[:, C_EM:C_EM + 1], scale=-half_e).then_inc(
                    R_ACT.sem, R_ACT.one("dec"))
                nc.scalar.activation(rT3, rT1, ACT.Exp, bias=con[:, C_EP:C_EP + 1], scale=half_e).then_inc(
                    R_ACT.sem, R_ACT.one("dnv"))
                act.wait_ge(R_PE.sem, R_PE.at("la", p))
                act.wait_ge(R_ACT.sem, R_ACT.at("dnv", p))
                nc.scalar.activation(rT1, two(2), ACT.Tanh, bias=par(4), scale=0.5).then_inc(
                    R_ACT.sem, R_ACT.one("ta"))
                act.wait_ge(R_PE.sem, R_PE.at("lg", p))
                nc.scalar.copy(rG, two(4)).then_inc(R_ACT.sem, R_ACT.one("g"))
                act.wait_ge(R_DVE.sem, R_DVE.at("kk", p))
                nc.scalar.activation(rBV, rY, ACT.Square).then_inc(R_ACT.sem, R_ACT.one("kksq"))
                act.wait_ge(R_DVE.sem, R_DVE.at("nkk", p))
                nc.scalar.copy(rAR[:, :, 0, :].rearrange("p w (c t) -> p w c t", c=2)[:, :, :, 0],
                               rY.rearrange("p (w c t) -> p w c t", w=NW, c=2)[:, :, :, 0]).then_inc(
                    R_ACT.sem, R_ACT.one("afirst"))
                wt = rW.rearrange("p (c t) -> p c t", c=NC)[:, :, CH - 1]
                nc.scalar.copy(rWT[:, :, 0], wt[0:HD]).then_inc(R_ACT.sem, R_ACT.one("wt0"))
                nc.scalar.copy(rWT[:, :, 1], wt[HD:P]).then_inc(R_ACT.sem, R_ACT.one("wt1"))
                act.wait_ge(R_DVE.sem, R_DVE.at("bt", p))
                nc.scalar.copy(rT3, proj[:, bass.ds(p + T_V, 1), :].rearrange("p a t -> p (a t)")).then_inc(
                    R_ACT.sem, R_ACT.one("vc"))
                for g in range(NW // 2):
                    ab = (2 * g, 2 * g + 1)
                    for w in ab:
                        s, bb = w % 2, 4 * (w % 2)
                        tok = PS[:, bb, :].rearrange("p (k h n) -> p k h n", k=4, h=2)
                        act.wait_ge(R_PE.sem, R_PE.at(f"tok{w}", p))
                        nc.scalar.copy(rAG[s][:, :, 0:HD], tok[:, 0]).then_inc(R_ACT.sem, R_ACT.one(f"ag{w}"))
                        nc.scalar.copy(rBK[s].rearrange("p k (h n) -> p k h n", h=2), tok[:, 1:3]).then_inc(
                            R_ACT.sem, R_ACT.one(f"bk{w}"))
                        nc.scalar.copy(rVZ[s][:, :, HD:P], tok[:, 3]).then_inc(R_ACT.sem, R_ACT.one(f"vz{w}"))
                    for w in ab:
                        s, bb = w % 2, 4 * (w % 2)
                        act.wait_ge(R_PE.sem, R_PE.at(f"akv{w}", p))
                        nc.scalar.copy(rAG[s][:, :, HD:P], PS[:, bb + 1, 0:P].rearrange("p (h n) -> p h n", h=2)
                                       ).then_inc(R_ACT.sem, R_ACT.one(f"akv{w}"))
                    for w in ab:
                        s, bb = w % 2, 4 * (w % 2)
                        act.wait_ge(R_PE.sem, R_PE.at(f"pg{w}", p))
                        nc.scalar.copy(rPG[s].rearrange("p h n -> p (h n)"), PS[:, bb + 2, 0:256]).then_inc(
                            R_ACT.sem, R_ACT.one(f"pg{w}"))
                    for w in ab:
                        s, bb = w % 2, 4 * (w % 2)
                        act.wait_ge(R_PE.sem, R_PE.at(f"ry{w}", p))
                        nc.scalar.copy(rRY[s].rearrange("p h n -> p (h n)"), PS[:, bb + 3, 0:256]).then_inc(
                            R_ACT.sem, R_ACT.one(f"ry{w}"))
                    for w in ab:
                        act.wait_ge(R_PE.sem, R_PE.at(f"y{2 * w + 1}", p))
                        nc.scalar.copy(rY[:, win(w)], PS[:, 4 * (w % 2) + 3, 0:P]).then_inc(
                            R_ACT.sem, R_ACT.one(f"y{w}"))
                act.wait_ge(R_DVE.sem, R_DVE.at("yc", p))
                nc.scalar.activation(rT1, rY, ACT.Square).then_inc(R_ACT.sem, R_ACT.one("ysq"))

            for kt in range(KT):
                act.wait_ge(R_DVE.sem, R_DVE.at("out", PAIRS - 1))
                nc.scalar.copy(xn[:, kt, 0, :], H[:, kt, :]).then_inc(head_ready, 1)

            act.wait_ge(mem_loaded, 16)
            nc.scalar.activation(cMt, cMem, ACT.Square).then_inc(mm_act, 1)

            def residual_squares(u0, n):
                with act.Fori(0, 4) as i:
                    for k in range(2):
                        act.wait_ge(h_added, 2 * i + (u0 + k + 1))
                        act.wait_ge(sq_added, 2 * i + (KT * n + k - 1))
                        square(k, H[:, bass.ds(2 * i + k, 1), :].rearrange("p a t -> p (a t)"))

            residual_squares(0, 1)
            act.wait_ge(mm_dve, 9)
            nc.scalar.activation(small[:, 34:36], small[:, 32:34], ACT.Sqrt).then_inc(mm_act, 1)
            for kt in range(KT):
                act.wait_ge(mm_dve, 10 + kt + 1)
                nc.scalar.copy(memn[:, kt, 0, :], cMt[:, kt, :]).then_inc(mm_act, 1)
            with act.Fori(0, 4) as i:
                for k in range(2):
                    act.wait_ge(acc_ready, 2 * i + (U_MK + k + 3))
                    nc.scalar.copy(cK[:, bass.ds(2 * i + k, 1), :].rearrange("p a t -> p (a t)"),
                                   PS[:, 2 * k, 0:MEM]).then_inc(acc_free, 1)
            norm(1)
            heads(1)
            with act.Fori(0, 4) as i:
                for k in range(2):
                    act.wait_ge(acc_ready, 2 * i + (U_MV + k + 3))
                    nc.scalar.copy(cV[:, :, bass.ds(256 * i + P * k, P)], PS[:, 2 * k:2 * k + 2, 0:P]).then_inc(
                        acc_free, 1)
            with act.Fori(0, 4) as i:
                for k in range(2):
                    act.wait_ge(acc_ready, 2 * i + (U_Q + k + 3))
                    nc.scalar.copy(cQ[:, bass.ds(2 * i + k, 1), :].rearrange("p a t -> p (a t)"),
                                   two(2 * k)).then_inc(acc_free, 1)

            with act.Fori(0, CA_HEADS) as h:
                def cheads(half):
                    act.wait_ge(C_PE.sem, C_PE.at(f"o{half}", h))
                    for m in range(2):
                        nc.scalar.copy(xn[:, bass.ds(2 * h + m, 1), 0, HALF * half:HALF * half + HALF].rearrange(
                            "p a t -> p (a t)"), PS[:, 2 * half + m, :]).then_inc(C_ACT.sem, C_ACT.one(f"h{half}{m}"))

                for q in range(NW):
                    act.wait_ge(C_DVE.sem, C_DVE.at(f"b{q}", h))
                    if q >= 2:
                        act.wait_ge(C_PE.sem, C_PE.at(f"t{q - 2}", h))
                    else:
                        act.wait_ge(C_PE.sem, C_PE.at(f"t{q + 6}", h - 1))
                    nc.scalar.activation(cP[q % 2], PS[:, 4 + q % 2, 0:MEM], ACT.Exp, bias=small[:, 8 + q:9 + q],
                                         scale=CA_SCALE, accum_out=small[:, 16 + q:17 + q]).then_inc(
                        C_ACT.sem, C_ACT.one(f"e{q}"))
                    if q == 6:
                        cheads(0)
                cheads(1)

            residual_squares(8, 2)
            norm(2)
            heads(2)

            def hidden(c):
                with act.Fori(0, 4) as i:
                    for k in range(2):
                        n = 8 * c + 2 * i
                        act.wait_ge(acc_ready, 16 * c + 2 * i + (U_MLP + k + 3))
                        act.wait_ge(hid_ready, n + (k + 1))
                        nc.scalar.activation(tmp[:, k, :], two(2 * k), ACT.Relu).then_inc(relu_ready, 1)
                        act.wait_ge(hsq_ready, n + (k + 1))
                        nc.scalar.copy(hid[:, bass.ds(2 * i + k, 1), 0, :].rearrange("p a t -> p (a t)"),
                                       tmp[:, k, :]).then_inc(hhead_ready, 1)

            with act.Fori(0, 4) as c:
                hidden(c)
            residual_squares(40, 3)
            norm(3)

        @block.vector
        def _(dve):
            nc.vector.sem_inc(acc_free, 2)
            nc.vector.sem_inc(hid_ready, 2)
            for st in (M_DVE, R_DVE, C_DVE):
                nc.vector.sem_inc(st.sem, st.n)

            def norm(n):
                dve.wait_ge(nsum_ready, n + 1)
                nc.vector.tensor_scalar(small[:, 0:8], PS[:, 4, 0:NW], 1.0 / D, EPS, ALU.mult, ALU.add).then_inc(
                    var_ready, 1)
                dve.wait_ge(std_ready, n + 1)
                nc.vector.reciprocal(small[:, 16:24], small[:, 8:16]).then_inc(rstd_ready, 1)

            def scale_and_split(n, pas, gain):
                def rest(kt):
                    dve.wait_ge(head_ready, KT * pas + kt + 1)
                    nc.vector.tensor_tensor(xn[:, kt, 1, :], tmp[:, kt % 2, :], xn[:, kt, 0, :].bitcast(F32),
                                            ALU.subtract).then_inc(xn_ready, 1)

                dve.wait_ge(nb_ready, n + 1)
                for kt in range(KT):
                    if kt >= 2:
                        dve.wait_ge(xn_ready, KT * pas + kt - 1)
                    nc.vector.scalar_tensor_tensor(tmp[:, kt % 2, :], H[:, kt, :], vec[:, gain + kt:gain + kt + 1],
                                                   two(5), ALU.mult, ALU.mult).then_inc(scaled, 1)
                    if kt >= 1:
                        rest(kt - 1)
                rest(KT - 1)

            for kt in range(KT):
                dve.wait_ge(sq_ready, kt + 1)
                if kt == 0:
                    nc.vector.tensor_copy(ssum[:, :], tmp[:, 0, :]).then_inc(sq_added, 1)
                else:
                    dve.wait_ge(sq_added, kt)
                    nc.vector.tensor_tensor(ssum[:, :], ssum[:, :], tmp[:, kt % 2, :], ALU.add).then_inc(sq_added, 1)
            dve.wait_ge(vec_loaded, 16)
            nc.vector.tensor_scalar(omu[:, :], vec[:, V_MU:V_MU + 16], -1.0, 1.0, ALU.mult, ALU.add).then_inc(vec_made, 1)
            nc.vector.tensor_scalar(vech[:, 0:8], vec[:, V_W0:V_W0 + 8], 0.5, None, ALU.mult).then_inc(vec_made, 1)
            nc.vector.tensor_scalar(vech[:, 8:12], vec[:, V_KA:V_KA + 4], 0.5, None, ALU.mult).then_inc(vec_made, 1)
            norm(0)
            scale_and_split(0, 0, V_MIX)

            dve.wait_ge(vec_made, 3)
            with dve.Fori(0, 8) as i:
                for k in range(2):
                    u = 2 * i + k
                    cur = proj[:, bass.ds(u, 1), :].rearrange("p a t -> p (a t)")
                    rest = proj[:, bass.ds(u, 1), 1:S].rearrange("p a t -> p (a t)")
                    dve.wait_ge(acc_ready, u + 3)
                    nc.vector.tensor_scalar(cur, two(2 * k), omu[:, bass.ds(u, 1)], None, ALU.mult).then_inc(proj_part, 1)
                    dve.wait_ge(proj_part, u + 1)
                    nc.vector.scalar_tensor_tensor(rest, two(2 * k)[:, 0:S - 1], vec[:, bass.ds(u + V_MU, 1)], rest,
                                                   ALU.mult, ALU.add).then_inc(acc_free, 1)

            def mp(ins, name):
                ins.then_inc(MP_DVE.sem, MP_DVE.one(name))

            def after(name):
                dve.wait_ge(MP_DVE.sem, MP_DVE.at(name, -1))

            dve.wait_ge(con_loaded, 16)
            dve.wait_ge(pos_loaded, 16)
            mp(nc.vector.tensor_copy(mT[0], posi), "posf")
            after("posf")
            mp(nc.vector.tensor_scalar(mT[0], mT[0], con[:, C_INV:C_INV + 1], None, ALU.mult), "ang")
            after("ang")
            mp(nc.vector.tensor_scalar(mT[1], mT[0], 1.0 / (2 * math.pi), MAGIC, ALU.mult, ALU.add), "turns")
            after("turns")
            mp(nc.vector.tensor_scalar(mCos, mT[1], -MAGIC, -6.28125, ALU.add, ALU.mult), "m1")
            after("m1")
            mp(nc.vector.tensor_tensor(mT[0], mT[0], mCos, ALU.add), "r1")
            mp(nc.vector.tensor_scalar(mT[1], mT[1], -MAGIC, -(2 * math.pi - 6.28125), ALU.add, ALU.mult), "m2")
            after("m2")
            mp(nc.vector.tensor_tensor(mT[0], mT[0], mT[1], ALU.add), "r2")
            after("r2")
            mp(nc.vector.tensor_scalar(mT[0], mT[0], 3.1415925, -3.1415925, ALU.min, ALU.max), "clamp")
            after("clamp")
            mp(nc.vector.scalar_tensor_tensor(mT[1], mT[0], -1.0, mT[0], ALU.mult, ALU.max), "abs")
            dve.wait_ge(MP_PE.sem, MP_PE.at("sums", -1))
            mp(nc.vector.tensor_scalar(small[:, 0:8], PS[:, 4, 0:8], 1.0 / QR, EPS, ALU.mult, ALU.add), "var1")
            mp(nc.vector.tensor_scalar(small[:, 8:16], PS[:, 4, 8:16], 1.0 / KVR, EPS, ALU.mult, ALU.add), "var")
            dve.wait_ge(MP_ACT.sem, MP_ACT.at("std", -1))
            mp(nc.vector.reciprocal(small[:, 32:48], small[:, 16:32]), "rstd")
            mp(nc.vector.memset(mCS[0:HD], 1.0), "one")
            mp(nc.vector.tensor_copy(mCS[64:96], mCos[64:96]), "csc")
            mp(nc.vector.tensor_scalar(mCS[96:P], mSin[96:P], con[96:P, C_SGN:C_SGN + 1], None, ALU.mult), "css")
            dve.wait_ge(MP_PE.sem, MP_PE.at("e12", -1))
            mp(nc.vector.tensor_tensor(mT[0][HD:P], two(0)[HD:P], mCos[HD:P], ALU.mult), "kr1")
            mp(nc.vector.tensor_tensor(mT[1][HD:P], two(2)[HD:P], mSin[HD:P], ALU.mult), "kr2")
            after("kr2")
            mp(nc.vector.tensor_tensor(mK[HD:P], mT[0][HD:P], mT[1][HD:P], ALU.add), "kr")
            dve.wait_ge(MP_PE.sem, MP_PE.at("bq", -1))
            mp(nc.vector.scalar_tensor_tensor(proj[:, T_CQ, :], proj[:, T_CQ, :], vec[:, V_QN:V_QN + 1], two(5),
                                              ALU.mult, ALU.mult), "cq0")
            mp(nc.vector.scalar_tensor_tensor(proj[0:HD, T_CQWA, :], proj[0:HD, T_CQWA, :],
                                              vec[0:HD, V_QN + 1:V_QN + 2], two(5)[0:HD], ALU.mult, ALU.mult), "cq1")
            dve.wait_ge(MP_PE.sem, MP_PE.at("bkv", -1))
            mp(nc.vector.scalar_tensor_tensor(proj[:, T_CKV, :], proj[:, T_CKV, :], vec[:, V_KVN:V_KVN + 1], two(0),
                                              ALU.mult, ALU.mult), "ckv")

            with dve.Fori(0, MLA_HEADS) as h:
                def m(ins, name):
                    ins.then_inc(M_DVE.sem, M_DVE.one(name))

                def own(name):
                    dve.wait_ge(M_DVE.sem, M_DVE.at(name, h))

                dve.wait_ge(M_PE.sem, M_PE.at("q", h))
                m(nc.vector.tensor_tensor(mQ, two(0), mCS, ALU.mult), "q")

                def row_max(q):
                    dve.wait_ge(M_PE.sem, M_PE.at(f"s{q}", h))
                    m(nc.vector.tensor_reduce(small[:, q:q + 1], two(2 * (q % 2))[:, 0:P * (q + 1)], AX_X, ALU.max),
                      f"m{q}")
                    own(f"m{q}")
                    m(nc.vector.tensor_scalar(small[:, 8 + q:9 + q], small[:, q:q + 1], -MLA_SCALE, None, ALU.mult),
                      f"b{q}")

                def copy_pt(q):
                    dve.wait_ge(M_PE.sem, M_PE.at(f"t{q}", h))
                    if q >= 2:
                        dve.wait_ge(M_PE.sem, M_PE.at(f"o{q - 2}", h))
                    m(nc.vector.tensor_copy(mPT[q % 2][:, 0:P * (q + 1)], two(4)[:, 0:P * (q + 1)]), f"t{q}")

                def divide(q):
                    m(nc.vector.reciprocal(small[:, 24 + q:25 + q], small[:, 16 + q:17 + q]), f"r{q}")
                    dve.wait_ge(M_PE.sem, M_PE.at(f"o{q}", h))
                    own(f"r{q}")
                    m(nc.vector.tensor_scalar(mO[:, q, bass.ds(HD * h, HD)], PS[:, 6 + q % 2, 0:HD],
                                              small[:, 24 + q:25 + q], None, ALU.mult), f"o{q}")

                row_max(0)
                for q in range(1, NW):
                    row_max(q)
                    copy_pt(q - 1)
                    if q >= 2:
                        divide(q - 2)
                copy_pt(NW - 1)
                divide(NW - 2)
                divide(NW - 1)

            o_all = mO.rearrange("p w (h n) -> p (w h) n", n=HD)
            sq_all = mOsq.rearrange("p (a n) -> p a n", n=HD)
            dve.wait_ge(M_DVE.sem, M_DVE.at("o7", MLA_HEADS - 1))
            nc.vector.tensor_tensor(sq_all, o_all, o_all, ALU.mult).then_inc(mo_dve, 1)
            dve.wait_ge(mo_dve, 1)
            nc.vector.tensor_reduce(mSt, sq_all, AX_X, ALU.add).then_inc(mo_dve, 1)
            dve.wait_ge(mo_dve, 2)
            nc.vector.tensor_scalar(mSt, mSt, 1.0 / HD, EPS, ALU.mult, ALU.add).then_inc(mo_dve, 1)
            dve.wait_ge(mo_act, 1)
            nc.vector.reciprocal(mSt, mSt).then_inc(mo_dve, 1)
            dve.wait_ge(mo_dve, 4)
            nc.vector.tensor_tensor(o_all, o_all, mSt.rearrange("p (a n) -> p a n", n=1).broadcast_to([P, 64, HD]),
                                    ALU.mult).then_inc(mo_dve, 1)
            for t in range(4):
                dve.wait_ge(mo_pe, t + 1)
                nc.vector.tensor_scalar(H[:, t, :], two(2 * (t % 2)), vec[:, V_ON + t:V_ON + t + 1], None,
                                        ALU.mult).then_inc(mo_dve, 1)

            nc.vector.tensor_copy(rST[HD:P], ident[HD:P, HD:P].rearrange("p (a b n) -> p a b n", a=1, b=1)
                                  .broadcast_to([HD, NC, 2, HD])).then_inc(rp_dve, 1)
            nc.vector.memset(rST[0:HD, 0], 0.0).then_inc(rp_dve, 1)
            for s in range(2):
                nc.vector.memset(rVZ[s][:, :, 0:HD], 0.0).then_inc(rp_dve, 1)
            dve.wait_ge(rp_act, 2)
            nc.vector.tensor_scalar(proj[0:96, T_GK, :], proj[0:96, T_GK, :], 0.5, 0.5, ALU.mult, ALU.add).then_inc(
                rp_dve, 1)
            with dve.Fori(0, PAIRS) as p:
                def r(ins, name):
                    ins.then_inc(R_DVE.sem, R_DVE.one(name))

                def own(name):
                    dve.wait_ge(R_DVE.sem, R_DVE.at(name, p))

                def of_act(name):
                    dve.wait_ge(R_ACT.sem, R_ACT.at(name, p))

                def of_pe(name):
                    dve.wait_ge(R_PE.sem, R_PE.at(name, p))

                def of_pool(name):
                    dve.wait_ge(R_POOL.sem, R_POOL.at(name, p))

                def tile(base):
                    return proj[:, bass.ds(p + base, 1), :].rearrange("p a t -> p (a t)")

                def par(base):
                    return vec[:, bass.ds(p + base, 1)]

                def chunks(ap):
                    return ap.rearrange("p (c t) -> p c t", c=NC)

                of_pe("lw")
                r(nc.vector.tensor_scalar(rY, tile(T_K), par(V_KK), None, ALU.mult), "kk")
                r(nc.vector.memset(rBh, 0.0), "zb")
                r(nc.vector.memset(rKh, 0.0), "zk")
                r(nc.vector.memset(rMT[HD:P], 0.0), "zm")
                of_act("dnv")
                r(nc.vector.tensor_tensor(rWi, rT2, rT3, ALU.mult), "nw")
                own("nw")
                r(nc.vector.scalar_tensor_tensor(rT3, rWi, 2.0, rT3, ALU.subtract, ALU.mult, reverse0=True), "dinv")
                own("dinv")
                own("zm")
                r(nc.vector.tensor_copy(chunks(rBh)[:, :, 0:1], chunks(rT2)[:, :, 0:1]), "f1")
                r(nc.vector.tensor_copy(chunks(rKh)[:, :, 0:1], chunks(rT3)[:, :, 0:1]), "f2")
                own("f2")
                r(nc.vector.memset(chunks(rT2)[:, :, 0:1], 0.0), "z1")
                r(nc.vector.memset(chunks(rT3)[:, :, 0:1], 0.0), "z2")
                own("z2")
                r(nc.vector.tensor_tensor_scan(rW, rT2, rBh, 0.0, ALU.mult, ALU.add), "W")
                r(nc.vector.tensor_tensor_scan(rWi, rT3, rKh, 0.0, ALU.mult, ALU.add), "Wi")
                of_pe("kks")
                r(nc.vector.tensor_scalar(small[:, 0:16], PS[:, 6, 0:16], 1e-24, None, ALU.max), "kkm")
                of_pe("kkb")
                r(nc.vector.scalar_tensor_tensor(rY, rY, -1.0, two(0), ALU.mult, ALU.mult), "nkk")
                own("nkk")
                r(nc.vector.tensor_tensor(
                    rAR[:, :, 0, :].rearrange("p w (c t) -> p w c t", c=2)[:, :, :, 1:CH],
                    rY.rearrange("p (w c t) -> p w c t", w=NW, c=2)[:, :, :, 1:CH],
                    rW.rearrange("p (w c t) -> p w c t", w=NW, c=2)[:, :, :, 0:CH - 1], ALU.mult), "at")
                of_act("ta")
                r(nc.vector.tensor_scalar(rT2, rT1, -0.5, -0.5, ALU.mult, ALU.add), "na")
                own("na")
                r(nc.vector.tensor_tensor(rT3, rT2, rY, ALU.mult), "b")
                own("b")
                r(nc.vector.tensor_tensor(rB, rT3, rWi, ALU.mult), "bt")
                r(nc.vector.tensor_scalar(rT1, rT1, -1.0, vech[:, bass.ds(p + 8, 1)], ALU.add, ALU.mult), "am")
                own("am")
                r(nc.vector.scalar_tensor_tensor(rT1, rT1, 1.0, tile(T_K), ALU.add, ALU.mult), "k2")
                own("k2")
                r(nc.vector.tensor_tensor(rK, rT1, rWi, ALU.mult), "kt")
                r(nc.vector.tensor_tensor(rAR[:, :, 1, :], tile(T_R).rearrange("p (w t) -> p w t", w=NW),
                                          rW.rearrange("p (w t) -> p w t", w=NW), ALU.mult), "rt")
                r(nc.vector.scalar_tensor_tensor(rT2, tile(T_R), par(V_RK), rT1, ALU.mult, ALU.mult), "rk")
                of_pe("rk")
                r(nc.vector.tensor_tensor(rBV, two(2), tile(T_V), ALU.mult), "bv")

                for g in range(NW // 2):
                    ab = (2 * g, 2 * g + 1)
                    for w in ab:
                        s, bb = w % 2, 4 * (w % 2)
                        of_pe(f"sc{w}")
                        for hh in range(2):
                            r(nc.vector.tensor_tensor(rSC[s][:, hh].rearrange("p k n -> p (k n)"), PS[:, bb + hh, :],
                                                      con[:, C_MS:C_MS + 512], ALU.mult), f"sc{hh}_{w}")
                        of_pe(f"al{w}")
                        for hh in range(2):
                            r(nc.vector.tensor_tensor(rAL[s][:, hh, :], PS[:, bb + 2 + hh, 0:P],
                                                      con[:, C_ML:C_ML + P], ALU.mult), f"al{hh}_{w}")
                    for lv in range(5):
                        for w in ab:
                            s, bb = w % 2, 4 * (w % 2)
                            of_pe(f"q{lv}_{w}")
                            mask = con[:, C_BQ + P * lv:C_BQ + P * lv + P].rearrange("p (a n) -> p a n", a=1)
                            r(nc.vector.tensor_tensor(rQ[s], PS[:, bb + 2, 0:256].rearrange("p (h n) -> p h n", h=2),
                                                      mask.broadcast_to([P, 2, P]), ALU.mult), f"q{lv}_{w}")
                        for w in ab:
                            s, bb = w % 2, 4 * (w % 2)
                            of_pe(f"z{lv}_{w}")
                            lo = 0 if lv < 4 else 256
                            xx = rXX[s].rearrange("p a h n -> p (a h n)")[:, lo:512]
                            r(nc.vector.tensor_tensor(xx, PS[:, bb + 3, lo:512], xx, ALU.add), f"z{lv}_{w}")
                    for w in ab:
                        s, bb = w % 2, 4 * (w % 2)
                        if w == 0:
                            of_pool("dg")
                        of_pe(f"mn{w}")
                        for c in range(2):
                            mt = rMT[:, 2 * w + c].rearrange("p h n -> p (h n)")
                            r(nc.vector.tensor_tensor(mt, PS[:, bb + c, 0:P], mt, ALU.add), f"mt{c}_{w}")
                    for c in range(4 * g, min(4 * g + 4, NC - 1)):
                        w = c // 2
                        of_pe(f"st{c}")
                        r(nc.vector.tensor_copy(rST[0:HD, c + 1].rearrange("p h n -> p (h n)"),
                                                PS[0:HD, 4 * (w % 2) + 2, 0:P]), f"st{c}")

                of_pe("mean")
                r(nc.vector.tensor_tensor(rY, rY, two(0), ALU.subtract), "yc")
                of_pe("vs")
                r(nc.vector.tensor_scalar(small[:, 0:16], PS[:, 4, 0:16], 1.0 / HD, GN_EPS, ALU.mult, ALU.add), "var")
                of_pe("vb")
                own("yc")
                r(nc.vector.tensor_tensor(rT2, rY, two(2), ALU.mult), "yn")
                own("yn")
                r(nc.vector.tensor_scalar(rT2, rT2, par(V_LW), par(V_LB), ALU.mult, ALU.add), "yl")
                own("yl")
                r(nc.vector.tensor_tensor(rT2, rT2, rBV, ALU.add), "yb")
                own("yb")
                r(nc.vector.tensor_tensor(H[:, bass.ds(p + 4, 1), :].rearrange("p a t -> p (a t)"), rT2, rG,
                                          ALU.mult), "out")

            for kt in range(KT):
                dve.wait_ge(head_ready, KT + kt + 1)
                nc.vector.tensor_tensor(xn[:, kt, 1, :], H[:, kt, :], xn[:, kt, 0, :].bitcast(F32),
                                        ALU.subtract).then_inc(xn_ready, 1)

            dve.wait_ge(mm_act, 1)
            nc.vector.tensor_copy(cMs, cMt[:, 0, :]).then_inc(mm_dve, 1)
            for kt in range(1, KT):
                dve.wait_ge(mm_dve, kt)
                nc.vector.tensor_tensor(cMs, cMs, cMt[:, kt, :], ALU.add).then_inc(mm_dve, 1)

            def residual(u0, j0, n):
                nc.vector.memset(ssum[:, :], 0.0).then_inc(ssum_zero, 1)
                dve.wait_ge(ssum_zero, n)
                with dve.Fori(0, 4) as i:
                    for k in range(2):
                        tile = H[:, bass.ds(2 * i + k, 1), :].rearrange("p a t -> p (a t)")
                        dve.wait_ge(acc_ready, 2 * i + (u0 + k + 3))
                        nc.vector.tensor_tensor(tile, two(2 * k), tile, ALU.add).then_inc(h_added, 1)
                        dve.wait_ge(h_added, 2 * i + (j0 + k + 1))
                        nc.vector.sem_inc(acc_free, 1)
                        dve.wait_ge(sq_ready, 2 * i + (KT * n + k + 1))
                        dve.wait_ge(sq_added, 2 * i + (KT * n + k))
                        nc.vector.tensor_tensor(ssum[:, :], ssum[:, :], tmp[:, k, :], ALU.add).then_inc(sq_added, 1)

            for kt in range(KT):
                dve.wait_ge(x_loaded[kt], 32)
            residual(U_OUT, 0, 1)

            dve.wait_ge(mm_pe, 1)
            nc.vector.tensor_scalar(small[:, 32:34], PS[:, 4, 0:2], 1.0 / D, EPS, ALU.mult, ALU.add).then_inc(mm_dve, 1)
            dve.wait_ge(mm_act, 2)
            nc.vector.reciprocal(small[:, 36:38], small[:, 34:36]).then_inc(mm_dve, 1)
            dve.wait_ge(mm_pe, 2)
            for kt in range(KT):
                nc.vector.scalar_tensor_tensor(cMt[:, kt, :], cMem[:, kt, :], vec[:, V_MEM + kt:V_MEM + kt + 1],
                                               PS[:, 7, 64:64 + MEM], ALU.mult, ALU.mult).then_inc(mm_dve, 1)
            for kt in range(KT):
                dve.wait_ge(mm_act, 2 + kt + 1)
                nc.vector.tensor_tensor(memn[:, kt, 1, :], cMt[:, kt, :], memn[:, kt, 0, :].bitcast(F32),
                                        ALU.subtract).then_inc(mm_dve, 1)
            norm(1)
            scale_and_split(1, 2, V_CA)

            with dve.Fori(0, CA_HEADS) as h:
                def c(ins, name):
                    ins.then_inc(C_DVE.sem, C_DVE.one(name))

                def own(name):
                    dve.wait_ge(C_DVE.sem, C_DVE.at(name, h))

                def crow_max(q):
                    dve.wait_ge(C_PE.sem, C_PE.at(f"s{q}", h))
                    c(nc.vector.tensor_reduce(small[:, q:q + 1], PS[:, 4 + q % 2, 0:MEM], AX_X, ALU.max), f"m{q}")
                    own(f"m{q}")
                    c(nc.vector.tensor_scalar(small[:, 8 + q:9 + q], small[:, q:q + 1], -CA_SCALE, None, ALU.mult),
                      f"b{q}")

                def normalise(q):
                    dve.wait_ge(C_ACT.sem, C_ACT.at(f"e{q}", h))
                    c(nc.vector.reciprocal(small[:, 24 + q:25 + q], small[:, 16 + q:17 + q]), f"r{q}")
                    own(f"r{q}")
                    c(nc.vector.tensor_scalar(cP[q % 2], cP[q % 2], small[:, 24 + q:25 + q], None, ALU.mult), f"p{q}")

                def copy_cpt(q):
                    dve.wait_ge(C_PE.sem, C_PE.at(f"t{q}", h))
                    c(nc.vector.tensor_copy(cPT[q // 4][:, :, P * (q % 4):P * (q % 4) + P],
                                            PS[:, 6 + q % 2, 0:256].rearrange("p (k n) -> p k n", k=2)), f"t{q}")

                def crest(half):
                    for m in range(2):
                        dve.wait_ge(C_ACT.sem, C_ACT.at(f"h{half}{m}", h))
                        dst = xn[:, bass.ds(2 * h + m, 1), :, HALF * half:HALF * half + HALF].rearrange(
                            "p a b t -> p (a b) t")
                        c(nc.vector.tensor_tensor(dst[:, 1, :], PS[:, 2 * half + m, :], dst[:, 0, :].bitcast(F32),
                                                  ALU.subtract), f"l{half}{m}")

                crow_max(0)
                for q in range(1, NW):
                    crow_max(q)
                    normalise(q - 1)
                    copy_cpt(q - 1)
                    if q == 6:
                        crest(0)
                normalise(NW - 1)
                copy_cpt(NW - 1)
                crest(1)

            residual(U_O, 8, 2)
            norm(2)
            scale_and_split(2, 3, V_MLP)

            def hidden(c):
                with dve.Fori(0, 4) as i:
                    for k in range(2):
                        n = 8 * c + 2 * i
                        dve.wait_ge(relu_ready, n + (k + 1))
                        nc.vector.tensor_tensor(tmp[:, k, :], tmp[:, k, :], tmp[:, k, :], ALU.mult).then_inc(
                            hsq_ready, 1)
                        nc.vector.sem_inc(acc_free, 1)
                        dve.wait_ge(hhead_ready, n + (k + 1))
                        dve.wait_ge(hsq_ready, n + (k + 1))
                        dst = hid[:, bass.ds(2 * i + k, 1), :, :].rearrange("p a b t -> p (a b) t")
                        nc.vector.tensor_tensor(dst[:, 1, :], tmp[:, k, :], dst[:, 0, :].bitcast(F32),
                                                ALU.subtract).then_inc(hid_ready, 1)

            with dve.Fori(0, 3) as c:
                hidden(c)
                with dve.Fori(0, 4) as i:
                    for k in range(2):
                        tile = H[:, bass.ds(2 * i + k, 1), :].rearrange("p a t -> p (a t)")
                        dve.wait_ge(acc_ready, 16 * c + 2 * i + (U_MLP + 8 + k + 3))
                        nc.vector.tensor_tensor(tile, two(2 * k), tile, ALU.add).then_inc(h_added, 1)
                        dve.wait_ge(h_added, 8 * c + 2 * i + (16 + k + 1))
                        nc.vector.sem_inc(acc_free, 1)
            hidden(3)
            residual(UNITS - 8, 40, 3)
            norm(3)
            dve.wait_ge(nb_ready, 4)
            for kt in range(KT):
                nc.vector.scalar_tensor_tensor(proj[:, kt, :], H[:, kt, :], vec[:, V_FIN + kt:V_FIN + kt + 1], two(5),
                                               ALU.mult, ALU.mult).then_inc(out_scaled, 1)

        for st in STEPS:
            assert st.next == st.n, st.names


def tiles(w, rows):
    k, n = w.shape
    return w.reshape(k // P, P, n // P, P).transpose(2, 1, 0, 3).reshape(n // P, P, k)


def layout(x, mem, positions, mix_norm, w_in_first, w_in_rest, shift_mu_first, shift_mu_rest,
           mla_q_norm, mla_w_uq, mla_kv_norm, mla_w_ukv, mla_out_norm,
           rwkv_w0, rwkv_w2, rwkv_a0, rwkv_a2, rwkv_g2, rwkv_v0, rwkv_v2,
           rwkv_k_k, rwkv_k_a, rwkv_r_k, rwkv_ln_w, rwkv_ln_b, w_out,
           ca_norm, mem_norm, ca_wq, ca_wkv, ca_wo,
           mlp_norm, mlp_w_up, mlp_w_down, final_norm):
    f32 = np.float32
    rw = 512
    mla = QR + KVR + ROPE
    at = mla + 3 * rw
    cols = np.concatenate([np.arange(0, QR), np.arange(at, at + 64), np.arange(QR, QR + KVR),
                           np.arange(at + 64, at + 160), np.arange(QR + KVR, mla), np.arange(mla, at)])
    w_in = np.asarray(w_in_first)[:, cols]
    mu = np.concatenate([np.zeros(mla, f32), np.asarray(shift_mu_first)])[cols]
    wkv = np.asarray(ca_wkv)[0]
    up, down = np.asarray(mlp_w_up)[0], np.asarray(mlp_w_down)[0]
    units = [tiles(w_in, D), tiles(np.asarray(w_out)[0], D), tiles(wkv[:, :D], D), tiles(wkv[:, D:], D),
             tiles(np.asarray(ca_wq)[0], D), tiles(np.asarray(ca_wo)[0], D)]
    for c in range(4):
        units += [tiles(up[:, D * c:D * c + D], D), tiles(down[D * c:D * c + D], D)]
    vecs = np.zeros((P, NV), f32)

    def put(col, v):
        v = np.asarray(v).reshape(-1, P).T
        vecs[:, col:col + v.shape[1]] = v

    for col, v in ((V_MIX, mix_norm), (V_CA, ca_norm), (V_MLP, mlp_norm), (V_FIN, final_norm), (V_MEM, mem_norm),
                   (V_MU, mu), (V_KVN, mla_kv_norm), (V_ON, mla_out_norm), (V_W0, rwkv_w0), (V_A0, rwkv_a0),
                   (V_KK, rwkv_k_k), (V_KA, rwkv_k_a), (V_RK, rwkv_r_k), (V_LW, rwkv_ln_w), (V_LB, rwkv_ln_b)):
        put(col, v)
    qn = np.asarray(mla_q_norm)[0]
    vecs[:, V_QN] = qn[:P]
    vecs[:QR - P, V_QN + 1] = qn[P:]
    uq = np.asarray(mla_w_uq)[0].reshape(QR, MLA_HEADS, HD + ROPE)
    swap = np.concatenate([np.arange(HD + ROPE), HD + np.arange(ROPE // 2, ROPE), HD + np.arange(ROPE // 2)])
    uq = uq[:, :, swap].transpose(1, 0, 2)
    ukv = np.asarray(mla_w_ukv)[0].reshape(KVR, MLA_HEADS, 2 * HD)
    headw = np.zeros((MLA_HEADS, P, 320), f32)
    headw[:, :, 0:P] = uq[:, :P]
    headw[:, :QR - P, P:2 * P] = uq[:, P:]
    headw[:, :, 2 * P:] = ukv[:, :, :HD].transpose(1, 0, 2)
    wv = ukv[:, :, HD:].reshape(KVR, MLA_HEADS * HD)
    lora = np.zeros((PAIRS, P, 384), f32)
    lora[:, 64:96, 0:P] = np.asarray(rwkv_w2)[0].reshape(32, PAIRS, P).transpose(1, 0, 2)
    lora[:, 96:128, P:2 * P] = np.asarray(rwkv_a2)[0].reshape(32, PAIRS, P).transpose(1, 0, 2)
    lora[:, 0:96, 2 * P:] = np.asarray(rwkv_g2)[0].reshape(96, PAIRS, P).transpose(1, 0, 2)
    return {
        "x": np.asarray(x)[0].T.reshape(KT, P, S), "mem": np.asarray(mem)[0].T.reshape(KT, P, MEM),
        "positions": np.asarray(positions), "weights": np.concatenate(units), "vectors": vecs,
        "constants": constants(), "head_weights": headw, "value_weights": wv, "lora": lora,
    }


def kernel(**inputs):
    import concourse.bacc as bacc
    from concourse.bass_utils import run_bass_kernel_spmd

    nc = bacc.Bacc("TRN2", target_bir_lowering=False, num_devices=1)
    arrays, args = {}, []
    for name, a in layout(**inputs).items():
        a = np.ascontiguousarray(a)
        arrays[f"in_{name}_dram"] = a
        args.append(nc.dram_tensor(f"in_{name}_dram", a.shape, mybir.dt.from_np(a.dtype), kind="ExternalInput").ap())
    args.append(nc.dram_tensor("out_0_dram", (KT, P, S), F32, kind="ExternalOutput").ap())
    build(nc, *args)
    r = run_bass_kernel_spmd(nc, [arrays], core_ids=[0])
    return np.ascontiguousarray(r.results[0]["out_0_dram"].reshape(1, D, S).transpose(0, 2, 1))
```

```python
from contextlib import ExitStack
import math

import numpy as np

import concourse.bass as bass
from concourse import mybir

F32 = mybir.dt.float32
F32R = mybir.dt.float32r
I32 = mybir.dt.int32
ACT = mybir.ActivationFunctionType
ALU = mybir.AluOpType
AX_X = mybir.AxisListType.X

P = 128
D = 1024
S = 1024
KT = D // P
NW = S // P
HALF = 512
MEM = 256
CH = 64
NC = S // CH
HD = 64
BLK = 16
LEVELS = 2
PAD = BLK * (P + 1)
MLA_HEADS = 8
PAIRS = 4
CA_HEADS = 4
QR, KVR, ROPE = 192, 128, 32
EPS = 1e-6
GN_EPS = 64e-5
EXPM05 = math.exp(-0.5)
MLA_SCALE = (HD + ROPE) ** -0.5
CA_SCALE = 256 ** -0.5
MAGIC = 12582912.0

T_CQ, T_CQWA, T_CKV, T_GK, T_R, T_K, T_V = 0, 1, 2, 3, 4, 8, 12

V_MIX, V_CA, V_MLP, V_FIN, V_MEM, V_MU = 0, 8, 16, 24, 32, 40
V_QN, V_KVN, V_ON = 56, 58, 59
V_W0, V_A0, V_KK, V_KA, V_RK, V_LW, V_LB = 63, 67, 71, 75, 79, 83, 87
NV = 91

C_ID, C_MS, C_ML, C_BQ, C_SEL, C_E1, C_E2, C_BO, C_BM, C_RA, C_RB = (
    0, 128, 512, 640, 896, 1152, 1280, 1408, 1536, 1664, 1792)
C_HO, C_ONE, C_INV, C_SGN, C_NH, C_PI2, C_EM, C_EP = 1920, 1922, 1923, 1924, 1925, 1941, 1942, 1943
NCON = 1944

U_IN, U_OUT, U_MK, U_MV, U_Q, U_O, U_MLP = 0, 16, 24, 32, 40, 48, 56
UNITS = U_MLP + 64


def constants():
    c = np.zeros((P, NCON), np.float32)
    i = np.arange(P)
    part, free = i[:, None], i[None, :]
    same = part // CH == free // CH
    c[:, C_ID:C_ID + P] = np.eye(P)
    for n in range(3):
        c[:, C_MS + P * n:C_MS + P * n + P] = same & ((part < free) if n == 1 else (part <= free))
    c[:, C_ML:C_ML + P] = same & (free < part)
    for n in range(LEVELS):
        m = BLK << n
        c[:, C_BQ + P * n:C_BQ + P * n + P] = (
            (part // (2 * m) == free // (2 * m)) & (part % (2 * m) < m) & (free % (2 * m) >= m))
    for h in range(2):
        c[:, C_SEL + P * h:C_SEL + P * h + P] = (free < HD) & (part == free + HD * h)
    r = np.arange(ROPE)
    half = ROPE // 2
    for base in (64, 96):
        c[96 + r, C_E1 + base + r] = 1.0
        c[96 + half + r[:half], C_E2 + base + r[:half]] = -1.0
        c[96 + r[:half], C_E2 + base + half + r[:half]] = 1.0
    c[:, C_BO:C_BO + P] = same
    c[:, C_BM:C_BM + P] = same / HD
    c[:, C_HO:C_HO + 2] = part // HD == free[:, :2]
    c[:, C_ONE] = 1.0
    inv = (10000.0 ** (-np.arange(0, ROPE, 2) / ROPE)).astype(np.float32)
    c[:, C_INV] = inv[i % half]
    c[:, C_SGN] = np.where(i % ROPE < half, -1.0, 1.0)
    c[0, C_RA:C_RA + P] = i < CH
    c[0, C_RB:C_RB + P] = np.where(i >= CH, -1e30, 0.0)
    c[:, C_NH:C_NH + 16] = -0.5
    c[:, C_PI2] = math.pi / 2
    c[:, C_EM] = -0.5 * EXPM05
    c[:, C_EP] = 0.5 * EXPM05
    return c


class Steps:

    def __init__(self, semaphore, names):
        self.sem, self.names, self.n = semaphore, names, len(names)
        self.pos = {name: i + 1 for i, name in enumerate(names)}
        assert len(self.pos) == self.n
        self.next = 0

    def at(self, name, turn=0):
        return (turn + 1) * self.n + self.pos[name]

    def one(self, name):
        assert self.names[self.next % self.n] == name, (self.names[self.next % self.n], name)
        self.next += 1
        return 1


def build(nc, x_t, mem_t, pos, wall, vecs, con_d, headw, wv_d, lora_d, out_t):
    with ExitStack() as ctx:
        def sb(name, shape, dt=F32):
            return ctx.enter_context(nc.sbuf_tensor(name, shape, dt))

        def overlay(*specs):
            made, size = [], 0
            for name, shape, dt in specs:
                with nc.sbuf_tensor(name, shape, dt) as t:
                    made.append(t)
                size = max(size, int(np.prod(shape[1:])))
            sb(specs[0][0] + "_place", [P, size])
            return made

        def sem(name):
            return ctx.enter_context(nc.semaphore(name))

        xn, sa = overlay(("xn", [P, KT, 2, S], F32R), ("sa", [P, 16384], F32))
        proj, hid, sbx, memr = overlay(("proj", [P, 16, S], F32), ("hid", [P, KT, 2, S], F32R),
                                       ("sbx", [P, 16384], F32), ("memr", [P, 16384], F32R))
        H = sb("H", [P, KT, S])
        wraw, sc_w = overlay(("wraw", [P, 2, KT * P], F32), ("sc_w", [P, 2048], F32))
        wsp, sc_s = overlay(("wsp", [P, 2, KT, 2, P], F32R), ("sc_s", [P, 4096], F32))
        con = sb("con", [P, NCON])
        vec = sb("vec", [P, NV])
        omu = sb("omu", [P, 16])
        vech = sb("vech", [P, 12])
        small = sb("small", [P, 128])
        tmp = sb("tmp", [P, 2, S])
        ssum = sb("ssum", [P, S])

        ident = con[:, C_ID:C_ID + P]
        PS = ctx.enter_context(nc.psum_tensor("PS", [P, 8, HALF], F32))

        def two(b):
            return PS[:, b:b + 2, :].rearrange("p a n -> p (a n)")

        def win(w):
            return slice(P * w, P * w + P)

        hs_ = H[:, :, :].rearrange("p k t -> p (k t)")
        mV = sa[:, 12288:16384].rearrange("p (w n) -> p w n", w=NW)
        mO = hs_[:, 0:1024].rearrange("p (w n) -> p w n", w=NW)
        mQ = hs_[:, 1024:2048]
        mK = hs_[:, 2048:3072]
        mP = [hs_[:, 3072:4096], hs_[:, 4096:5120]]
        mPT = [hs_[:, 5120:6144], hs_[:, 6144:7168]]
        mCS = hs_[:, 7168:8192]
        mCos = sa[:, 0:1024]
        mSin = sa[:, 1024:2048]
        mT = [tmp[:, 0, :], tmp[:, 1, :]]
        mOsq = hs_[:, 1024:2048]
        mSt = small[:, 96:112]
        headw_sb = sc_s[:, 2944:3584]
        wv_sb = sc_s[:, 3584:4096]
        posi = sc_w[:, 0:1024].bitcast(I32)

        rAR = sa[:, 0:2048].rearrange("p (w a t) -> p w a t", w=NW, a=2)
        rB = sa[:, 2048:3072]
        rK = sa[:, 3072:4096]
        rBh = sa[:, 4096:5120]
        rKh = sa[:, 5120:6144]
        rW = sa[:, 6144:7168]
        rWi = rBV = sa[:, 7168:8192]
        rT1, rT2, rT3 = (sa[:, 8192 + 1024 * n:9216 + 1024 * n] for n in range(3))
        rY = sa[:, 11264:12288]
        rSt = small[:, 64:96]
        rSC = [t[:, 0:768].rearrange("p (h k n) -> p h k n", h=2, k=3) for t in (rT1, rT2)]
        rQ = [sc_w[:, 256 * n:256 * n + 256].rearrange("p (h n) -> p h n", h=2) for n in range(2)]
        rAL = [place.rearrange("p (w n) -> p w n", w=4) for place in
               [sc_w[:, 512 + 512 * n:1024 + 512 * n] for n in range(3)] + [hs_[:, 1024:1536]]]
        rXX = [hs_[:, 3072 + 512 * w:3584 + 512 * w].rearrange("p (a h n) -> p a h n", a=2, h=2)
               for w in range(NW)]
        bA = sc_s[:, 768:1024].rearrange("p (i n) -> p i n", n=BLK)
        bT = sc_s[:, 1024:1280].rearrange("p (i n) -> p i n", n=BLK)
        bX, bXT = (sc_s[:, 2048 + 256 * k:2304 + 256 * k].rearrange("p (i n) -> p i n", n=BLK) for k in range(2))
        zeros = sa[:, 2048:2048 + PAD]

        matrices = [nc.dram_tensor(name, (P, PAD), F32, kind="Internal").ap() for name in ("a_dram", "x_dram", "xt_dram")]

        def window_in_dram(k, w):
            return matrices[k].rearrange("(w h b) n -> w h (b n)", h=2, b=8)[w, :, 0:P * P].rearrange(
                "h (p n) -> p h n", n=P)

        def head_in_dram(k, n):
            return matrices[k].rearrange("(w h b) n -> w h (b n)", h=2, b=8)[
                4 * (n // 2):4 * (n // 2) + 4, n % 2, 0:P * P].rearrange("w (p n) -> p w n", n=P)

        def blocks_in_dram(k):
            return matrices[k][:, 0:BLK * P].rearrange("p (i n) -> p i n", n=P)[:, :, 0:BLK]

        def wbuf(n, k):
            return sc_s[:, 1280 * n + 256 * k:1280 * n + 256 * k + 256]

        rAG, rBK, rVZ, rPG, rRY = ([wbuf(n, k).rearrange("p (h n) -> p h n", h=2) for n in range(2)]
                                   for k in range(5))
        lora = sc_s[:, 2560:2944]
        rDg, rMT = ([ssum[:, 512 * k + 256 * n:512 * k + 256 * n + 256].rearrange("p (c h n) -> p c h n", c=2, h=2)
                     for n in range(2)] for k in range(2))
        rST = tmp[:, :, :].rearrange("p a (c h n) -> p (a c) h n", h=2, n=HD)
        rWT = small[0:HD, 32:64].rearrange("p (c h) -> p c h", h=2)

        def mixed(t):
            return proj[:, T_K + t if t < 4 else T_R + t - 4, :]

        cQ = sbx[:, 0:8192].rearrange("p (k t) -> p k t", k=KT)
        cMem = sbx[:, 0:2048].rearrange("p (k t) -> p k t", k=KT)
        cMt = sbx[:, 2048:4096].rearrange("p (k t) -> p k t", k=KT)
        cMs = sbx[:, 16128:16384]
        cK = sbx[:, 8192:10240].rearrange("p (k t) -> p k t", k=KT)
        cV = sbx[:, 10240:12288].rearrange("p (k t) -> p k t", k=2)
        memn = memr[:, 12288:16384].rearrange("p (k a t) -> p k a t", k=KT, a=2)
        cVh = sbx[:, 12288:12800].rearrange("p (k n) -> p k n", k=2)
        cP = [sbx[:, 12800 + 256 * n:13056 + 256 * n] for n in range(2)]
        cPT = [sbx[:, 13312 + 1024 * n:14336 + 1024 * n].rearrange("p (k q) -> p k q", k=2) for n in range(2)]
        cQh = tmp[:, :, :]

        con_loaded, vec_loaded = sem("con_loaded"), sem("vec_loaded")
        x_loaded = [sem(f"x_loaded{k}") for k in range(KT)]
        raw_loaded = [sem("raw_loaded0"), sem("raw_loaded1")]
        pos_loaded, wv_loaded, headw_loaded = sem("pos_loaded"), sem("wv_loaded"), sem("headw_loaded")
        lora_loaded, mem_loaded = sem("lora_loaded"), sem("mem_loaded")
        zeros_made, zeros_stored = sem("zeros_made"), sem("zeros_stored")
        a_stored, a_blocks_loaded, x_blocks_stored = sem("a_stored"), sem("a_blocks_loaded"), sem("x_blocks_stored")
        xx_loaded = [sem(f"xx_loaded{g}") for g in range(NW // 2)]
        sp_turn = sem("sp_turn")
        stored = sem("stored")
        vec_made = sem("vec_made")
        w_split = sem("w_split")
        w_head = sem("w_head")
        acc_ready = sem("acc_ready")
        acc_free = sem("acc_free")
        proj_part = sem("proj_part")
        sq_ready = sem("sq_ready")
        sq_added = sem("sq_added")
        nsum_ready, var_ready, std_ready, rstd_ready, nb_ready = (
            sem("nsum_ready"), sem("var_ready"), sem("std_ready"), sem("rstd_ready"), sem("nb_ready"))
        scaled = sem("scaled")
        head_ready = sem("head_ready")
        xn_ready = sem("xn_ready")
        h_added = sem("h_added")
        ssum_zero = sem("ssum_zero")
        pool_turn = sem("pool_turn")
        act_turn = sem("act_turn")
        relu_ready, hsq_ready, hhead_ready, hid_ready = (
            sem("relu_ready"), sem("hsq_ready"), sem("hhead_ready"), sem("hid_ready"))
        ca_hi, ca_lo = sem("ca_hi"), sem("ca_lo")
        out_scaled = sem("out_scaled")

        MP_ACT = Steps(sem("mla_pre_act"), ["sq1", "sq2", "sq3", "sin", "cos", "std"] + [f"v{w}" for w in range(NW)])
        MP_DVE = Steps(sem("mla_pre_dve"), ["posf", "ang", "turns", "m1", "r1", "m2", "r2", "clamp", "abs",
                                            "var1", "var", "rstd", "one", "csc", "css", "kr1", "kr2", "kr",
                                            "cq0", "cq1", "ckv"])
        MP_PE = Steps(sem("mla_pre_pe"), ["e12", "sums", "bq", "bkv"] + [f"v{w}" for w in range(NW)])
        qn = range(NW)
        M_PE = Steps(sem("mla_pe"), ["q", "k", "s0", "s1", "t0"]
                     + [x for q in range(2, NW) for x in (f"s{q}", f"t{q - 1}", f"o{q - 2}")]
                     + ["t7", "o6", "o7"])
        M_ACT = Steps(sem("mla_act"), ["k", "e0"] + [x for q in range(1, NW) for x in (f"e{q}", f"t{q - 1}")] + ["t7"])
        M_DVE = Steps(sem("mla_dve"), ["q", "m0", "b0", "m1", "b1"]
                      + [x for q in range(2, NW) for x in (f"m{q}", f"b{q}", f"r{q - 2}", f"o{q - 2}")]
                      + ["r6", "o6", "r7", "o7"])
        MO_PE = Steps(sem("mla_out_pe"), ["turn"])
        MO_ACT = Steps(sem("mla_out_act"), ["std"])
        MO_DVE = Steps(sem("mla_out_dve"), ["sq", "sum", "var", "rstd", "norm", "out"])
        rp_act, rp_dve = sem("rwkv_set_act"), sem("rwkv_set_dve")

        pe_names = ["lw0", "lw1", "la0", "la1", "kks", "kkb0", "kkb1", "al0", "al1", "al2", "al3", "rk0", "rk1"]
        act_names = ["tw0", "tw1", "ta0", "ta1", "kksq", "dec", "dnv", "afirst", "wt0", "wt1", "vc"]
        dve_names = ["kk", "zk", "kkm", "zb", "nw", "dinv", "f1", "f2", "z1", "z2", "W", "Wi", "nkk0", "nkk1",
                     "at", "na", "b", "bt", "am", "al0", "k2", "al1", "kt", "al2", "rk", "al3", "bv0", "bv1"]
        pool_names = ["pow", "rt", "bh", "kh"]
        for g in range(NW // 2):
            ab = (2 * g, 2 * g + 1)
            for w in ab:
                pe_names += [f"sc{w}"]
                dve_names += [f"sc0_{w}", f"sc1_{w}"]
                pool_names += [f"dg_{w}"]
            if g == 0:
                dve_names += ["x0", "x1"] + [x for j in range(BLK - 1) for x in (f"xm{j}", f"xa{j}")] + ["xt"]
            for w in ab:
                pe_names += [f"tok{w}"]
                act_names += [f"ag{w}", f"bk{w}", f"vz{w}"]
            for w in ab:
                pe_names += [f"akv{w}"]
                act_names += [f"akv{w}"]
            for lv in range(LEVELS):
                pe_names += [f"q{lv}_{w}" for w in ab] + [f"z{lv}_{w}" for w in ab]
                dve_names += [f"q{lv}_{w}" for w in ab] + [f"z{lv}_{w}" for w in ab]
            for st in ("pg", "ry"):
                pe_names += [f"{st}{w}" for w in ab]
                act_names += [f"{st}{w}" for w in ab]
            pe_names += [f"mn{w}" for w in ab]
            for w in ab:
                dve_names += [f"mt0_{w}", f"mt1_{w}"]
            for w in ab:
                for c in (2 * w, 2 * w + 1):
                    if c < NC - 1:
                        pe_names += [f"st{c}"]
                        dve_names += [f"st{c}"]
                    pe_names += [f"y{c}"]
                act_names += [f"y{w}"]
        pe_names += ["mean0", "mean1", "vs", "vb0", "vb1", "lg0", "lg1"]
        act_names += ["ysq"]
        dve_names += ["yc0", "yc1", "var", "yn0", "yn1", "yl", "yb", "out0", "out"]
        pool_names += ["gpow"]
        R_PE, R_ACT, R_DVE, R_POOL = (Steps(sem("rwkv_pe"), pe_names), Steps(sem("rwkv_act"), act_names),
                                      Steps(sem("rwkv_dve"), dve_names), Steps(sem("rwkv_pool"), pool_names))

        mm_act, mm_dve, mm_pe = sem("mem_act"), sem("mem_dve"), sem("mem_pe")
        ca_stage = sem("ca_stage")
        C_PE = Steps(sem("ca_pe"), ["s0"] + [x for q in range(1, NW) for x in
                                             ([f"s{q}", f"t{q - 1}"] + (["o0"] if q == 5 else []))] + ["t7", "o1"])
        C_ACT = Steps(sem("ca_act"), [x for q in range(NW) for x in
                                      ([f"e{q}"] + (["h00", "h01"] if q == 6 else []))] + ["h10", "h11"])
        C_DVE = Steps(sem("ca_dve"), ["m0", "b0"]
                      + [x for q in range(1, NW) for x in
                         ([f"m{q}", f"b{q}", f"r{q - 1}", f"p{q - 1}", f"t{q - 1}"] + (["l00", "l01"] if q == 6 else []))]
                      + ["r7", "p7", "t7", "l10", "l11"])
        STEPS = (MP_ACT, MP_DVE, MP_PE, MO_PE, MO_ACT, MO_DVE, M_PE, M_ACT, M_DVE, R_PE, R_ACT, R_DVE, R_POOL, C_PE, C_ACT, C_DVE)

        block = ctx.enter_context(nc.Block())

        @block.sync
        def _(sp):
            def weights(u0, n):
                with sp.Fori(0, n // 2) as i:
                    for k in range(2):
                        sp.wait_ge(w_split, 2 * i + (u0 + k + 1))
                        sp.dma_start(wraw[:, k, :], wall[bass.ds(2 * i + (u0 + k), 1)].rearrange(
                            "a p n -> (a p) n")).then_inc(raw_loaded[k], 16)

            for kt in range(KT):
                sp.dma_start(H[:, kt, :], x_t[kt]).then_inc(x_loaded[kt], 16)
            sp.dma_start(vec[:, :], vecs).then_inc(vec_loaded, 16)
            sp.dma_start(con[:, :], con_d).then_inc(con_loaded, 16)
            weights(U_IN, 16)

            sp.wait_ge(acc_ready, U_OUT + 2)
            sp.dma_start(posi, pos.broadcast_to([P, S])).then_inc(pos_loaded, 16)
            sp.dma_start(wv_sb, wv_d).then_inc(wv_loaded, 16)
            sp.wait_ge(zeros_made, 1)
            for k in (1, 2):
                sp.dma_start(matrices[k], zeros).then_inc(zeros_stored, 16)
            with sp.Fori(0, PAIRS) as p:
                sp.wait_ge(R_PE.sem, R_PE.at("lg1", p - 1))
                sp.dma_start(lora, lora_d[bass.ds(p, 1)].rearrange("a p n -> (a p) n")).then_inc(lora_loaded, 16)
                sp.wait_ge(M_PE.sem, M_PE.at("k", 2 * p - 1))
                sp.dma_start(headw_sb, headw[bass.ds(p, 1)].rearrange("a p n -> (a p) n")).then_inc(headw_loaded, 16)
                for n in range(4):
                    sp.wait_ge(R_DVE.sem, R_DVE.at(f"al{n}", p))
                    sp.dma_start(head_in_dram(0, n), rAL[n]).then_inc(a_stored, 16)
                sp.wait_ge(a_stored, 64 * (p + 1))
                sp.dma_start(bA, blocks_in_dram(0)).then_inc(a_blocks_loaded, 16)
                sp.wait_ge(R_DVE.sem, R_DVE.at("xt", p))
                sp.dma_start(blocks_in_dram(1), bX).then_inc(x_blocks_stored, 16)
                sp.dma_start(blocks_in_dram(2), bXT).then_inc(x_blocks_stored, 16)
                sp.wait_ge(M_PE.sem, M_PE.at("o7", 2 * p))
                nc.sync.sem_inc(sp_turn, 1)
                sp.wait_ge(x_blocks_stored, 32 * (p + 1))
                for w in range(NW):
                    for k in range(2):
                        sp.dma_start(rXX[w][:, k], window_in_dram(1 + k, w)).then_inc(xx_loaded[w // 2], 16)

            sp.wait_ge(R_DVE.sem, R_DVE.at("out", PAIRS - 1))
            sp.wait_ge(MO_DVE.sem, MO_DVE.at("out", PAIRS - 1))
            sp.wait_ge(M_PE.sem, M_PE.at("o7", MLA_HEADS - 1))
            sp.dma_start(cMem, mem_t.rearrange("k p t -> p k t")).then_inc(mem_loaded, 16)
            weights(U_OUT, 2)
            for kt in range(KT):
                sp.wait_ge(xn_ready, KT + kt + 1)
                sp.dma_start(H[:, kt, :], x_t[kt]).then_inc(x_loaded[kt], 16)
            weights(U_OUT + 2, UNITS - U_OUT - 2)

            for kt in range(KT):
                sp.wait_ge(out_scaled, kt + 1)
                sp.dma_start(out_t[kt], proj[:, kt, :]).then_inc(stored, 16)
            sp.wait_ge(stored, 16 * KT)

        @block.gpsimd
        def _(pool):
            def split_weights(u0, n):
                with pool.Fori(0, n // 2) as i:
                    for k in range(2):
                        raw = wraw[:, k, :].rearrange("p (k n) -> p k n", k=KT)
                        pool.wait_ge(raw_loaded[k], 16 * (i + (u0 // 2 + 1)))
                        pool.wait_ge(acc_ready, 2 * i + (u0 + k + 1))
                        nc.gpsimd.sem_inc(pool_turn, 1)
                        nc.gpsimd.tensor_copy(wsp[:, k, :, 0, :], raw).then_inc(w_head, 1)
                        pool.wait_ge(w_head, 2 * i + (u0 + k + 1))
                        nc.gpsimd.tensor_tensor(wsp[:, k, :, 1, :], raw, wsp[:, k, :, 0, :].bitcast(F32),
                                                ALU.subtract).then_inc(w_split, 1)

            nc.gpsimd.sem_inc(w_split, 2)
            nc.gpsimd.sem_inc(R_POOL.sem, R_POOL.n)
            split_weights(U_IN, 16)

            with pool.Fori(0, PAIRS) as p:
                pool.wait_ge(R_DVE.sem, R_DVE.at("kkm", p))
                nc.gpsimd.tensor_tensor(rSt[:, 16:32], rSt[:, 0:16], con[:, C_NH:C_NH + 16],
                                        ALU.pow).then_inc(R_POOL.sem, R_POOL.one("pow"))
                wt = rW.rearrange("p (c t) -> p c t", c=NC)[:, :, CH - 1:CH].broadcast_to([P, NC, CH])
                pool.wait_ge(R_DVE.sem, R_DVE.at("Wi", p))
                nc.gpsimd.tensor_tensor(rAR[:, :, 1, :], proj[:, bass.ds(p + T_R, 1), :].rearrange(
                    "p a (w t) -> p (a w) t", w=NW), rW.rearrange("p (w t) -> p w t", w=NW),
                    ALU.mult).then_inc(R_POOL.sem, R_POOL.one("rt"))
                pool.wait_ge(R_DVE.sem, R_DVE.at("bt", p))
                nc.gpsimd.tensor_tensor(rBh.rearrange("p (c t) -> p c t", c=NC),
                                        rB.rearrange("p (c t) -> p c t", c=NC), wt,
                                        ALU.mult).then_inc(R_POOL.sem, R_POOL.one("bh"))
                pool.wait_ge(R_DVE.sem, R_DVE.at("kt", p))
                nc.gpsimd.tensor_tensor(rKh.rearrange("p (c t) -> p c t", c=NC),
                                        rK.rearrange("p (c t) -> p c t", c=NC), wt,
                                        ALU.mult).then_inc(R_POOL.sem, R_POOL.one("kh"))
                for w in range(NW):
                    s = w % 2
                    if w == 0:
                        pool.wait_ge(R_ACT.sem, R_ACT.at("wt1", p))
                    if w >= 2:
                        pool.wait_ge(R_DVE.sem, R_DVE.at(f"mt1_{w - 2}", p))
                    nc.gpsimd.tensor_tensor(
                        rDg[s][0:HD],
                        ident[0:HD, 0:HD].rearrange("p (a b n) -> p a b n", a=1, b=1).broadcast_to([HD, 2, 2, HD]),
                        rWT[:, 2 * w:2 * w + 2].rearrange("p c (h n) -> p c h n", n=1).broadcast_to([HD, 2, 2, HD]),
                        ALU.mult).then_inc(R_POOL.sem, R_POOL.one(f"dg_{w}"))
                pool.wait_ge(R_DVE.sem, R_DVE.at("var", p))
                nc.gpsimd.tensor_tensor(rSt[:, 16:32], rSt[:, 0:16], con[:, C_NH:C_NH + 16],
                                        ALU.pow).then_inc(R_POOL.sem, R_POOL.one("gpow"))

            pool.wait_ge(R_PE.sem, R_PE.at("lg1", PAIRS - 1))
            pool.wait_ge(M_PE.sem, M_PE.at("k", MLA_HEADS - 1))
            split_weights(U_OUT, U_O - U_OUT)

            with pool.Fori(0, CA_HEADS) as h:
                pool.wait_ge(C_PE.sem, C_PE.at("o1", h - 1))
                pool.wait_ge(acc_free, U_O + 2)
                pool.wait_ge(xn_ready, 3 * KT)
                nc.gpsimd.sem_inc(pool_turn, 1)
                for k in range(2):
                    nc.gpsimd.tensor_copy(cQh[:, k, :], cQ[:, bass.ds(2 * h + k, 1), :].rearrange(
                        "p a t -> p (a t)")).then_inc(ca_stage, 1)
                    nc.gpsimd.tensor_copy(cVh[:, k, :], cV[:, k, bass.ds(256 * h, 256)]).then_inc(ca_stage, 1)
            split_weights(U_O, UNITS - U_O)

        @block.tensor
        def _(pe):
            nc.tensor.sem_inc(acc_ready, 2)
            for st in (M_PE, MO_PE, R_PE, C_PE):
                nc.tensor.sem_inc(st.sem, st.n)

            def gemm(u0, n, src, ready):
                with pe.Fori(0, n // 2) as i:
                    for k in range(2):
                        unit(2 * i + (u0 + k), k, src, ready)

            def unit(u, k, src, ready):
                pe.wait_ge(w_split, u + 3)
                pe.wait_ge(acc_free, u + 1)
                for kt in range(KT):
                    ready(kt)
                    for a, b in ((0, 0), (0, 1), (1, 0)):
                        for half in range(2):
                            last = nc.tensor.matmul(
                                PS[:, 2 * k + half, :], wsp[:, k, kt, a, :],
                                src[:, kt, b, HALF * half:HALF * half + HALF],
                                start=(kt == 0 and (a, b) == (0, 0)), stop=(kt == KT - 1 and a == 1))
                last.then_inc(acc_ready, 1)

            def norm(n):
                pe.wait_ge(sq_added, KT * (n + 1))
                for w in range(NW):
                    last = nc.tensor.matmul(PS[:, 4, w:w + 1], ssum[:, win(w)], con[:, C_ONE:C_ONE + 1],
                                            start=True, stop=True)
                last.then_inc(nsum_ready, 1)
                pe.wait_ge(rstd_ready, n + 1)
                for w in range(NW):
                    last = nc.tensor.matmul(PS[:, 5 + w // 4, P * (w % 4):P * (w % 4) + P],
                                            small[:, 16 + w:17 + w].broadcast_to([P, P]), ident,
                                            start=True, stop=True)
                last.then_inc(nb_ready, 1)

            def split_ready(n):
                return lambda kt: pe.wait_ge(xn_ready, KT * n + kt + 1)

            pe.wait_ge(con_loaded, 16)
            norm(0)
            gemm(U_IN, 16, xn, split_ready(0))

            pe.wait_ge(acc_free, U_OUT + 2)
            for half in range(2):
                hs = slice(HALF * half, HALF * half + HALF)
                nc.tensor.matmul(PS[:, half, :], con[96:P, C_E1:C_E1 + P], proj[96:P, T_GK, hs], start=True, stop=True)
                last = nc.tensor.matmul(PS[:, 2 + half, :], con[96:P, C_E2:C_E2 + P], proj[96:P, T_GK, hs],
                                        start=True, stop=True)
            last.then_inc(MP_PE.sem, MP_PE.one("e12"))
            pe.wait_ge(MP_ACT.sem, MP_ACT.at("sq3", -1))
            for w in range(NW):
                nc.tensor.matmul(PS[:, 4, w:w + 1], mQ[:, win(w)], con[:, C_ONE:C_ONE + 1], start=True, stop=False)
                nc.tensor.matmul(PS[:, 4, w:w + 1], mK[0:HD, win(w)], con[0:HD, C_ONE:C_ONE + 1], start=False, stop=True)
            for w in range(NW):
                last = nc.tensor.matmul(PS[:, 4, NW + w:NW + w + 1], mP[0][:, win(w)], con[:, C_ONE:C_ONE + 1],
                                        start=True, stop=True)
            last.then_inc(MP_PE.sem, MP_PE.one("sums"))
            pe.wait_ge(MP_DVE.sem, MP_DVE.at("rstd", -1))
            for w in range(NW):
                last = nc.tensor.matmul(PS[:, 5 + w // 4, P * (w % 4):P * (w % 4) + P],
                                        small[:, 32 + w:33 + w].broadcast_to([P, P]), ident, start=True, stop=True)
            last.then_inc(MP_PE.sem, MP_PE.one("bq"))
            pe.wait_ge(MP_DVE.sem, MP_DVE.at("kr2", -1))
            for w in range(NW):
                last = nc.tensor.matmul(PS[:, w // 4, P * (w % 4):P * (w % 4) + P],
                                        small[:, 40 + w:41 + w].broadcast_to([P, P]), ident, start=True, stop=True)
            last.then_inc(MP_PE.sem, MP_PE.one("bkv"))
            pe.wait_ge(wv_loaded, 16)
            pe.wait_ge(MP_DVE.sem, MP_DVE.at("ckv", -1))
            for w in range(NW):
                if w >= 2:
                    pe.wait_ge(MP_ACT.sem, MP_ACT.at(f"v{w - 2}", -1))
                nc.tensor.matmul(PS[:, 4 + w % 2, :], proj[:, T_CKV, win(w)], wv_sb, start=True, stop=True).then_inc(
                    MP_PE.sem, MP_PE.one(f"v{w}"))

            pe.wait_ge(rp_dve, 6)
            pe.wait_ge(rp_act, 2)
            with pe.Fori(0, PAIRS) as p:
                def halves(k):
                    return slice(HALF * k, HALF * k + HALF)

                def head(hd, between):
                    h = 2 * p + hd
                    wq, o = 320 * hd, HD * hd
                    if hd == 0:
                        pe.wait_ge(headw_loaded, 16 * (p + 1))
                    pe.wait_ge(M_ACT.sem, M_ACT.at("t7", h - 1))
                    pe.wait_ge(M_DVE.sem, M_DVE.at("o7", h - 1))
                    for half in range(2):
                        nc.tensor.matmul(PS[:, half, :], headw_sb[:, wq:wq + P], proj[:, T_CQ, halves(half)],
                                         start=True, stop=False)
                        last = nc.tensor.matmul(PS[:, half, :], headw_sb[0:HD, wq + P:wq + 2 * P],
                                                proj[0:HD, T_CQWA, halves(half)], start=False, stop=True)
                    last.then_inc(M_PE.sem, M_PE.one("q"))
                    for half in range(2):
                        last = nc.tensor.matmul(PS[0:HD, 2 + half, :], headw_sb[:, wq + 2 * P:wq + 2 * P + HD],
                                                proj[:, T_CKV, halves(half)], start=True, stop=True)
                    last.then_inc(M_PE.sem, M_PE.one("k"))
                    between("qk")

                    def scores(q):
                        if q == 0:
                            pe.wait_ge(M_DVE.sem, M_DVE.at("q", h))
                            pe.wait_ge(M_ACT.sem, M_ACT.at("k", h))
                        if q >= 2:
                            pe.wait_ge(M_ACT.sem, M_ACT.at(f"e{q - 2}", h))
                        b = 2 * (q % 2)
                        for part in range(q // 4 + 1):
                            n = min(HALF, P * (q + 1) - HALF * part)
                            nc.tensor.matmul(PS[:, b + part, 0:n], mQ[:, win(q)], mK[:, HALF * part:HALF * part + n],
                                             start=True, stop=(part < q // 4))
                        nc.tensor.matmul(PS[:, b + q // 4, P * (q % 4):P * (q % 4) + P], con[0:1, C_RA:C_RA + P],
                                         con[0:1, C_RB:C_RB + P], start=False, stop=True).then_inc(
                            M_PE.sem, M_PE.one(f"s{q}"))

                    def turn(q):
                        pe.wait_ge(M_ACT.sem, M_ACT.at(f"e{q}", h))
                        if q >= 1:
                            pe.wait_ge(M_ACT.sem, M_ACT.at(f"t{q - 1}", h))
                        elif hd == 0:
                            pe.wait_ge(MO_DVE.sem, MO_DVE.at("out", p - 1))
                        for k in range(q + 1):
                            last = nc.tensor.transpose(PS[:, 4 + k // 4, P * (k % 4):P * (k % 4) + P],
                                                       mP[q % 2][:, win(k)], ident)
                        last.then_inc(M_PE.sem, M_PE.one(f"t{q}"))

                    def values(q):
                        pe.wait_ge(M_ACT.sem, M_ACT.at(f"t{q}", h))
                        if q >= 1:
                            pe.wait_ge(M_DVE.sem, M_DVE.at(f"o{q - 1}", h))
                        for k in range(q + 1):
                            last = nc.tensor.matmul(PS[:, 6, 0:HD], mPT[q % 2][:, win(k)],
                                                    mV[:, k, bass.ds(P * p + HD * hd, HD)],
                                                    start=(k == 0), stop=(k == q))
                        last.then_inc(M_PE.sem, M_PE.one(f"o{q}"))

                    scores(0)
                    between(0)
                    for q in range(1, NW):
                        scores(q)
                        turn(q - 1)
                        if q >= 2:
                            values(q - 2)
                        between(q)
                    turn(NW - 1)
                    values(NW - 2)
                    between(8)
                    values(NW - 1)

                def low_rank(name, rows, col, t, free):
                    if free is not None:
                        pe.wait_ge(R_ACT.sem, R_ACT.at(free, p))
                    nc.tensor.matmul(PS[:, 7, :], lora[rows, col:col + P], proj[rows, t, halves(int(name[2]))],
                                     start=True, stop=True).then_inc(R_PE.sem, R_PE.one(name))

                def head_sums(src):
                    for w in range(NW):
                        last = nc.tensor.matmul(PS[:, 7, 2 * w:2 * w + 2], src[:, win(w)],
                                                con[:, C_HO:C_HO + 2], start=True, stop=True)
                    return last

                def spread(half):
                    for w in range(4):
                        for h in range(2):
                            c = 16 + 8 * half + 2 * w + h
                            last = nc.tensor.matmul(PS[HD * h:HD * h + HD, 7, win(w)],
                                                    rSt[:, c:c + 1].broadcast_to([P, HD]), ident,
                                                    start=True, stop=True)
                    return last

                def block_sums(half, mask, src):
                    return nc.tensor.matmul(PS[:, 7, :], con[:, mask:mask + P], src[:, halves(half)],
                                            start=True, stop=True)

                def during_first(q):
                    wa = slice(64, P)
                    if q == "qk":
                        pe.wait_ge(lora_loaded, 16 * (p + 1))
                        pe.wait_ge(R_DVE.sem, R_DVE.at("out", p - 1))
                        low_rank("lw0", wa, 0, T_CQWA, None)
                        low_rank("lw1", wa, 0, T_CQWA, "tw0")
                    if q == 0:
                        low_rank("la0", wa, P, T_CQWA, "tw1")
                        low_rank("la1", wa, P, T_CQWA, "ta0")
                    if q == 1:
                        pe.wait_ge(R_ACT.sem, R_ACT.at("kksq", p))
                        head_sums(rBh).then_inc(R_PE.sem, R_PE.one("kks"))
                    if q == 4:
                        pe.wait_ge(R_POOL.sem, R_POOL.at("pow", p))
                        spread(0).then_inc(R_PE.sem, R_PE.one("kkb0"))
                    if q == 5:
                        pe.wait_ge(R_DVE.sem, R_DVE.at("nkk0", p))
                        spread(1).then_inc(R_PE.sem, R_PE.one("kkb1"))
                    if q == 7:
                        lower(0)
                        lower(1)
                    if q == 8:
                        lower(2)
                        lower(3)

                def lower(n):
                    if n == 0:
                        pe.wait_ge(R_DVE.sem, R_DVE.at("bt", p))
                        pe.wait_ge(R_ACT.sem, R_ACT.at("afirst", p))
                    else:
                        pe.wait_ge(R_DVE.sem, R_DVE.at(f"al{n - 1}", p))
                    rows = slice(HD * (n % 2), HD * (n % 2) + HD)
                    for k in range(4):
                        w = 4 * (n // 2) + k
                        last = nc.tensor.matmul(PS[:, 7, win(k)], rAR[rows, w, 0, :], rB[rows, win(w)],
                                                start=True, stop=True)
                    last.then_inc(R_PE.sem, R_PE.one(f"al{n}"))

                head(0, during_first)
                pe.wait_ge(R_DVE.sem, R_DVE.at("al3", p))
                block_sums(0, C_BO, rT2).then_inc(R_PE.sem, R_PE.one("rk0"))
                pe.wait_ge(R_DVE.sem, R_DVE.at("bv0", p))
                block_sums(1, C_BO, rT2).then_inc(R_PE.sem, R_PE.one("rk1"))

                def scores(w):
                    s, bb = w % 2, 4 * (w % 2)
                    if w == 0:
                        pe.wait_ge(R_POOL.sem, R_POOL.at("rt", p))
                        pe.wait_ge(R_DVE.sem, R_DVE.at("bv1", p))
                        pe.wait_ge(R_ACT.sem, R_ACT.at("afirst", p))
                        pe.wait_ge(M_ACT.sem, M_ACT.at("t7", 2 * p))
                        pe.wait_ge(M_DVE.sem, M_DVE.at("o7", 2 * p))
                    if w >= 2:
                        pe.wait_ge(R_DVE.sem, R_DVE.at(f"mt1_{w - 2}", p))
                        pe.wait_ge(R_DVE.sem, R_DVE.at(f"st{2 * (w - 2) + 1}", p))
                        pe.wait_ge(R_ACT.sem, R_ACT.at(f"y{w - 2}", p))
                    for h in range(2):
                        rows = slice(HD * h, HD * h + HD)
                        nc.tensor.matmul(PS[:, bb + h, 0:P], rB[rows, win(w)], rAR[rows, w, 1, :],
                                         start=True, stop=True)
                        last = nc.tensor.matmul(PS[:, bb + h, P:3 * P], rK[rows, win(w)], rAR[rows, w, :, :],
                                                start=True, stop=True)
                    last.then_inc(R_PE.sem, R_PE.one(f"sc{w}"))

                def tokens(w):
                    bb = 4 * (w % 2)
                    if w == 0:
                        pe.wait_ge(R_POOL.sem, R_POOL.at("kh", p))
                        pe.wait_ge(R_ACT.sem, R_ACT.at("vc", p))
                    pe.wait_ge(R_DVE.sem, R_DVE.at(f"sc0_{w}", p))
                    nc.tensor.transpose(PS[:, bb, 0:P], rAR[:, w, 0, :], ident)
                    nc.tensor.transpose(PS[:, bb, P:2 * P], rBh[:, win(w)], ident)
                    nc.tensor.transpose(PS[:, bb, 2 * P:3 * P], rKh[:, win(w)], ident)
                    nc.tensor.transpose(PS[:, bb, 3 * P:4 * P], rT3[:, win(w)], ident).then_inc(
                        R_PE.sem, R_PE.one(f"tok{w}"))

                def a_v(w):
                    s, bb = w % 2, 4 * (w % 2)
                    pe.wait_ge(R_DVE.sem, R_DVE.at(f"sc1_{w}", p))
                    pe.wait_ge(R_ACT.sem, R_ACT.at(f"vz{w}", p))
                    for h in range(2):
                        last = nc.tensor.matmul(PS[:, bb + 1, HD * h:HD * h + HD], rSC[s][:, h, 1, :],
                                                rVZ[s][:, h, HD:P], start=True, stop=True)
                    last.then_inc(R_PE.sem, R_PE.one(f"akv{w}"))

                def double_q(lv, w):
                    s, bb = w % 2, 4 * (w % 2)
                    if lv == 0:
                        pe.wait_ge(xx_loaded[w // 2], 64 * (p + 1))
                    else:
                        pe.wait_ge(R_DVE.sem, R_DVE.at(f"z{lv - 1}_{w}", p))
                    for h in range(2):
                        last = nc.tensor.matmul(PS[:, bb + 2, win(h)], rAL[2 * (w // 4) + h][:, w % 4, :], rXX[w][:, 1, h, :],
                                                start=True, stop=True)
                    last.then_inc(R_PE.sem, R_PE.one(f"q{lv}_{w}"))

                def double_z(lv, w):
                    s, bb = w % 2, 4 * (w % 2)
                    pe.wait_ge(R_DVE.sem, R_DVE.at(f"q{lv}_{w}", p))
                    for h in range(2):
                        if lv < LEVELS - 1:
                            nc.tensor.matmul(PS[:, bb + 3, win(h)], rQ[s][:, h, :], rXX[w][:, 0, h, :],
                                             start=True, stop=True)
                        last = nc.tensor.matmul(PS[:, bb + 3, win(2 + h)], rXX[w][:, 0, h, :], rQ[s][:, h, :],
                                                start=True, stop=True)
                    last.then_inc(R_PE.sem, R_PE.one(f"z{lv}_{w}"))

                def solve(w):
                    s, bb = w % 2, 4 * (w % 2)
                    pe.wait_ge(R_ACT.sem, R_ACT.at(f"akv{w}", p))
                    pe.wait_ge(R_DVE.sem, R_DVE.at(f"z{LEVELS - 1}_{w}", p))
                    for h in range(2):
                        last = nc.tensor.matmul(PS[:, bb + 2, win(h)], rXX[w][:, 1, h, :], rAG[s][:, h, :],
                                                start=True, stop=True)
                    last.then_inc(R_PE.sem, R_PE.one(f"pg{w}"))

                def local(w):
                    s, bb = w % 2, 4 * (w % 2)
                    pe.wait_ge(R_ACT.sem, R_ACT.at(f"pg{w}", p))
                    for h in range(2):
                        nc.tensor.matmul(PS[:, bb + 3, win(h)], rPG[s][:, h, :], rSC[s][:, h, 0, :],
                                         start=True, stop=False)
                        nc.tensor.matmul(PS[:, bb + 3, win(h)], rVZ[s][:, h, :], rSC[s][:, h, 2, :],
                                         start=False, stop=False)
                        last = nc.tensor.matmul(PS[:, bb + 3, win(h)], con[:, C_SEL + P * h:C_SEL + P * h + P],
                                                rAR[:, w, 1, :], start=False, stop=True)
                    last.then_inc(R_PE.sem, R_PE.one(f"ry{w}"))

                def carry(w):
                    s, bb = w % 2, 4 * (w % 2)
                    for c in range(2):
                        rows = slice(CH * c, CH * c + CH)
                        for h in range(2):
                            hc = slice(HD * h, HD * h + HD)
                            nc.tensor.matmul(PS[:, bb + c, hc], rPG[s][rows, h, :], rBK[s][rows, 0, hc],
                                             start=True, stop=False)
                            last = nc.tensor.matmul(PS[:, bb + c, hc], rVZ[s][rows, h, :], rBK[s][rows, 1, hc],
                                                    start=False, stop=True)
                    last.then_inc(R_PE.sem, R_PE.one(f"mn{w}"))

                def state(c):
                    w = c // 2
                    bb = 4 * (w % 2)
                    pe.wait_ge(R_DVE.sem, R_DVE.at(f"mt1_{w}", p))
                    if c >= 1:
                        pe.wait_ge(R_DVE.sem, R_DVE.at(f"st{c - 1}", p))
                    for h in range(2):
                        last = nc.tensor.matmul(PS[0:HD, bb + 2, HD * h:HD * h + HD], rMT[w % 2][:, c % 2, h, :],
                                                rST[:, c, h, :], start=True, stop=True)
                    last.then_inc(R_PE.sem, R_PE.one(f"st{c}"))

                def outputs(c):
                    w = c // 2
                    s, bb = w % 2, 4 * (w % 2)
                    pe.wait_ge(R_ACT.sem, R_ACT.at(f"ry{w}", p))
                    if c >= 1:
                        pe.wait_ge(R_DVE.sem, R_DVE.at(f"st{c - 1}", p))
                    cc = slice(CH * (c % 2), CH * (c % 2) + CH)
                    for h in range(2):
                        last = nc.tensor.matmul(PS[HD * h:HD * h + HD, bb + 3, cc], rST[:, c, h, :],
                                                rRY[s][:, h, cc], start=True, stop=True)
                    last.then_inc(R_PE.sem, R_PE.one(f"y{c}"))

                for g in range(NW // 2):
                    ab = (2 * g, 2 * g + 1)
                    for stage in (scores, tokens, a_v):
                        for w in ab:
                            stage(w)
                    for lv in range(LEVELS):
                        for w in ab:
                            double_q(lv, w)
                        for w in ab:
                            double_z(lv, w)
                    for stage in (solve, local, carry):
                        for w in ab:
                            stage(w)
                    for c in range(4 * g, 4 * g + 4):
                        if c < NC - 1:
                            state(c)
                        outputs(c)

                pe.wait_ge(R_ACT.sem, R_ACT.at("y7", p))
                pe.wait_ge(R_DVE.sem, R_DVE.at("st14", p))

                def during_second(q):
                    if q == "qk":
                        block_sums(0, C_BM, rY).then_inc(R_PE.sem, R_PE.one("mean0"))
                    if q == 0:
                        pe.wait_ge(R_DVE.sem, R_DVE.at("yc0", p))
                        block_sums(1, C_BM, rY).then_inc(R_PE.sem, R_PE.one("mean1"))
                    if q == 2:
                        pe.wait_ge(R_ACT.sem, R_ACT.at("ysq", p))
                        head_sums(rT1).then_inc(R_PE.sem, R_PE.one("vs"))
                    if q == 4:
                        pe.wait_ge(R_POOL.sem, R_POOL.at("gpow", p))
                        spread(0).then_inc(R_PE.sem, R_PE.one("vb0"))
                    if q == 5:
                        pe.wait_ge(R_DVE.sem, R_DVE.at("yn0", p))
                        spread(1).then_inc(R_PE.sem, R_PE.one("vb1"))
                    if q == 7:
                        pe.wait_ge(R_DVE.sem, R_DVE.at("yn1", p))
                        low_rank("lg0", slice(0, 96), 2 * P, T_GK, None)
                    if q == 8:
                        pe.wait_ge(R_DVE.sem, R_DVE.at("out0", p))
                        low_rank("lg1", slice(0, 96), 2 * P, T_GK, None)

                head(1, during_second)

                pe.wait_ge(MO_DVE.sem, MO_DVE.at("norm", p))
                for w in range(NW):
                    last = nc.tensor.transpose(PS[:, 4 + w // 4, P * (w % 4):P * (w % 4) + P], mO[:, w, :], ident)
                last.then_inc(MO_PE.sem, MO_PE.one("turn"))

            gemm(U_OUT, 8, xn, split_ready(1))

            pe.wait_ge(mm_dve, 8)
            for w in range(2):
                last = nc.tensor.matmul(PS[:, 4, w:w + 1], cMs[:, win(w)], con[:, C_ONE:C_ONE + 1], start=True, stop=True)
            last.then_inc(mm_pe, 1)
            pe.wait_ge(mm_dve, 10)
            for w in range(2):
                last = nc.tensor.matmul(PS[:, 7, P * w + 64:P * w + 64 + P], small[:, 36 + w:37 + w].broadcast_to([P, P]),
                                        ident, start=True, stop=True)
            last.then_inc(mm_pe, 1)
            with pe.Fori(0, 4) as i:
                for k in range(2):
                    pe.wait_ge(w_split, 2 * i + (U_MK + k + 3))
                    pe.wait_ge(acc_free, 2 * i + (U_MK + k + 1))
                    pe.wait_ge(mm_dve, 10 + 2 * KT)
                    for kt in range(KT):
                        for a, b in ((0, 0), (0, 1), (1, 0)):
                            last = nc.tensor.matmul(PS[:, 2 * k, 0:MEM], wsp[:, k, kt, a, :], memn[:, kt, b, :],
                                                    start=(kt == 0 and (a, b) == (0, 0)), stop=(kt == KT - 1 and a == 1))
                    last.then_inc(acc_ready, 1)
            norm(1)
            with pe.Fori(0, 4) as i:
                for k in range(2):
                    pe.wait_ge(w_split, 2 * i + (U_MV + k + 3))
                    pe.wait_ge(acc_free, 2 * i + (U_MV + k + 1))
                    for t in range(2):
                        for kt in range(KT):
                            for a, b in ((0, 0), (0, 1), (1, 0)):
                                last = nc.tensor.matmul(PS[:, 2 * k + t, 0:P], memn[:, kt, b, win(t)],
                                                        wsp[:, k, kt, a, :], start=(kt == 0 and (a, b) == (0, 0)),
                                                        stop=(kt == KT - 1 and a == 1))
                    last.then_inc(acc_ready, 1)
            gemm(U_Q, 8, xn, split_ready(2))

            with pe.Fori(0, CA_HEADS) as h:
                pe.wait_ge(ca_stage, 4 * h + 4)
                pe.wait_ge(acc_free, U_O + 2)

                def cscores(q):
                    if q >= 2:
                        pe.wait_ge(C_ACT.sem, C_ACT.at(f"e{q - 2}", h))
                    else:
                        pe.wait_ge(C_ACT.sem, C_ACT.at(f"e{q + 6}", h - 1))
                    for k in range(2):
                        last = nc.tensor.matmul(PS[:, 4 + q % 2, 0:MEM], cQh[:, k, win(q)],
                                                cK[:, bass.ds(2 * h + k, 1), :].rearrange("p a t -> p (a t)"),
                                                start=(k == 0), stop=(k == 1))
                    last.then_inc(C_PE.sem, C_PE.one(f"s{q}"))

                def cturn(q):
                    pe.wait_ge(C_DVE.sem, C_DVE.at(f"p{q}", h))
                    if q >= 2:
                        pe.wait_ge(C_DVE.sem, C_DVE.at(f"t{q - 2}", h))
                    else:
                        pe.wait_ge(C_DVE.sem, C_DVE.at(f"t{q + 6}", h - 1))
                    for k in range(2):
                        last = nc.tensor.transpose(PS[:, 6 + q % 2, P * k:P * k + P], cP[q % 2][:, win(k)], ident)
                    last.then_inc(C_PE.sem, C_PE.one(f"t{q}"))

                def cvalues(half):
                    pe.wait_ge(C_DVE.sem, C_DVE.at(f"t{4 * half + 3}", h))
                    pe.wait_ge(C_DVE.sem, C_DVE.at(f"l{half}1", h - 1))
                    for m in range(2):
                        for k in range(2):
                            last = nc.tensor.matmul(PS[:, 2 * half + m, :], cVh[:, k, win(m)], cPT[half][:, k, :],
                                                    start=(k == 0), stop=(k == 1))
                    last.then_inc(C_PE.sem, C_PE.one(f"o{half}"))

                cscores(0)
                for q in range(1, NW):
                    cscores(q)
                    cturn(q - 1)
                    if q == 5:
                        cvalues(0)
                cturn(NW - 1)
                cvalues(1)

            def ca_ready(kt):
                pe.wait_ge(C_DVE.sem, C_DVE.at("l11", CA_HEADS - 1))

            gemm(U_O, 8, xn, ca_ready)
            norm(2)

            with pe.Fori(0, 4) as c:
                with pe.Fori(0, 4) as i:
                    for k in range(2):
                        unit(16 * c + 2 * i + (U_MLP + k), k, xn, split_ready(3))
                with pe.Fori(0, 4) as i:
                    for k in range(2):
                        unit(16 * c + 2 * i + (U_MLP + 8 + k), k, hid,
                             lambda kt: pe.wait_ge(hid_ready, 8 * c + kt + 3))
            norm(3)

        @block.scalar
        def _(act):
            for st in (M_ACT, MO_ACT, R_ACT, C_ACT):
                nc.scalar.sem_inc(st.sem, st.n)

            def square(i, src):
                nc.scalar.activation(tmp[:, i % 2, :], src, ACT.Square).then_inc(sq_ready, 1)

            def norm(n):
                act.wait_ge(var_ready, n + 1)
                nc.scalar.activation(small[:, 8:16], small[:, 0:8], ACT.Sqrt).then_inc(std_ready, 1)

            def heads(n):
                for kt in range(KT):
                    act.wait_ge(scaled, KT * n + kt + 1)
                    nc.scalar.copy(xn[:, kt, 0, :], tmp[:, kt % 2, :]).then_inc(head_ready, 1)

            for kt in range(KT):
                act.wait_ge(x_loaded[kt], 16)
                if kt >= 2:
                    act.wait_ge(sq_added, kt - 1)
                square(kt, H[:, kt, :])
            norm(0)
            heads(0)

            act.wait_ge(acc_free, U_OUT + 2)
            act.wait_ge(acc_ready, U_OUT + 2)
            nc.scalar.activation(mQ, proj[:, T_CQ, :], ACT.Square).then_inc(MP_ACT.sem, MP_ACT.one("sq1"))
            nc.scalar.activation(mK[0:HD], proj[0:HD, T_CQWA, :], ACT.Square).then_inc(MP_ACT.sem, MP_ACT.one("sq2"))
            nc.scalar.activation(mP[0], proj[:, T_CKV, :], ACT.Square).then_inc(MP_ACT.sem, MP_ACT.one("sq3"))
            act.wait_ge(MP_DVE.sem, MP_DVE.at("clamp", -1))
            nc.scalar.activation(mSin, mT[0], ACT.Sin).then_inc(MP_ACT.sem, MP_ACT.one("sin"))
            act.wait_ge(MP_DVE.sem, MP_DVE.at("abs", -1))
            nc.scalar.activation(mCos, mT[1], ACT.Sin, bias=con[:, C_PI2:C_PI2 + 1], scale=-1.0).then_inc(
                MP_ACT.sem, MP_ACT.one("cos"))
            act.wait_ge(MP_DVE.sem, MP_DVE.at("var", -1))
            nc.scalar.activation(small[:, 16:32], small[:, 0:16], ACT.Sqrt).then_inc(MP_ACT.sem, MP_ACT.one("std"))
            for w in range(NW):
                act.wait_ge(MP_PE.sem, MP_PE.at(f"v{w}", -1))
                nc.scalar.copy(mV[:, w, :], PS[:, 4 + w % 2, :]).then_inc(MP_ACT.sem, MP_ACT.one(f"v{w}"))

            nc.scalar.activation(proj[64:96, T_CQWA, :], proj[64:96, T_CQWA, :], ACT.Tanh).then_inc(rp_act, 1)
            nc.scalar.activation(proj[0:96, T_GK, :], proj[0:96, T_GK, :], ACT.Tanh, scale=0.5).then_inc(rp_act, 1)

            act.wait_ge(MP_DVE.sem, MP_DVE.at("kr", -1))
            with act.Fori(0, PAIRS) as p:
                half_e = 0.5 * EXPM05

                def par(base):
                    return vech[:, bass.ds(p + base, 1)]

                def halves(k):
                    return slice(HALF * k, HALF * k + HALF)

                def head(hd, between):
                    h = 2 * p + hd
                    act.wait_ge(M_PE.sem, M_PE.at("k", h))
                    nc.scalar.copy(mK[0:HD], two(2)[0:HD]).then_inc(M_ACT.sem, M_ACT.one("k"))
                    between("qk")

                    def turned(q):
                        act.wait_ge(M_PE.sem, M_PE.at(f"t{q}", h))
                        if q >= 2:
                            act.wait_ge(M_PE.sem, M_PE.at(f"o{q - 2}", h))
                        else:
                            act.wait_ge(M_PE.sem, M_PE.at(f"o{q + 6}", h - 1))
                        nc.scalar.copy(mPT[q % 2][:, 0:P * (q + 1)], two(4)[:, 0:P * (q + 1)]).then_inc(
                            M_ACT.sem, M_ACT.one(f"t{q}"))

                    for q in range(NW):
                        n = P * (q + 1)
                        act.wait_ge(M_DVE.sem, M_DVE.at(f"b{q}", h))
                        if q >= 2:
                            act.wait_ge(M_PE.sem, M_PE.at(f"t{q - 2}", h))
                        else:
                            act.wait_ge(M_PE.sem, M_PE.at(f"t{q + 6}", h - 1))
                        nc.scalar.activation(mP[q % 2][:, 0:n], two(2 * (q % 2))[:, 0:n], ACT.Exp,
                                             bias=small[:, 8 + q:9 + q], scale=MLA_SCALE,
                                             accum_out=small[:, 16 + q:17 + q]).then_inc(M_ACT.sem, M_ACT.one(f"e{q}"))
                        if q >= 1:
                            turned(q - 1)
                        between(q)
                    turned(NW - 1)

                def during_first(q):
                    if q == "qk":
                        for k in range(2):
                            act.wait_ge(R_PE.sem, R_PE.at(f"lw{k}", p))
                            nc.scalar.sem_inc(act_turn, 1)
                            nc.scalar.activation(rT1[:, halves(k)], PS[:, 7, :], ACT.Tanh, bias=par(0),
                                                 scale=0.5).then_inc(R_ACT.sem, R_ACT.one(f"tw{k}"))
                    if q == 0:
                        for k in range(2):
                            act.wait_ge(R_PE.sem, R_PE.at(f"la{k}", p))
                            nc.scalar.sem_inc(act_turn, 1)
                            nc.scalar.activation(rK[:, halves(k)], PS[:, 7, :], ACT.Tanh, bias=par(4),
                                                 scale=0.5).then_inc(R_ACT.sem, R_ACT.one(f"ta{k}"))
                        act.wait_ge(R_DVE.sem, R_DVE.at("kk", p))
                        nc.scalar.activation(rBh, rY, ACT.Square).then_inc(R_ACT.sem, R_ACT.one("kksq"))
                    if q == 1:
                        nc.scalar.activation(rT2, rT1, ACT.Exp, bias=con[:, C_EM:C_EM + 1], scale=-half_e).then_inc(
                            R_ACT.sem, R_ACT.one("dec"))
                        nc.scalar.activation(rT3, rT1, ACT.Exp, bias=con[:, C_EP:C_EP + 1], scale=half_e).then_inc(
                            R_ACT.sem, R_ACT.one("dnv"))
                    if q == 6:
                        act.wait_ge(R_DVE.sem, R_DVE.at("nkk1", p))
                        nc.scalar.copy(rAR[:, :, 0, :].rearrange("p w (c t) -> p w c t", c=2)[:, :, :, 0],
                                       rY.rearrange("p (w c t) -> p w c t", w=NW, c=2)[:, :, :, 0]).then_inc(
                            R_ACT.sem, R_ACT.one("afirst"))
                        wt = rW.rearrange("p (c t) -> p c t", c=NC)[:, :, CH - 1]
                        nc.scalar.copy(rWT[:, :, 0], wt[0:HD]).then_inc(R_ACT.sem, R_ACT.one("wt0"))
                        nc.scalar.copy(rWT[:, :, 1], wt[HD:P]).then_inc(R_ACT.sem, R_ACT.one("wt1"))

                head(0, during_first)
                act.wait_ge(R_DVE.sem, R_DVE.at("bt", p))
                nc.scalar.copy(rT3, proj[:, bass.ds(p + T_V, 1), :].rearrange("p a t -> p (a t)")).then_inc(
                    R_ACT.sem, R_ACT.one("vc"))
                for g in range(NW // 2):
                    ab = (2 * g, 2 * g + 1)
                    for w in ab:
                        s, bb = w % 2, 4 * (w % 2)
                        tok = PS[:, bb, :].rearrange("p (k h n) -> p k h n", k=4, h=2)
                        act.wait_ge(R_PE.sem, R_PE.at(f"tok{w}", p))
                        nc.scalar.copy(rAG[s][:, :, 0:HD], tok[:, 0]).then_inc(R_ACT.sem, R_ACT.one(f"ag{w}"))
                        nc.scalar.copy(rBK[s].rearrange("p k (h n) -> p k h n", h=2), tok[:, 1:3]).then_inc(
                            R_ACT.sem, R_ACT.one(f"bk{w}"))
                        nc.scalar.copy(rVZ[s][:, :, HD:P], tok[:, 3]).then_inc(R_ACT.sem, R_ACT.one(f"vz{w}"))
                    for w in ab:
                        s, bb = w % 2, 4 * (w % 2)
                        act.wait_ge(R_PE.sem, R_PE.at(f"akv{w}", p))
                        nc.scalar.copy(rAG[s][:, :, HD:P], PS[:, bb + 1, 0:P].rearrange("p (h n) -> p h n", h=2)
                                       ).then_inc(R_ACT.sem, R_ACT.one(f"akv{w}"))
                    for w in ab:
                        s, bb = w % 2, 4 * (w % 2)
                        act.wait_ge(R_PE.sem, R_PE.at(f"pg{w}", p))
                        nc.scalar.copy(rPG[s].rearrange("p h n -> p (h n)"), PS[:, bb + 2, 0:256]).then_inc(
                            R_ACT.sem, R_ACT.one(f"pg{w}"))
                    for w in ab:
                        s, bb = w % 2, 4 * (w % 2)
                        act.wait_ge(R_PE.sem, R_PE.at(f"ry{w}", p))
                        nc.scalar.copy(rRY[s].rearrange("p h n -> p (h n)"), PS[:, bb + 3, 0:256]).then_inc(
                            R_ACT.sem, R_ACT.one(f"ry{w}"))
                    for w in ab:
                        act.wait_ge(R_PE.sem, R_PE.at(f"y{2 * w + 1}", p))
                        nc.scalar.copy(rY[:, win(w)], PS[:, 4 * (w % 2) + 3, 0:P]).then_inc(
                            R_ACT.sem, R_ACT.one(f"y{w}"))

                def during_second(q):
                    if q == 1:
                        act.wait_ge(R_DVE.sem, R_DVE.at("yc1", p))
                        nc.scalar.activation(rT1, rY, ACT.Square).then_inc(R_ACT.sem, R_ACT.one("ysq"))

                head(1, during_second)
                act.wait_ge(MO_DVE.sem, MO_DVE.at("var", p))
                nc.scalar.activation(mSt, mSt, ACT.Sqrt).then_inc(MO_ACT.sem, MO_ACT.one("std"))

            for kt in range(KT):
                act.wait_ge(R_DVE.sem, R_DVE.at("out", PAIRS - 1))
                act.wait_ge(MO_DVE.sem, MO_DVE.at("out", PAIRS - 1))
                nc.scalar.copy(xn[:, kt, 0, :], mixed(kt)).then_inc(head_ready, 1)

            act.wait_ge(mem_loaded, 16)
            nc.scalar.activation(cMt, cMem, ACT.Square).then_inc(mm_act, 1)

            def residual_squares(u0, n):
                with act.Fori(0, 4) as i:
                    for k in range(2):
                        act.wait_ge(h_added, 2 * i + (u0 + k + 1))
                        act.wait_ge(sq_added, 2 * i + (KT * n + k - 1))
                        square(k, H[:, bass.ds(2 * i + k, 1), :].rearrange("p a t -> p (a t)"))

            residual_squares(0, 1)
            act.wait_ge(mm_dve, 9)
            nc.scalar.activation(small[:, 34:36], small[:, 32:34], ACT.Sqrt).then_inc(mm_act, 1)
            for kt in range(KT):
                act.wait_ge(mm_dve, 10 + kt + 1)
                nc.scalar.copy(memn[:, kt, 0, :], cMt[:, kt, :]).then_inc(mm_act, 1)
            with act.Fori(0, 4) as i:
                for k in range(2):
                    act.wait_ge(acc_ready, 2 * i + (U_MK + k + 3))
                    nc.scalar.copy(cK[:, bass.ds(2 * i + k, 1), :].rearrange("p a t -> p (a t)"),
                                   PS[:, 2 * k, 0:MEM]).then_inc(acc_free, 1)
            norm(1)
            heads(1)
            with act.Fori(0, 4) as i:
                for k in range(2):
                    act.wait_ge(acc_ready, 2 * i + (U_MV + k + 3))
                    nc.scalar.copy(cV[:, :, bass.ds(256 * i + P * k, P)], PS[:, 2 * k:2 * k + 2, 0:P]).then_inc(
                        acc_free, 1)
            with act.Fori(0, 4) as i:
                for k in range(2):
                    act.wait_ge(acc_ready, 2 * i + (U_Q + k + 3))
                    nc.scalar.copy(cQ[:, bass.ds(2 * i + k, 1), :].rearrange("p a t -> p (a t)"),
                                   two(2 * k)).then_inc(acc_free, 1)

            with act.Fori(0, CA_HEADS) as h:
                def cheads(half):
                    act.wait_ge(C_PE.sem, C_PE.at(f"o{half}", h))
                    for m in range(2):
                        nc.scalar.copy(xn[:, bass.ds(2 * h + m, 1), 0, HALF * half:HALF * half + HALF].rearrange(
                            "p a t -> p (a t)"), PS[:, 2 * half + m, :]).then_inc(C_ACT.sem, C_ACT.one(f"h{half}{m}"))

                for q in range(NW):
                    act.wait_ge(C_DVE.sem, C_DVE.at(f"b{q}", h))
                    if q >= 2:
                        act.wait_ge(C_PE.sem, C_PE.at(f"t{q - 2}", h))
                    else:
                        act.wait_ge(C_PE.sem, C_PE.at(f"t{q + 6}", h - 1))
                    nc.scalar.activation(cP[q % 2], PS[:, 4 + q % 2, 0:MEM], ACT.Exp, bias=small[:, 8 + q:9 + q],
                                         scale=CA_SCALE, accum_out=small[:, 16 + q:17 + q]).then_inc(
                        C_ACT.sem, C_ACT.one(f"e{q}"))
                    if q == 6:
                        cheads(0)
                cheads(1)

            residual_squares(8, 2)
            norm(2)
            heads(2)

            def hidden(c):
                with act.Fori(0, 4) as i:
                    for k in range(2):
                        n = 8 * c + 2 * i
                        act.wait_ge(acc_ready, 16 * c + 2 * i + (U_MLP + k + 3))
                        act.wait_ge(hid_ready, n + (k + 1))
                        nc.scalar.activation(tmp[:, k, :], two(2 * k), ACT.Relu).then_inc(relu_ready, 1)
                        act.wait_ge(hsq_ready, n + (k + 1))
                        nc.scalar.copy(hid[:, bass.ds(2 * i + k, 1), 0, :].rearrange("p a t -> p (a t)"),
                                       tmp[:, k, :]).then_inc(hhead_ready, 1)

            with act.Fori(0, 4) as c:
                hidden(c)
            residual_squares(40, 3)
            norm(3)

        @block.vector
        def _(dve):
            nc.vector.sem_inc(acc_free, 2)
            nc.vector.sem_inc(hid_ready, 2)
            for st in (M_DVE, MO_DVE, R_DVE, C_DVE):
                nc.vector.sem_inc(st.sem, st.n)

            def norm(n):
                dve.wait_ge(nsum_ready, n + 1)
                nc.vector.tensor_scalar(small[:, 0:8], PS[:, 4, 0:NW], 1.0 / D, EPS, ALU.mult, ALU.add).then_inc(
                    var_ready, 1)
                dve.wait_ge(std_ready, n + 1)
                nc.vector.reciprocal(small[:, 16:24], small[:, 8:16]).then_inc(rstd_ready, 1)

            def scale_and_split(n, pas, gain):
                def rest(kt):
                    dve.wait_ge(head_ready, KT * pas + kt + 1)
                    nc.vector.tensor_tensor(xn[:, kt, 1, :], tmp[:, kt % 2, :], xn[:, kt, 0, :].bitcast(F32),
                                            ALU.subtract).then_inc(xn_ready, 1)

                dve.wait_ge(nb_ready, n + 1)
                for kt in range(KT):
                    if kt >= 2:
                        dve.wait_ge(xn_ready, KT * pas + kt - 1)
                    nc.vector.scalar_tensor_tensor(tmp[:, kt % 2, :], H[:, kt, :], vec[:, gain + kt:gain + kt + 1],
                                                   two(5), ALU.mult, ALU.mult).then_inc(scaled, 1)
                    if kt >= 1:
                        rest(kt - 1)
                rest(KT - 1)

            for kt in range(KT):
                dve.wait_ge(sq_ready, kt + 1)
                if kt == 0:
                    nc.vector.tensor_copy(ssum[:, :], tmp[:, 0, :]).then_inc(sq_added, 1)
                else:
                    dve.wait_ge(sq_added, kt)
                    nc.vector.tensor_tensor(ssum[:, :], ssum[:, :], tmp[:, kt % 2, :], ALU.add).then_inc(sq_added, 1)
            dve.wait_ge(vec_loaded, 16)
            nc.vector.tensor_scalar(omu[:, :], vec[:, V_MU:V_MU + 16], -1.0, 1.0, ALU.mult, ALU.add).then_inc(vec_made, 1)
            nc.vector.tensor_scalar(vech[:, 0:8], vec[:, V_W0:V_W0 + 8], 0.5, None, ALU.mult).then_inc(vec_made, 1)
            nc.vector.tensor_scalar(vech[:, 8:12], vec[:, V_KA:V_KA + 4], 0.5, None, ALU.mult).then_inc(vec_made, 1)
            norm(0)
            scale_and_split(0, 0, V_MIX)

            dve.wait_ge(vec_made, 3)
            with dve.Fori(0, 8) as i:
                for k in range(2):
                    u = 2 * i + k
                    cur = proj[:, bass.ds(u, 1), :].rearrange("p a t -> p (a t)")
                    rest = proj[:, bass.ds(u, 1), 1:S].rearrange("p a t -> p (a t)")
                    dve.wait_ge(acc_ready, u + 3)
                    nc.vector.tensor_scalar(cur, two(2 * k), omu[:, bass.ds(u, 1)], None, ALU.mult).then_inc(proj_part, 1)
                    dve.wait_ge(proj_part, u + 1)
                    nc.vector.scalar_tensor_tensor(rest, two(2 * k)[:, 0:S - 1], vec[:, bass.ds(u + V_MU, 1)], rest,
                                                   ALU.mult, ALU.add).then_inc(acc_free, 1)

            def mp(ins, name):
                ins.then_inc(MP_DVE.sem, MP_DVE.one(name))

            def after(name):
                dve.wait_ge(MP_DVE.sem, MP_DVE.at(name, -1))

            dve.wait_ge(con_loaded, 16)
            dve.wait_ge(pos_loaded, 16)
            mp(nc.vector.tensor_copy(mT[0], posi), "posf")
            after("posf")
            mp(nc.vector.tensor_scalar(mT[0], mT[0], con[:, C_INV:C_INV + 1], None, ALU.mult), "ang")
            after("ang")
            mp(nc.vector.tensor_scalar(mT[1], mT[0], 1.0 / (2 * math.pi), MAGIC, ALU.mult, ALU.add), "turns")
            after("turns")
            mp(nc.vector.tensor_scalar(mCos, mT[1], -MAGIC, -6.28125, ALU.add, ALU.mult), "m1")
            after("m1")
            mp(nc.vector.tensor_tensor(mT[0], mT[0], mCos, ALU.add), "r1")
            mp(nc.vector.tensor_scalar(mT[1], mT[1], -MAGIC, -(2 * math.pi - 6.28125), ALU.add, ALU.mult), "m2")
            after("m2")
            mp(nc.vector.tensor_tensor(mT[0], mT[0], mT[1], ALU.add), "r2")
            after("r2")
            mp(nc.vector.tensor_scalar(mT[0], mT[0], 3.1415925, -3.1415925, ALU.min, ALU.max), "clamp")
            after("clamp")
            mp(nc.vector.scalar_tensor_tensor(mT[1], mT[0], -1.0, mT[0], ALU.mult, ALU.max), "abs")
            dve.wait_ge(MP_PE.sem, MP_PE.at("sums", -1))
            mp(nc.vector.tensor_scalar(small[:, 0:8], PS[:, 4, 0:8], 1.0 / QR, EPS, ALU.mult, ALU.add), "var1")
            mp(nc.vector.tensor_scalar(small[:, 8:16], PS[:, 4, 8:16], 1.0 / KVR, EPS, ALU.mult, ALU.add), "var")
            dve.wait_ge(MP_ACT.sem, MP_ACT.at("std", -1))
            mp(nc.vector.reciprocal(small[:, 32:48], small[:, 16:32]), "rstd")
            mp(nc.vector.memset(mCS[0:HD], 1.0), "one")
            mp(nc.vector.tensor_copy(mCS[64:96], mCos[64:96]), "csc")
            mp(nc.vector.tensor_scalar(mCS[96:P], mSin[96:P], con[96:P, C_SGN:C_SGN + 1], None, ALU.mult), "css")
            dve.wait_ge(MP_PE.sem, MP_PE.at("e12", -1))
            mp(nc.vector.tensor_tensor(mT[0][HD:P], two(0)[HD:P], mCos[HD:P], ALU.mult), "kr1")
            mp(nc.vector.tensor_tensor(mT[1][HD:P], two(2)[HD:P], mSin[HD:P], ALU.mult), "kr2")
            after("kr2")
            mp(nc.vector.tensor_tensor(mK[HD:P], mT[0][HD:P], mT[1][HD:P], ALU.add), "kr")
            dve.wait_ge(MP_PE.sem, MP_PE.at("bq", -1))
            mp(nc.vector.scalar_tensor_tensor(proj[:, T_CQ, :], proj[:, T_CQ, :], vec[:, V_QN:V_QN + 1], two(5),
                                              ALU.mult, ALU.mult), "cq0")
            mp(nc.vector.scalar_tensor_tensor(proj[0:HD, T_CQWA, :], proj[0:HD, T_CQWA, :],
                                              vec[0:HD, V_QN + 1:V_QN + 2], two(5)[0:HD], ALU.mult, ALU.mult), "cq1")
            dve.wait_ge(MP_PE.sem, MP_PE.at("bkv", -1))
            mp(nc.vector.scalar_tensor_tensor(proj[:, T_CKV, :], proj[:, T_CKV, :], vec[:, V_KVN:V_KVN + 1], two(0),
                                              ALU.mult, ALU.mult), "ckv")

            nc.vector.memset(zeros, 0.0).then_inc(zeros_made, 1)
            dve.wait_ge(MP_DVE.sem, MP_DVE.at("ckv", -1))
            nc.vector.tensor_copy(rST[HD:P], ident[HD:P, HD:P].rearrange("p (a b n) -> p a b n", a=1, b=1)
                                  .broadcast_to([HD, NC, 2, HD])).then_inc(rp_dve, 1)
            nc.vector.memset(rST[0:HD, 0], 0.0).then_inc(rp_dve, 1)
            for s in range(2):
                nc.vector.memset(rVZ[s][:, :, 0:HD], 0.0).then_inc(rp_dve, 1)
            nc.vector.memset(ssum[HD:P, 0:512], 0.0).then_inc(rp_dve, 1)
            dve.wait_ge(rp_act, 2)
            nc.vector.tensor_scalar(proj[0:96, T_GK, :], proj[0:96, T_GK, :], 0.5, 0.5, ALU.mult, ALU.add).then_inc(
                rp_dve, 1)

            dve.wait_ge(zeros_stored, 32)
            with dve.Fori(0, PAIRS) as p:
                def r(ins, name):
                    ins.then_inc(R_DVE.sem, R_DVE.one(name))

                def own(name):
                    dve.wait_ge(R_DVE.sem, R_DVE.at(name, p))

                def of_act(name):
                    dve.wait_ge(R_ACT.sem, R_ACT.at(name, p))

                def of_pe(name):
                    dve.wait_ge(R_PE.sem, R_PE.at(name, p))

                def of_pool(name):
                    dve.wait_ge(R_POOL.sem, R_POOL.at(name, p))

                def tile(base):
                    return proj[:, bass.ds(p + base, 1), :].rearrange("p a t -> p (a t)")

                def half_tile(base, k):
                    return proj[:, bass.ds(p + base, 1), HALF * k:HALF * k + HALF].rearrange("p a t -> p (a t)")

                def par(base):
                    return vec[:, bass.ds(p + base, 1)]

                def chunks(ap):
                    return ap.rearrange("p (c t) -> p c t", c=NC)

                def halves(k):
                    return slice(HALF * k, HALF * k + HALF)

                def head(hd, between):
                    h = 2 * p + hd

                    def m(ins, name):
                        ins.then_inc(M_DVE.sem, M_DVE.one(name))

                    def mown(name):
                        dve.wait_ge(M_DVE.sem, M_DVE.at(name, h))

                    dve.wait_ge(M_PE.sem, M_PE.at("q", h))
                    m(nc.vector.tensor_tensor(mQ, two(0), mCS, ALU.mult), "q")

                    def row_max(q):
                        dve.wait_ge(M_PE.sem, M_PE.at(f"s{q}", h))
                        m(nc.vector.tensor_reduce(small[:, q:q + 1], two(2 * (q % 2))[:, 0:P * (q + 1)], AX_X,
                                                  ALU.max), f"m{q}")
                        mown(f"m{q}")
                        m(nc.vector.tensor_scalar(small[:, 8 + q:9 + q], small[:, q:q + 1], -MLA_SCALE, None,
                                                  ALU.mult), f"b{q}")

                    def divide(q):
                        m(nc.vector.reciprocal(small[:, 24 + q:25 + q], small[:, 16 + q:17 + q]), f"r{q}")
                        dve.wait_ge(M_PE.sem, M_PE.at(f"o{q}", h))
                        mown(f"r{q}")
                        m(nc.vector.tensor_scalar(mO[:, q, HD * hd:HD * hd + HD], PS[:, 6, 0:HD],
                                                  small[:, 24 + q:25 + q], None, ALU.mult), f"o{q}")

                    row_max(0)
                    between(0)
                    for q in range(1, NW):
                        row_max(q)
                        if q >= 2:
                            divide(q - 2)
                        between(q)
                    divide(NW - 2)
                    between(8)
                    divide(NW - 1)

                of_pe("lw0")
                r(nc.vector.tensor_scalar(rY, tile(T_K), par(V_KK), None, ALU.mult), "kk")

                def during_first(q):
                    if q == 1:
                        r(nc.vector.memset(rKh, 0.0), "zk")
                    if q == 2:
                        of_pe("kks")
                        r(nc.vector.tensor_scalar(rSt[:, 0:16], PS[:, 7, 0:16], 1e-24, None, ALU.max), "kkm")
                        r(nc.vector.memset(rBh, 0.0), "zb")
                        of_act("dnv")
                        r(nc.vector.tensor_tensor(rWi, rT2, rT3, ALU.mult), "nw")
                        own("nw")
                        r(nc.vector.scalar_tensor_tensor(rT3, rWi, 2.0, rT3, ALU.subtract, ALU.mult,
                                                         reverse0=True), "dinv")
                        own("dinv")
                    if q == 3:
                        r(nc.vector.tensor_copy(chunks(rBh)[:, :, 0:1], chunks(rT2)[:, :, 0:1]), "f1")
                        r(nc.vector.tensor_copy(chunks(rKh)[:, :, 0:1], chunks(rT3)[:, :, 0:1]), "f2")
                        own("f2")
                        r(nc.vector.memset(chunks(rT2)[:, :, 0:1], 0.0), "z1")
                        r(nc.vector.memset(chunks(rT3)[:, :, 0:1], 0.0), "z2")
                        own("z2")
                        r(nc.vector.tensor_tensor_scan(rW, rT2, rBh, 0.0, ALU.mult, ALU.add), "W")
                    if q == 4:
                        r(nc.vector.tensor_tensor_scan(rWi, rT3, rKh, 0.0, ALU.mult, ALU.add), "Wi")
                    if q == 5:
                        for k in range(2):
                            of_pe(f"kkb{k}")
                            r(nc.vector.scalar_tensor_tensor(rY[:, halves(k)], rY[:, halves(k)], -1.0, PS[:, 7, :],
                                                             ALU.mult, ALU.mult), f"nkk{k}")
                        own("nkk1")
                        r(nc.vector.tensor_tensor(
                            rAR[:, :, 0, :].rearrange("p w (c t) -> p w c t", c=2)[:, :, :, 1:CH],
                            rY.rearrange("p (w c t) -> p w c t", w=NW, c=2)[:, :, :, 1:CH],
                            rW.rearrange("p (w c t) -> p w c t", w=NW, c=2)[:, :, :, 0:CH - 1], ALU.mult), "at")
                    if q == 6:
                        of_act("ta1")
                        r(nc.vector.tensor_scalar(rT2, rK, -0.5, -0.5, ALU.mult, ALU.add), "na")
                        own("na")
                        r(nc.vector.tensor_tensor(rT3, rT2, rY, ALU.mult), "b")
                        own("b")
                        r(nc.vector.tensor_tensor(rB, rT3, rWi, ALU.mult), "bt")
                        r(nc.vector.tensor_scalar(rT1, rK, -1.0, vech[:, bass.ds(p + 8, 1)], ALU.add, ALU.mult),
                          "am")
                    if q == 7:
                        lower(0)
                        own("am")
                        r(nc.vector.scalar_tensor_tensor(rT1, rT1, 1.0, tile(T_K), ALU.add, ALU.mult), "k2")
                        lower(1)
                        own("k2")
                        r(nc.vector.tensor_tensor(rK, rT1, rWi, ALU.mult), "kt")
                    if q == 8:
                        lower(2)
                        r(nc.vector.scalar_tensor_tensor(rT2, tile(T_R), par(V_RK), rT1, ALU.mult, ALU.mult), "rk")
                        lower(3)

                def lower(n):
                    of_pe(f"al{n}")
                    r(nc.vector.tensor_tensor(
                        rAL[n], PS[:, 7, :].rearrange("p (a n) -> p a n", a=4),
                        con[:, C_ML:C_ML + P].rearrange("p (a n) -> p a n", a=1).broadcast_to([P, 4, P]), ALU.mult),
                        f"al{n}")

                def invert_blocks():
                    r(nc.vector.memset(sc_s[:, 2048:2304], 0.0), "x0")
                    own("x0")
                    r(nc.vector.memset(sc_s[:, 2048:2304:BLK + 1], 1.0), "x1")
                    own("x1")
                    dve.wait_ge(a_blocks_loaded, 16 * (p + 1))
                    for j in range(BLK - 1):
                        shape = [P, BLK - 1 - j, j + 1]
                        below, part = bX[:, j + 1:BLK, 0:j + 1], bT[:, j + 1:BLK, 0:j + 1]
                        r(nc.vector.tensor_tensor(part, bA[:, j + 1:BLK, j:j + 1].broadcast_to(shape),
                                                  bX[:, j:j + 1, 0:j + 1].broadcast_to(shape), ALU.mult), f"xm{j}")
                        own(f"xm{j}")
                        r(nc.vector.tensor_tensor(below, below, part, ALU.add), f"xa{j}")
                        own(f"xa{j}")
                    r(nc.vector.tensor_copy(bXT, bX.rearrange("p i n -> p n i")), "xt")

                head(0, during_first)
                for k in range(2):
                    of_pe(f"rk{k}")
                    r(nc.vector.tensor_tensor(rBV[:, halves(k)], PS[:, 7, :], half_tile(T_V, k), ALU.mult), f"bv{k}")

                for g in range(NW // 2):
                    ab = (2 * g, 2 * g + 1)
                    for w in ab:
                        s, bb = w % 2, 4 * (w % 2)
                        of_pe(f"sc{w}")
                        for hh in range(2):
                            r(nc.vector.tensor_tensor(rSC[s][:, hh].rearrange("p k n -> p (k n)"),
                                                      PS[:, bb + hh, 0:3 * P], con[:, C_MS:C_MS + 3 * P], ALU.mult),
                              f"sc{hh}_{w}")
                    if g == 0:
                        invert_blocks()
                    for lv in range(LEVELS):
                        for w in ab:
                            s, bb = w % 2, 4 * (w % 2)
                            of_pe(f"q{lv}_{w}")
                            mask = con[:, C_BQ + P * lv:C_BQ + P * lv + P].rearrange("p (a n) -> p a n", a=1)
                            r(nc.vector.tensor_tensor(rQ[s], PS[:, bb + 2, 0:256].rearrange("p (h n) -> p h n", h=2),
                                                      mask.broadcast_to([P, 2, P]), ALU.mult), f"q{lv}_{w}")
                        for w in ab:
                            s, bb = w % 2, 4 * (w % 2)
                            of_pe(f"z{lv}_{w}")
                            lo = 0 if lv < LEVELS - 1 else 256
                            xx = rXX[w].rearrange("p a h n -> p (a h n)")[:, lo:512]
                            r(nc.vector.tensor_tensor(xx, PS[:, bb + 3, lo:512], xx, ALU.add), f"z{lv}_{w}")
                    for w in ab:
                        s, bb = w % 2, 4 * (w % 2)
                        of_pool(f"dg_{w}")
                        of_pe(f"mn{w}")
                        for c in range(2):
                            r(nc.vector.tensor_tensor(rMT[s][:, c].rearrange("p h n -> p (h n)"), PS[:, bb + c, 0:P],
                                                      rDg[s][:, c].rearrange("p h n -> p (h n)"), ALU.add),
                              f"mt{c}_{w}")
                    for c in range(4 * g, min(4 * g + 4, NC - 1)):
                        w = c // 2
                        of_pe(f"st{c}")
                        r(nc.vector.tensor_copy(rST[0:HD, c + 1].rearrange("p h n -> p (h n)"),
                                                PS[0:HD, 4 * (w % 2) + 2, 0:P]), f"st{c}")

                def during_second(q):
                    if q in (0, 1):
                        k = q
                        of_pe(f"mean{k}")
                        r(nc.vector.tensor_tensor(rY[:, halves(k)], rY[:, halves(k)], PS[:, 7, :], ALU.subtract),
                          f"yc{k}")
                    if q == 3:
                        of_pe("vs")
                        r(nc.vector.tensor_scalar(rSt[:, 0:16], PS[:, 7, 0:16], 1.0 / HD, GN_EPS, ALU.mult,
                                                  ALU.add), "var")
                    if q in (5, 6):
                        k = q - 5
                        of_pe(f"vb{k}")
                        r(nc.vector.tensor_tensor(rT2[:, halves(k)], rY[:, halves(k)], PS[:, 7, :], ALU.mult),
                          f"yn{k}")
                    if q == 7:
                        own("yn1")
                        r(nc.vector.tensor_scalar(rT2, rT2, par(V_LW), par(V_LB), ALU.mult, ALU.add), "yl")
                        own("yl")
                        r(nc.vector.tensor_tensor(rT2, rT2, rBV, ALU.add), "yb")
                        own("yb")
                        of_pe("lg0")
                        r(nc.vector.tensor_tensor(half_tile(T_R, 0), rT2[:, halves(0)], PS[:, 7, :], ALU.mult), "out0")

                head(1, during_second)
                of_pe("lg1")
                r(nc.vector.tensor_tensor(half_tile(T_R, 1), rT2[:, halves(1)], PS[:, 7, :], ALU.mult), "out")

                def mo(ins, name):
                    ins.then_inc(MO_DVE.sem, MO_DVE.one(name))
                    dve.wait_ge(MO_DVE.sem, MO_DVE.at(name, p))

                o_all = mO.rearrange("p w (h n) -> p (w h) n", n=HD)
                sq_all = mOsq.rearrange("p (a n) -> p a n", n=HD)
                dve.wait_ge(M_DVE.sem, M_DVE.at("o7", 2 * p + 1))
                mo(nc.vector.tensor_tensor(sq_all, o_all, o_all, ALU.mult), "sq")
                mo(nc.vector.tensor_reduce(mSt, sq_all, AX_X, ALU.add), "sum")
                mo(nc.vector.tensor_scalar(mSt, mSt, 1.0 / HD, EPS, ALU.mult, ALU.add), "var")
                dve.wait_ge(MO_ACT.sem, MO_ACT.at("std", p))
                mo(nc.vector.reciprocal(mSt, mSt), "rstd")
                mo(nc.vector.tensor_tensor(o_all, o_all, mSt.rearrange("p (a n) -> p a n", n=1).broadcast_to(
                    [P, 16, HD]), ALU.mult), "norm")
                dve.wait_ge(MO_PE.sem, MO_PE.at("turn", p))
                mo(nc.vector.tensor_scalar(tile(T_K), two(4), par(V_ON), None, ALU.mult), "out")

            for kt in range(KT):
                dve.wait_ge(head_ready, KT + kt + 1)
                nc.vector.tensor_tensor(xn[:, kt, 1, :], mixed(kt), xn[:, kt, 0, :].bitcast(F32),
                                        ALU.subtract).then_inc(xn_ready, 1)

            dve.wait_ge(mm_act, 1)
            nc.vector.tensor_copy(cMs, cMt[:, 0, :]).then_inc(mm_dve, 1)
            for kt in range(1, KT):
                dve.wait_ge(mm_dve, kt)
                nc.vector.tensor_tensor(cMs, cMs, cMt[:, kt, :], ALU.add).then_inc(mm_dve, 1)

            def residual(u0, j0, n):
                nc.vector.memset(ssum[:, :], 0.0).then_inc(ssum_zero, 1)
                dve.wait_ge(ssum_zero, n)
                with dve.Fori(0, 4) as i:
                    for k in range(2):
                        tile = H[:, bass.ds(2 * i + k, 1), :].rearrange("p a t -> p (a t)")
                        dve.wait_ge(acc_ready, 2 * i + (u0 + k + 3))
                        nc.vector.tensor_tensor(tile, two(2 * k), tile, ALU.add).then_inc(h_added, 1)
                        dve.wait_ge(h_added, 2 * i + (j0 + k + 1))
                        nc.vector.sem_inc(acc_free, 1)
                        dve.wait_ge(sq_ready, 2 * i + (KT * n + k + 1))
                        dve.wait_ge(sq_added, 2 * i + (KT * n + k))
                        nc.vector.tensor_tensor(ssum[:, :], ssum[:, :], tmp[:, k, :], ALU.add).then_inc(sq_added, 1)

            for kt in range(KT):
                dve.wait_ge(x_loaded[kt], 32)
            residual(U_OUT, 0, 1)

            dve.wait_ge(mm_pe, 1)
            nc.vector.tensor_scalar(small[:, 32:34], PS[:, 4, 0:2], 1.0 / D, EPS, ALU.mult, ALU.add).then_inc(mm_dve, 1)
            dve.wait_ge(mm_act, 2)
            nc.vector.reciprocal(small[:, 36:38], small[:, 34:36]).then_inc(mm_dve, 1)
            dve.wait_ge(mm_pe, 2)
            for kt in range(KT):
                nc.vector.scalar_tensor_tensor(cMt[:, kt, :], cMem[:, kt, :], vec[:, V_MEM + kt:V_MEM + kt + 1],
                                               PS[:, 7, 64:64 + MEM], ALU.mult, ALU.mult).then_inc(mm_dve, 1)
            for kt in range(KT):
                dve.wait_ge(mm_act, 2 + kt + 1)
                nc.vector.tensor_tensor(memn[:, kt, 1, :], cMt[:, kt, :], memn[:, kt, 0, :].bitcast(F32),
                                        ALU.subtract).then_inc(mm_dve, 1)
            norm(1)
            scale_and_split(1, 2, V_CA)

            with dve.Fori(0, CA_HEADS) as h:
                def c(ins, name):
                    ins.then_inc(C_DVE.sem, C_DVE.one(name))

                def own(name):
                    dve.wait_ge(C_DVE.sem, C_DVE.at(name, h))

                def crow_max(q):
                    dve.wait_ge(C_PE.sem, C_PE.at(f"s{q}", h))
                    c(nc.vector.tensor_reduce(small[:, q:q + 1], PS[:, 4 + q % 2, 0:MEM], AX_X, ALU.max), f"m{q}")
                    own(f"m{q}")
                    c(nc.vector.tensor_scalar(small[:, 8 + q:9 + q], small[:, q:q + 1], -CA_SCALE, None, ALU.mult),
                      f"b{q}")

                def normalise(q):
                    dve.wait_ge(C_ACT.sem, C_ACT.at(f"e{q}", h))
                    c(nc.vector.reciprocal(small[:, 24 + q:25 + q], small[:, 16 + q:17 + q]), f"r{q}")
                    own(f"r{q}")
                    c(nc.vector.tensor_scalar(cP[q % 2], cP[q % 2], small[:, 24 + q:25 + q], None, ALU.mult), f"p{q}")

                def copy_cpt(q):
                    dve.wait_ge(C_PE.sem, C_PE.at(f"t{q}", h))
                    c(nc.vector.tensor_copy(cPT[q // 4][:, :, P * (q % 4):P * (q % 4) + P],
                                            PS[:, 6 + q % 2, 0:256].rearrange("p (k n) -> p k n", k=2)), f"t{q}")

                def crest(half):
                    for m in range(2):
                        dve.wait_ge(C_ACT.sem, C_ACT.at(f"h{half}{m}", h))
                        dst = xn[:, bass.ds(2 * h + m, 1), :, HALF * half:HALF * half + HALF].rearrange(
                            "p a b t -> p (a b) t")
                        c(nc.vector.tensor_tensor(dst[:, 1, :], PS[:, 2 * half + m, :], dst[:, 0, :].bitcast(F32),
                                                  ALU.subtract), f"l{half}{m}")

                crow_max(0)
                for q in range(1, NW):
                    crow_max(q)
                    normalise(q - 1)
                    copy_cpt(q - 1)
                    if q == 6:
                        crest(0)
                normalise(NW - 1)
                copy_cpt(NW - 1)
                crest(1)

            residual(U_O, 8, 2)
            norm(2)
            scale_and_split(2, 3, V_MLP)

            def hidden(c):
                with dve.Fori(0, 4) as i:
                    for k in range(2):
                        n = 8 * c + 2 * i
                        dve.wait_ge(relu_ready, n + (k + 1))
                        nc.vector.tensor_tensor(tmp[:, k, :], tmp[:, k, :], tmp[:, k, :], ALU.mult).then_inc(
                            hsq_ready, 1)
                        nc.vector.sem_inc(acc_free, 1)
                        dve.wait_ge(hhead_ready, n + (k + 1))
                        dve.wait_ge(hsq_ready, n + (k + 1))
                        dst = hid[:, bass.ds(2 * i + k, 1), :, :].rearrange("p a b t -> p (a b) t")
                        nc.vector.tensor_tensor(dst[:, 1, :], tmp[:, k, :], dst[:, 0, :].bitcast(F32),
                                                ALU.subtract).then_inc(hid_ready, 1)

            with dve.Fori(0, 3) as c:
                hidden(c)
                with dve.Fori(0, 4) as i:
                    for k in range(2):
                        tile = H[:, bass.ds(2 * i + k, 1), :].rearrange("p a t -> p (a t)")
                        dve.wait_ge(acc_ready, 16 * c + 2 * i + (U_MLP + 8 + k + 3))
                        nc.vector.tensor_tensor(tile, two(2 * k), tile, ALU.add).then_inc(h_added, 1)
                        dve.wait_ge(h_added, 8 * c + 2 * i + (16 + k + 1))
                        nc.vector.sem_inc(acc_free, 1)
            hidden(3)
            residual(UNITS - 8, 40, 3)
            norm(3)
            dve.wait_ge(nb_ready, 4)
            for kt in range(KT):
                nc.vector.scalar_tensor_tensor(proj[:, kt, :], H[:, kt, :], vec[:, V_FIN + kt:V_FIN + kt + 1], two(5),
                                               ALU.mult, ALU.mult).then_inc(out_scaled, 1)

        for st in STEPS:
            assert st.next > 0 and st.next % st.n == 0, st.names


def tiles(w, rows):
    k, n = w.shape
    return w.reshape(k // P, P, n // P, P).transpose(2, 1, 0, 3).reshape(n // P, P, k)


def layout(x, mem, positions, mix_norm, w_in_first, w_in_rest, shift_mu_first, shift_mu_rest,
           mla_q_norm, mla_w_uq, mla_kv_norm, mla_w_ukv, mla_out_norm,
           rwkv_w0, rwkv_w2, rwkv_a0, rwkv_a2, rwkv_g2, rwkv_v0, rwkv_v2,
           rwkv_k_k, rwkv_k_a, rwkv_r_k, rwkv_ln_w, rwkv_ln_b, w_out,
           ca_norm, mem_norm, ca_wq, ca_wkv, ca_wo,
           mlp_norm, mlp_w_up, mlp_w_down, final_norm):
    f32 = np.float32
    rw = 512
    mla = QR + KVR + ROPE
    at = mla + 3 * rw
    cols = np.concatenate([np.arange(0, QR), np.arange(at, at + 64), np.arange(QR, QR + KVR),
                           np.arange(at + 64, at + 160), np.arange(QR + KVR, mla), np.arange(mla, at)])
    w_in = np.asarray(w_in_first)[:, cols]
    mu = np.concatenate([np.zeros(mla, f32), np.asarray(shift_mu_first)])[cols]
    wkv = np.asarray(ca_wkv)[0]
    up, down = np.asarray(mlp_w_up)[0], np.asarray(mlp_w_down)[0]
    units = [tiles(w_in, D), tiles(np.asarray(w_out)[0], D), tiles(wkv[:, :D], D), tiles(wkv[:, D:], D),
             tiles(np.asarray(ca_wq)[0], D), tiles(np.asarray(ca_wo)[0], D)]
    for c in range(4):
        units += [tiles(up[:, D * c:D * c + D], D), tiles(down[D * c:D * c + D], D)]
    vecs = np.zeros((P, NV), f32)

    def put(col, v):
        v = np.asarray(v).reshape(-1, P).T
        vecs[:, col:col + v.shape[1]] = v

    for col, v in ((V_MIX, mix_norm), (V_CA, ca_norm), (V_MLP, mlp_norm), (V_FIN, final_norm), (V_MEM, mem_norm),
                   (V_MU, mu), (V_KVN, mla_kv_norm), (V_ON, mla_out_norm), (V_W0, rwkv_w0), (V_A0, rwkv_a0),
                   (V_KK, rwkv_k_k), (V_KA, rwkv_k_a), (V_RK, rwkv_r_k), (V_LW, rwkv_ln_w), (V_LB, rwkv_ln_b)):
        put(col, v)
    qn = np.asarray(mla_q_norm)[0]
    vecs[:, V_QN] = qn[:P]
    vecs[:QR - P, V_QN + 1] = qn[P:]
    uq = np.asarray(mla_w_uq)[0].reshape(QR, MLA_HEADS, HD + ROPE)
    swap = np.concatenate([np.arange(HD + ROPE), HD + np.arange(ROPE // 2, ROPE), HD + np.arange(ROPE // 2)])
    uq = uq[:, :, swap].transpose(1, 0, 2)
    ukv = np.asarray(mla_w_ukv)[0].reshape(KVR, MLA_HEADS, 2 * HD)
    headw = np.zeros((MLA_HEADS, P, 320), f32)
    headw[:, :, 0:P] = uq[:, :P]
    headw[:, :QR - P, P:2 * P] = uq[:, P:]
    headw[:, :, 2 * P:] = ukv[:, :, :HD].transpose(1, 0, 2)
    headw = headw.reshape(PAIRS, 2, P, 320).transpose(0, 2, 1, 3).reshape(PAIRS, P, 640)
    wv = ukv[:, :, HD:].reshape(KVR, MLA_HEADS * HD)
    lora = np.zeros((PAIRS, P, 384), f32)
    lora[:, 64:96, 0:P] = np.asarray(rwkv_w2)[0].reshape(32, PAIRS, P).transpose(1, 0, 2)
    lora[:, 96:128, P:2 * P] = np.asarray(rwkv_a2)[0].reshape(32, PAIRS, P).transpose(1, 0, 2)
    lora[:, 0:96, 2 * P:] = np.asarray(rwkv_g2)[0].reshape(96, PAIRS, P).transpose(1, 0, 2)
    return {
        "x": np.asarray(x)[0].T.reshape(KT, P, S), "mem": np.asarray(mem)[0].T.reshape(KT, P, MEM),
        "positions": np.asarray(positions), "weights": np.concatenate(units), "vectors": vecs,
        "constants": constants(), "head_weights": headw, "value_weights": wv, "lora": lora,
    }


def kernel(**inputs):
    import concourse.bacc as bacc
    from concourse.bass_utils import run_bass_kernel_spmd

    nc = bacc.Bacc("TRN2", target_bir_lowering=False, num_devices=1)
    arrays, args = {}, []
    for name, a in layout(**inputs).items():
        a = np.ascontiguousarray(a)
        arrays[f"in_{name}_dram"] = a
        args.append(nc.dram_tensor(f"in_{name}_dram", a.shape, mybir.dt.from_np(a.dtype), kind="ExternalInput").ap())
    args.append(nc.dram_tensor("out_0_dram", (KT, P, S), F32, kind="ExternalOutput").ap())
    build(nc, *args)
    r = run_bass_kernel_spmd(nc, [arrays], core_ids=[0])
    return np.ascontiguousarray(r.results[0]["out_0_dram"].reshape(1, D, S).transpose(0, 2, 1))
```

```python
from contextlib import ExitStack
import math

import numpy as np

import concourse.bass as bass
from concourse import mybir

F32 = mybir.dt.float32
F32R = mybir.dt.float32r
I32 = mybir.dt.int32
ACT = mybir.ActivationFunctionType
ALU = mybir.AluOpType
AX_X = mybir.AxisListType.X

P = 128
D = 1024
S = 1024
KT = D // P
NW = S // P
HALF = 512
MEM = 256
CH = 64
NC = S // CH
HD = 64
BLK = 16
LEVELS = 2
SUBST = (range(0, 8), range(8, BLK - 1))
PAD = BLK * (P + 1)
MLA_HEADS = 8
PAIRS = 4
CA_HEADS = 4
QR, KVR, ROPE = 192, 128, 32
EPS = 1e-6
GN_EPS = 64e-5
EXPM05 = math.exp(-0.5)
MLA_SCALE = (HD + ROPE) ** -0.5
CA_SCALE = 256 ** -0.5
MAGIC = 12582912.0

T_CQ, T_CQWA, T_CKV, T_GK, T_R, T_K, T_V = 0, 1, 2, 3, 4, 8, 12

V_MIX, V_CA, V_MLP, V_FIN, V_MEM, V_MU = 0, 8, 16, 24, 32, 40
V_QN, V_KVN, V_ON = 56, 58, 59
V_W0, V_A0, V_KK, V_KA, V_RK, V_LW, V_LB = 63, 67, 71, 75, 79, 83, 87
NV = 91

C_ID, C_MS, C_ML, C_BQ, C_SEL, C_E1, C_E2, C_BO, C_BM, C_RA, C_RB = (
    0, 128, 512, 640, 896, 1152, 1280, 1408, 1536, 1664, 1792)
C_HO, C_ONE, C_INV, C_SGN, C_NH, C_PI2, C_EM, C_EP = 1920, 1922, 1923, 1924, 1925, 1941, 1942, 1943
NCON = 1944

U_IN, U_OUT, U_MK, U_MV, U_Q, U_O, U_MLP = 0, 16, 24, 32, 40, 48, 56
UNITS = U_MLP + 64
MEM_UNITS = U_Q - U_MK


def constants():
    c = np.zeros((P, NCON), np.float32)
    i = np.arange(P)
    part, free = i[:, None], i[None, :]
    same = part // CH == free // CH
    c[:, C_ID:C_ID + P] = np.eye(P)
    for n in range(3):
        c[:, C_MS + P * n:C_MS + P * n + P] = same & ((part < free) if n == 1 else (part <= free))
    c[:, C_ML:C_ML + P] = same & (free < part)
    for n in range(LEVELS):
        m = BLK << n
        c[:, C_BQ + P * n:C_BQ + P * n + P] = (
            (part // (2 * m) == free // (2 * m)) & (part % (2 * m) < m) & (free % (2 * m) >= m))
    for h in range(2):
        c[:, C_SEL + P * h:C_SEL + P * h + P] = (free < HD) & (part == free + HD * h)
    r = np.arange(ROPE)
    half = ROPE // 2
    for base in (64, 96):
        c[96 + r, C_E1 + base + r] = 1.0
        c[96 + half + r[:half], C_E2 + base + r[:half]] = -1.0
        c[96 + r[:half], C_E2 + base + half + r[:half]] = 1.0
    c[:, C_BO:C_BO + P] = same
    c[:, C_BM:C_BM + P] = same / HD
    c[:, C_HO:C_HO + 2] = part // HD == free[:, :2]
    c[:, C_ONE] = 1.0
    inv = (10000.0 ** (-np.arange(0, ROPE, 2) / ROPE)).astype(np.float32)
    c[:, C_INV] = inv[i % half]
    c[:, C_SGN] = np.where(i % ROPE < half, -1.0, 1.0)
    c[0, C_RA:C_RA + P] = i < CH
    c[0, C_RB:C_RB + P] = np.where(i >= CH, -1e30, 0.0)
    c[:, C_NH:C_NH + 16] = -0.5
    c[:, C_PI2] = math.pi / 2
    c[:, C_EM] = -0.5 * EXPM05
    c[:, C_EP] = 0.5 * EXPM05
    return c


class Steps:

    def __init__(self, semaphore, names):
        self.sem, self.names, self.n = semaphore, names, len(names)
        self.pos = {name: i + 1 for i, name in enumerate(names)}
        assert len(self.pos) == self.n
        self.next = 0

    def at(self, name, turn=0):
        return (turn + 1) * self.n + self.pos[name]

    def one(self, name):
        assert self.names[self.next % self.n] == name, (self.names[self.next % self.n], name)
        self.next += 1
        return 1


def build(nc, x_t, mem_t, pos, wall, vecs, con_d, headw, wv_d, lora_d, out_t):
    with ExitStack() as ctx:
        def sb(name, shape, dt=F32):
            return ctx.enter_context(nc.sbuf_tensor(name, shape, dt))

        def overlay(*specs):
            made, size = [], 0
            for name, shape, dt in specs:
                with nc.sbuf_tensor(name, shape, dt) as t:
                    made.append(t)
                size = max(size, int(np.prod(shape[1:])))
            sb(specs[0][0] + "_place", [P, size])
            return made

        def sem(name):
            return ctx.enter_context(nc.semaphore(name))

        xn, sa = overlay(("xn", [P, KT, 2, S], F32R), ("sa", [P, 16384], F32))
        proj, hid, sbx, memr = overlay(("proj", [P, 16, S], F32), ("hid", [P, KT, 2, S], F32R),
                                       ("sbx", [P, 16384], F32), ("memr", [P, 16384], F32R))
        H = sb("H", [P, KT, S])
        wraw, sc_w = overlay(("wraw", [P, 2, KT * P], F32), ("sc_w", [P, 2048], F32))
        wsp, sc_s = overlay(("wsp", [P, 2, KT, 2, P], F32R), ("sc_s", [P, 4096], F32))
        con = sb("con", [P, NCON])
        vec = sb("vec", [P, NV])
        omu = sb("omu", [P, 16])
        vech = sb("vech", [P, 12])
        small = sb("small", [P, 128])
        tmp = sb("tmp", [P, 2, S])
        ssum = sb("ssum", [P, S])

        mOsq = sb("o_squares", [P, HD])[:, :]

        ident = con[:, C_ID:C_ID + P]
        PS = ctx.enter_context(nc.psum_tensor("PS", [P, 8, HALF], F32))

        def two(b):
            return PS[:, b:b + 2, :].rearrange("p a n -> p (a n)")

        def win(w):
            return slice(P * w, P * w + P)

        hs_ = H[:, :, :].rearrange("p k t -> p (k t)")
        mV = sa[:, 12288:16384].rearrange("p (w n) -> p w n", w=NW)
        mO = hs_[:, 0:1024].rearrange("p (w n) -> p w n", w=NW)
        mQ = hs_[:, 1024:2048]
        mK = hs_[:, 2048:3072]
        mP = [hs_[:, 3072:4096], hs_[:, 4096:5120]]
        mPT = [hs_[:, 5120:6144], hs_[:, 6144:7168]]
        mCS = hs_[:, 7168:8192]
        mCos = sa[:, 0:1024]
        mSin = sa[:, 1024:2048]
        mT = [tmp[:, 0, :], tmp[:, 1, :]]
        mSt = small[:, 96:112]
        headw_sb = sc_s[:, 2944:3584]
        wv_sb = sc_s[:, 3584:4096]
        posi = sc_w[:, 0:1024].bitcast(I32)

        rAR = sa[:, 0:2048].rearrange("p (w a t) -> p w a t", w=NW, a=2)
        rB = sa[:, 2048:3072]
        rK = sa[:, 3072:4096]
        rBh = sa[:, 4096:5120]
        rKh = sa[:, 5120:6144]
        rW = sa[:, 6144:7168]
        rWi = rBV = sa[:, 7168:8192]
        rT1, rT2, rT3 = (sa[:, 8192 + 1024 * n:9216 + 1024 * n] for n in range(3))
        rY = sa[:, 11264:12288]
        rSt = small[:, 64:96]
        rSC = [t[:, 0:768].rearrange("p (h k n) -> p h k n", h=2, k=3) for t in (rT1, rT2)]
        rQ = [sc_w[:, 256 * n:256 * n + 256].rearrange("p (h n) -> p h n", h=2) for n in range(2)]
        rAL = [place.rearrange("p (w n) -> p w n", w=4) for place in
               [sc_w[:, 512 + 512 * n:1024 + 512 * n] for n in range(3)] + [hs_[:, 1024:1536]]]
        rXX = [hs_[:, 3072 + 512 * w:3584 + 512 * w].rearrange("p (a h n) -> p a h n", a=2, h=2)
               for w in range(NW)]
        bA = sc_s[:, 768:1024].rearrange("p (i n) -> p i n", n=BLK)
        bT = sc_s[:, 1024:1280].rearrange("p (i n) -> p i n", n=BLK)
        bX, bXT = (sc_s[:, 2048 + 256 * k:2304 + 256 * k].rearrange("p (i n) -> p i n", n=BLK) for k in range(2))
        zeros = sa[:, 2048:2048 + PAD]

        matrices = [nc.dram_tensor(name, (P, PAD), F32, kind="Internal").ap() for name in ("a_dram", "x_dram", "xt_dram")]

        def window_in_dram(k, w):
            return matrices[k].rearrange("(w h b) n -> w h (b n)", h=2, b=8)[w, :, 0:P * P].rearrange(
                "h (p n) -> p h n", n=P)

        def head_in_dram(k, n):
            return matrices[k].rearrange("(w h b) n -> w h (b n)", h=2, b=8)[
                4 * (n // 2):4 * (n // 2) + 4, n % 2, 0:P * P].rearrange("w (p n) -> p w n", n=P)

        def blocks_in_dram(k):
            return matrices[k][:, 0:BLK * P].rearrange("p (i n) -> p i n", n=P)[:, :, 0:BLK]

        def wbuf(n, k):
            return sc_s[:, 1280 * n + 256 * k:1280 * n + 256 * k + 256]

        rAG, rBK, rVZ, rPG, rRY = ([wbuf(n, k).rearrange("p (h n) -> p h n", h=2) for n in range(2)]
                                   for k in range(5))
        lora = sc_s[:, 2560:2944]
        rDg, rMT = ([ssum[:, 512 * k + 256 * n:512 * k + 256 * n + 256].rearrange("p (c h n) -> p c h n", c=2, h=2)
                     for n in range(2)] for k in range(2))
        rST = tmp[:, :, :].rearrange("p a (c h n) -> p (a c) h n", h=2, n=HD)
        rWT = small[0:HD, 32:64].rearrange("p (c h) -> p c h", h=2)

        def mixed(t):
            return proj[:, T_K + t if t < 4 else T_R + t - 4, :]

        cQ = sbx[:, 0:8192].rearrange("p (k t) -> p k t", k=KT)
        cMem = sbx[:, 0:2048].rearrange("p (k t) -> p k t", k=KT)
        cMt = sbx[:, 2048:4096].rearrange("p (k t) -> p k t", k=KT)
        cMs = sbx[:, 16128:16384]
        cK = sbx[:, 8192:10240].rearrange("p (k t) -> p k t", k=KT)
        cV = sbx[:, 10240:12288].rearrange("p (k t) -> p k t", k=2)
        memn = memr[:, 12288:16384].rearrange("p (k a t) -> p k a t", k=KT, a=2)
        cVT = [sbx[:, 4096 + MEM * n:4096 + MEM * n + MEM] for n in range(2)]
        cVh = [sbx[:, 12288 + 512 * n:12800 + 512 * n].rearrange("p (k n) -> p k n", k=2) for n in range(2)]
        cP = [sbx[:, 13312 + 512 * n:13824 + 512 * n].rearrange("p (w n) -> p w n", w=2) for n in range(2)]
        cPT = [sbx[:, 14336 + 1024 * n:15360 + 1024 * n].rearrange("p (k q) -> p k q", k=2) for n in range(2)]
        cQh = [tmp[:, :, :], sa[:, 14336:16384].rearrange("p (k t) -> p k t", k=2)]
        cMax, cBias, cSum, cInv = (small[:, 16 * n:16 * n + 16] for n in range(4))

        con_loaded, vec_loaded = sem("con_loaded"), sem("vec_loaded")
        x_loaded = [sem(f"x_loaded{k}") for k in range(KT)]
        raw_loaded = [sem("raw_loaded0"), sem("raw_loaded1")]
        pos_loaded, wv_loaded, headw_loaded = sem("pos_loaded"), sem("wv_loaded"), sem("headw_loaded")
        lora_loaded, mem_loaded = sem("lora_loaded"), sem("mem_loaded")
        zeros_made, zeros_stored = sem("zeros_made"), sem("zeros_stored")
        a_stored, a_blocks_loaded, x_blocks_stored = sem("a_stored"), sem("a_blocks_loaded"), sem("x_blocks_stored")
        xx_loaded = [sem(f"xx_loaded{g}") for g in range(NW // 2)]
        sp_turn = sem("sp_turn")
        stored = sem("stored")
        vec_made = sem("vec_made")
        w_split = sem("w_split")
        w_head = sem("w_head")
        mem_head, mem_split = sem("mem_head"), sem("mem_split")
        acc_ready = sem("acc_ready")
        acc_free = sem("acc_free")
        proj_part = sem("proj_part")
        sq_ready = sem("sq_ready")
        sq_added = sem("sq_added")
        nsum_ready, var_ready, std_ready, rstd_ready, nb_ready = (
            sem("nsum_ready"), sem("var_ready"), sem("std_ready"), sem("rstd_ready"), sem("nb_ready"))
        scaled = sem("scaled")
        head_ready = sem("head_ready")
        xn_ready = sem("xn_ready")
        h_added = sem("h_added")
        ssum_zero = sem("ssum_zero")
        pool_turn = sem("pool_turn")
        act_turn = sem("act_turn")
        relu_ready, hsq_ready, hhead_ready, hid_ready = (
            sem("relu_ready"), sem("hsq_ready"), sem("hhead_ready"), sem("hid_ready"))
        ca_hi, ca_lo = sem("ca_hi"), sem("ca_lo")
        out_scaled = sem("out_scaled")

        MP_ACT = Steps(sem("mla_pre_act"), ["sq1", "sq2", "sq3", "sin", "cos", "std"] + [f"v{w}" for w in range(NW)])
        MP_DVE = Steps(sem("mla_pre_dve"), ["posf", "ang", "turns", "m1", "r1", "m2", "r2", "clamp", "abs",
                                            "var1", "var", "rstd", "one", "csc", "css", "kr1", "kr2", "kr",
                                            "cq0", "cq1", "ckv"])
        MP_PE = Steps(sem("mla_pre_pe"), ["e12", "sums", "bq", "bkv"] + [f"v{w}" for w in range(NW)])
        qn = range(NW)
        M_PE = Steps(sem("mla_pe"), ["q", "k", "s0", "s1", "t0"]
                     + [x for q in range(2, NW) for x in (f"s{q}", f"t{q - 1}", f"o{q - 2}")]
                     + ["t7", "o6", "o7"])
        M_ACT = Steps(sem("mla_act"), ["k", "e0"] + [x for q in range(1, NW) for x in (f"e{q}", f"t{q - 1}")] + ["t7"])
        M_DVE = Steps(sem("mla_dve"), ["q", "m0", "b0", "m1", "b1"]
                      + [x for q in range(2, NW) for x in (f"m{q}", f"b{q}", f"r{q - 2}", f"o{q - 2}", f"sq{q - 2}",
                                                           f"ss{q - 2}")]
                      + [f"{x}{q}" for q in (6, 7) for x in ("r", "o", "sq", "ss")])
        MO_PE = Steps(sem("mla_out_pe"), ["turn"])
        MO_ACT = Steps(sem("mla_out_act"), ["std"])
        MO_DVE = Steps(sem("mla_out_dve"), ["var", "rstd", "norm", "out"])
        rp_act, rp_dve = sem("rwkv_set_act"), sem("rwkv_set_dve")

        pe_names = ["lw0", "lw1", "la0", "la1", "kks", "kkb0", "kkb1", "al0", "al1", "al2", "al3"]
        act_names = ["tw0", "tw1", "ta0", "ta1", "kksq", "dec", "dnv", "afirst", "wt0", "wt1", "vc"]
        dve_names = ["kk", "zk", "kkm", "zb", "nw", "dinv", "f1", "f2", "z1", "z2", "W", "Wi", "nkk0", "nkk1",
                     "at", "na", "b", "bt", "am", "al0", "k2", "al1", "kt", "al2", "rk", "x0", "x1", "al3"]
        pool_names = ["pow", "rt", "bh", "kh"]
        for g in range(NW // 2):
            ab = (2 * g, 2 * g + 1)
            pool_names += [f"dg_{w}" for w in ab]
            if g == 0:
                for w in ab:
                    pe_names += [f"sc{w}"]
                    dve_names += [f"sc0_{w}", f"sc1_{w}"] + [x for j in SUBST[w] for x in (f"xm{j}", f"xa{j}")]
                pe_names += [f"tok{w}" for w in ab] + [f"akv{w}" for w in ab] + ["rk0", "rk1"]
                dve_names += ["xt", "bv0", "bv1"]
                act_names += [f"{x}{w}" for w in ab for x in ("ag", "bk", "vz")] + [f"akv{w}" for w in ab]
            for lv in range(LEVELS):
                pe_names += [f"q{lv}_{w}" for w in ab] + [f"z{lv}_{w}" for w in ab]
                dve_names += [f"q{lv}_{w}" for w in ab] + [f"z{lv}_{w}" for w in ab]
            for st in ("pg", "ry"):
                pe_names += [f"{st}{w}" for w in ab]
                act_names += [f"{st}{w}" for w in ab]
            pe_names += [f"mn{w}" for w in ab]
            for w in ab:
                dve_names += [f"mt0_{w}", f"mt1_{w}"]
            for k in range(4):
                c, w = 4 * g + k, 2 * g + k // 2
                if c < NC - 1:
                    pe_names += [f"st{c}"]
                    dve_names += [f"st{c}"]
                pe_names += [f"y{c}"]
                if k % 2:
                    act_names += [f"y{w}"]
                if g < NW // 2 - 1:
                    n = 2 * g + 2 + k % 2
                    if k < 2:
                        pe_names += [f"sc{n}"]
                        dve_names += [f"sc0_{n}", f"sc1_{n}"]
                    else:
                        pe_names += [f"tok{n}"]
                        if k == 3:
                            act_names += [f"{x}{v}" for v in (n - 1, n) for x in ("ag", "bk", "vz")]
            if g < NW // 2 - 1:
                pe_names += [f"akv{n - 1}", f"akv{n}"]
                act_names += [f"akv{n - 1}", f"akv{n}"]
        pe_names += ["mean0", "mean1", "vs", "vb0", "vb1", "lg0", "lg1"]
        act_names += ["ysq"]
        dve_names += ["yc0", "yc1", "var", "yn0", "yn1", "yl", "yb", "out0", "out"]
        pool_names += ["gpow"]
        R_PE, R_ACT, R_DVE, R_POOL = (Steps(sem("rwkv_pe"), pe_names), Steps(sem("rwkv_act"), act_names),
                                      Steps(sem("rwkv_dve"), dve_names), Steps(sem("rwkv_pool"), pool_names))

        vt_copied, vt_turned = sem("vt_copied"), sem("vt_turned")
        mm_act, mm_dve, mm_pe = sem("mem_act"), sem("mem_dve"), sem("mem_pe")
        ca_stage = sem("ca_stage")
        C_PE = Steps(sem("ca_pe"), ["s0"] + [x for g in range(8) for x in
                                             ([f"s{g + 1}"] if g < 7 else []) + [f"t{g}"]
                                             + ([f"o{g // 2 - 1}"] if g in (2, 4, 6) else [])] + ["o3"])
        C_ACT = Steps(sem("ca_act"), [x for g in range(8) for x in
                                      [f"e{g}"] + ([f"h{g // 2 - 1}"] if g in (3, 5, 7) else [])] + ["h3"])
        C_DVE = Steps(sem("ca_dve"), ["m0", "b0"] + [x for g in range(8) for x in
                                                     [f"r{g}", f"p{g}"] + ([f"m{g + 1}", f"b{g + 1}"] if g < 7 else [])
                                                     + ([f"c{g - 1}"] if g else [])
                                                     + ([f"l{g // 2 - 2}"] if g in (4, 6) else [])]
                      + ["c7", "l2", "l3"])
        STEPS = (MP_ACT, MP_DVE, MP_PE, MO_PE, MO_ACT, MO_DVE, M_PE, M_ACT, M_DVE, R_PE, R_ACT, R_DVE, R_POOL, C_PE, C_ACT, C_DVE)

        def by_pool(u):
            return u - MEM_UNITS if u >= U_Q else u

        block = ctx.enter_context(nc.Block())

        @block.sync
        def _(sp):
            def weights(u0, n):
                with sp.Fori(0, n // 2) as i:
                    for k in range(2):
                        if U_MK + 2 <= u0 <= U_Q + 1:
                            sp.wait_ge(mem_split, 2 * i + (u0 - U_MK - 1 + k))
                        else:
                            sp.wait_ge(w_split, 2 * i + (by_pool(u0) + k + 1))
                        sp.dma_start(wraw[:, k, :], wall[bass.ds(2 * i + (u0 + k), 1)].rearrange(
                            "a p n -> (a p) n")).then_inc(raw_loaded[k], 16)

            for kt in range(KT):
                sp.dma_start(H[:, kt, :], x_t[kt]).then_inc(x_loaded[kt], 16)
            sp.dma_start(vec[:, :], vecs).then_inc(vec_loaded, 16)
            sp.dma_start(con[:, :], con_d).then_inc(con_loaded, 16)
            weights(U_IN, 16)

            sp.wait_ge(acc_ready, U_OUT + 2)
            sp.dma_start(posi, pos.broadcast_to([P, S])).then_inc(pos_loaded, 16)
            sp.dma_start(wv_sb, wv_d).then_inc(wv_loaded, 16)
            sp.wait_ge(zeros_made, 1)
            for k in (1, 2):
                sp.dma_start(matrices[k], zeros).then_inc(zeros_stored, 16)
            with sp.Fori(0, PAIRS) as p:
                sp.wait_ge(R_PE.sem, R_PE.at("lg1", p - 1))
                sp.dma_start(lora, lora_d[bass.ds(p, 1)].rearrange("a p n -> (a p) n")).then_inc(lora_loaded, 16)
                sp.wait_ge(M_PE.sem, M_PE.at("k", 2 * p - 1))
                sp.dma_start(headw_sb, headw[bass.ds(p, 1)].rearrange("a p n -> (a p) n")).then_inc(headw_loaded, 16)
                for n in range(4):
                    sp.wait_ge(R_DVE.sem, R_DVE.at(f"al{n}", p))
                    sp.dma_start(head_in_dram(0, n), rAL[n]).then_inc(a_stored, 16)
                sp.wait_ge(a_stored, 64 * (p + 1))
                sp.dma_start(bA, blocks_in_dram(0)).then_inc(a_blocks_loaded, 16)
                sp.wait_ge(R_DVE.sem, R_DVE.at("xt", p))
                sp.dma_start(blocks_in_dram(1), bX).then_inc(x_blocks_stored, 16)
                sp.dma_start(blocks_in_dram(2), bXT).then_inc(x_blocks_stored, 16)
                sp.wait_ge(M_PE.sem, M_PE.at("o7", 2 * p))
                nc.sync.sem_inc(sp_turn, 1)
                sp.wait_ge(x_blocks_stored, 32 * (p + 1))
                for w in range(NW):
                    for k in range(2):
                        sp.dma_start(rXX[w][:, k], window_in_dram(1 + k, w)).then_inc(xx_loaded[w // 2], 16)

            sp.wait_ge(R_DVE.sem, R_DVE.at("out", PAIRS - 1))
            sp.wait_ge(MO_DVE.sem, MO_DVE.at("out", PAIRS - 1))
            sp.wait_ge(M_PE.sem, M_PE.at("o7", MLA_HEADS - 1))
            sp.dma_start(cMem, mem_t.rearrange("k p t -> p k t")).then_inc(mem_loaded, 16)
            weights(U_OUT, 2)
            for kt in range(KT):
                sp.wait_ge(xn_ready, KT + kt + 1)
                sp.dma_start(H[:, kt, :], x_t[kt]).then_inc(x_loaded[kt], 16)
            weights(U_OUT + 2, U_MK - U_OUT)
            weights(U_MK + 2, MEM_UNITS)
            weights(U_Q + 2, UNITS - U_Q - 2)

            for kt in range(KT):
                sp.wait_ge(out_scaled, kt + 1)
                sp.dma_start(out_t[kt], proj[:, kt, :]).then_inc(stored, 16)
            sp.wait_ge(stored, 16 * KT)

        @block.gpsimd
        def _(pool):
            def split_weights(u0, n):
                with pool.Fori(0, n // 2) as i:
                    for k in range(2):
                        raw = wraw[:, k, :].rearrange("p (k n) -> p k n", k=KT)
                        pool.wait_ge(raw_loaded[k], 16 * (i + (u0 // 2 + 1)))
                        pool.wait_ge(acc_ready, 2 * i + (u0 + k + 1))
                        nc.gpsimd.sem_inc(pool_turn, 1)
                        nc.gpsimd.tensor_copy(wsp[:, k, :, 0, :], raw).then_inc(w_head, 1)
                        pool.wait_ge(w_head, 2 * i + (by_pool(u0) + k + 1))
                        nc.gpsimd.tensor_tensor(wsp[:, k, :, 1, :], raw, wsp[:, k, :, 0, :].bitcast(F32),
                                                ALU.subtract).then_inc(w_split, 1)

            nc.gpsimd.sem_inc(w_split, 2)
            nc.gpsimd.sem_inc(R_POOL.sem, R_POOL.n)
            split_weights(U_IN, 16)

            with pool.Fori(0, PAIRS) as p:
                pool.wait_ge(R_DVE.sem, R_DVE.at("kkm", p))
                nc.gpsimd.tensor_tensor(rSt[:, 16:32], rSt[:, 0:16], con[:, C_NH:C_NH + 16],
                                        ALU.pow).then_inc(R_POOL.sem, R_POOL.one("pow"))
                wt = rW.rearrange("p (c t) -> p c t", c=NC)[:, :, CH - 1:CH].broadcast_to([P, NC, CH])
                pool.wait_ge(R_DVE.sem, R_DVE.at("Wi", p))
                nc.gpsimd.tensor_tensor(rAR[:, :, 1, :], proj[:, bass.ds(p + T_R, 1), :].rearrange(
                    "p a (w t) -> p (a w) t", w=NW), rW.rearrange("p (w t) -> p w t", w=NW),
                    ALU.mult).then_inc(R_POOL.sem, R_POOL.one("rt"))
                pool.wait_ge(R_DVE.sem, R_DVE.at("bt", p))
                nc.gpsimd.tensor_tensor(rBh.rearrange("p (c t) -> p c t", c=NC),
                                        rB.rearrange("p (c t) -> p c t", c=NC), wt,
                                        ALU.mult).then_inc(R_POOL.sem, R_POOL.one("bh"))
                pool.wait_ge(R_DVE.sem, R_DVE.at("kt", p))
                nc.gpsimd.tensor_tensor(rKh.rearrange("p (c t) -> p c t", c=NC),
                                        rK.rearrange("p (c t) -> p c t", c=NC), wt,
                                        ALU.mult).then_inc(R_POOL.sem, R_POOL.one("kh"))
                for w in range(NW):
                    s = w % 2
                    if w == 0:
                        pool.wait_ge(R_ACT.sem, R_ACT.at("wt1", p))
                    if w >= 2:
                        pool.wait_ge(R_DVE.sem, R_DVE.at(f"mt1_{w - 2}", p))
                    nc.gpsimd.tensor_tensor(
                        rDg[s][0:HD],
                        ident[0:HD, 0:HD].rearrange("p (a b n) -> p a b n", a=1, b=1).broadcast_to([HD, 2, 2, HD]),
                        rWT[:, 2 * w:2 * w + 2].rearrange("p c (h n) -> p c h n", n=1).broadcast_to([HD, 2, 2, HD]),
                        ALU.mult).then_inc(R_POOL.sem, R_POOL.one(f"dg_{w}"))
                pool.wait_ge(R_DVE.sem, R_DVE.at("var", p))
                nc.gpsimd.tensor_tensor(rSt[:, 16:32], rSt[:, 0:16], con[:, C_NH:C_NH + 16],
                                        ALU.pow).then_inc(R_POOL.sem, R_POOL.one("gpow"))

            pool.wait_ge(R_PE.sem, R_PE.at("lg1", PAIRS - 1))
            pool.wait_ge(M_PE.sem, M_PE.at("k", MLA_HEADS - 1))
            split_weights(U_OUT, U_MK - U_OUT)
            split_weights(U_Q, U_O - U_Q)

            pool.wait_ge(acc_free, U_Q + 4)
            pool.wait_ge(xn_ready, 3 * KT)
            with pool.Fori(0, CA_HEADS // 2) as i:
                for a in range(2):
                    if a == 1:
                        pool.wait_ge(acc_free, U_O + 2)
                    pool.wait_ge(C_PE.sem, C_PE.at(f"o{2 * a + 1}", i - 1))
                    nc.gpsimd.sem_inc(pool_turn, 1)
                    for k in range(2):
                        nc.gpsimd.tensor_copy(cQh[a][:, k, :], cQ[:, bass.ds(4 * i + (2 * a + k), 1), :].rearrange(
                            "p a t -> p (a t)")).then_inc(ca_stage, 1)
                    for k in range(2):
                        nc.gpsimd.tensor_copy(cVh[a][:, k, :], cV[:, k, bass.ds(512 * i + 256 * a, 256)]).then_inc(
                            ca_stage, 1)
            split_weights(U_O, UNITS - U_O)

        @block.tensor
        def _(pe):
            nc.tensor.sem_inc(acc_ready, 2)
            for st in (M_PE, MO_PE, R_PE, C_PE):
                nc.tensor.sem_inc(st.sem, st.n)

            def gemm(u0, n, src, ready):
                with pe.Fori(0, n // 2) as i:
                    for k in range(2):
                        unit(2 * i + (u0 + k), k, src, ready, u0 >= U_Q)

            def unit(u, k, src, ready, after_memory=True):
                pe.wait_ge(w_split, u + (3 - MEM_UNITS if after_memory else 3))
                pe.wait_ge(acc_free, u + 1)
                for kt in range(KT):
                    ready(kt)
                    for a, b in ((0, 0), (0, 1), (1, 0)):
                        for half in range(2):
                            last = nc.tensor.matmul(
                                PS[:, 2 * k + half, :], wsp[:, k, kt, a, :],
                                src[:, kt, b, HALF * half:HALF * half + HALF],
                                start=(kt == 0 and (a, b) == (0, 0)), stop=(kt == KT - 1 and a == 1))
                last.then_inc(acc_ready, 1)

            def norm(n):
                pe.wait_ge(sq_added, KT * (n + 1))
                for w in range(NW):
                    last = nc.tensor.matmul(PS[:, 4, w:w + 1], ssum[:, win(w)], con[:, C_ONE:C_ONE + 1],
                                            start=True, stop=True)
                last.then_inc(nsum_ready, 1)
                pe.wait_ge(rstd_ready, n + 1)
                for w in range(NW):
                    last = nc.tensor.matmul(PS[:, 5 + w // 4, P * (w % 4):P * (w % 4) + P],
                                            small[:, 16 + w:17 + w].broadcast_to([P, P]), ident,
                                            start=True, stop=True)
                last.then_inc(nb_ready, 1)

            def split_ready(n):
                return lambda kt: pe.wait_ge(xn_ready, KT * n + kt + 1)

            pe.wait_ge(con_loaded, 16)
            norm(0)
            gemm(U_IN, 16, xn, split_ready(0))

            pe.wait_ge(acc_free, U_OUT + 2)
            for half in range(2):
                hs = slice(HALF * half, HALF * half + HALF)
                nc.tensor.matmul(PS[:, half, :], con[96:P, C_E1:C_E1 + P], proj[96:P, T_GK, hs], start=True, stop=True)
                last = nc.tensor.matmul(PS[:, 2 + half, :], con[96:P, C_E2:C_E2 + P], proj[96:P, T_GK, hs],
                                        start=True, stop=True)
            last.then_inc(MP_PE.sem, MP_PE.one("e12"))
            pe.wait_ge(MP_ACT.sem, MP_ACT.at("sq3", -1))
            for w in range(NW):
                nc.tensor.matmul(PS[:, 4, w:w + 1], mQ[:, win(w)], con[:, C_ONE:C_ONE + 1], start=True, stop=False)
                nc.tensor.matmul(PS[:, 4, w:w + 1], mK[0:HD, win(w)], con[0:HD, C_ONE:C_ONE + 1], start=False, stop=True)
            for w in range(NW):
                last = nc.tensor.matmul(PS[:, 4, NW + w:NW + w + 1], mP[0][:, win(w)], con[:, C_ONE:C_ONE + 1],
                                        start=True, stop=True)
            last.then_inc(MP_PE.sem, MP_PE.one("sums"))
            pe.wait_ge(MP_DVE.sem, MP_DVE.at("rstd", -1))
            for w in range(NW):
                last = nc.tensor.matmul(PS[:, 5 + w // 4, P * (w % 4):P * (w % 4) + P],
                                        small[:, 32 + w:33 + w].broadcast_to([P, P]), ident, start=True, stop=True)
            last.then_inc(MP_PE.sem, MP_PE.one("bq"))
            pe.wait_ge(MP_DVE.sem, MP_DVE.at("kr2", -1))
            for w in range(NW):
                last = nc.tensor.matmul(PS[:, w // 4, P * (w % 4):P * (w % 4) + P],
                                        small[:, 40 + w:41 + w].broadcast_to([P, P]), ident, start=True, stop=True)
            last.then_inc(MP_PE.sem, MP_PE.one("bkv"))
            pe.wait_ge(wv_loaded, 16)
            pe.wait_ge(MP_DVE.sem, MP_DVE.at("ckv", -1))
            for w in range(NW):
                if w >= 2:
                    pe.wait_ge(MP_ACT.sem, MP_ACT.at(f"v{w - 2}", -1))
                nc.tensor.matmul(PS[:, 4 + w % 2, :], proj[:, T_CKV, win(w)], wv_sb, start=True, stop=True).then_inc(
                    MP_PE.sem, MP_PE.one(f"v{w}"))

            pe.wait_ge(rp_dve, 6)
            pe.wait_ge(rp_act, 2)
            with pe.Fori(0, PAIRS) as p:
                def halves(k):
                    return slice(HALF * k, HALF * k + HALF)

                def head(hd, between):
                    h = 2 * p + hd
                    wq, o = 320 * hd, HD * hd
                    if hd == 0:
                        pe.wait_ge(headw_loaded, 16 * (p + 1))
                    pe.wait_ge(M_ACT.sem, M_ACT.at("t7", h - 1))
                    pe.wait_ge(M_DVE.sem, M_DVE.at("o7", h - 1))
                    for half in range(2):
                        nc.tensor.matmul(PS[:, half, :], headw_sb[:, wq:wq + P], proj[:, T_CQ, halves(half)],
                                         start=True, stop=False)
                        last = nc.tensor.matmul(PS[:, half, :], headw_sb[0:HD, wq + P:wq + 2 * P],
                                                proj[0:HD, T_CQWA, halves(half)], start=False, stop=True)
                    last.then_inc(M_PE.sem, M_PE.one("q"))
                    for half in range(2):
                        last = nc.tensor.matmul(PS[0:HD, 2 + half, :], headw_sb[:, wq + 2 * P:wq + 2 * P + HD],
                                                proj[:, T_CKV, halves(half)], start=True, stop=True)
                    last.then_inc(M_PE.sem, M_PE.one("k"))
                    between("qk")

                    def scores(q):
                        if q == 0:
                            pe.wait_ge(M_DVE.sem, M_DVE.at("q", h))
                            pe.wait_ge(M_ACT.sem, M_ACT.at("k", h))
                        if q >= 2:
                            pe.wait_ge(M_ACT.sem, M_ACT.at(f"e{q - 2}", h))
                        b = 2 * (q % 2)
                        for part in range(q // 4 + 1):
                            n = min(HALF, P * (q + 1) - HALF * part)
                            nc.tensor.matmul(PS[:, b + part, 0:n], mQ[:, win(q)], mK[:, HALF * part:HALF * part + n],
                                             start=True, stop=(part < q // 4))
                        nc.tensor.matmul(PS[:, b + q // 4, P * (q % 4):P * (q % 4) + P], con[0:1, C_RA:C_RA + P],
                                         con[0:1, C_RB:C_RB + P], start=False, stop=True).then_inc(
                            M_PE.sem, M_PE.one(f"s{q}"))

                    def turn(q):
                        pe.wait_ge(M_ACT.sem, M_ACT.at(f"e{q}", h))
                        if q >= 1:
                            pe.wait_ge(M_ACT.sem, M_ACT.at(f"t{q - 1}", h))
                        elif hd == 0:
                            pe.wait_ge(MO_DVE.sem, MO_DVE.at("out", p - 1))
                        for k in range(q + 1):
                            last = nc.tensor.transpose(PS[:, 4 + k // 4, P * (k % 4):P * (k % 4) + P],
                                                       mP[q % 2][:, win(k)], ident)
                        last.then_inc(M_PE.sem, M_PE.one(f"t{q}"))

                    def values(q):
                        pe.wait_ge(M_ACT.sem, M_ACT.at(f"t{q}", h))
                        if q >= 1:
                            pe.wait_ge(M_DVE.sem, M_DVE.at(f"o{q - 1}", h))
                        for k in range(q + 1):
                            last = nc.tensor.matmul(PS[:, 6, 0:HD], mPT[q % 2][:, win(k)],
                                                    mV[:, k, bass.ds(P * p + HD * hd, HD)],
                                                    start=(k == 0), stop=(k == q))
                        last.then_inc(M_PE.sem, M_PE.one(f"o{q}"))

                    scores(0)
                    between(0)
                    for q in range(1, NW):
                        scores(q)
                        turn(q - 1)
                        if q >= 2:
                            values(q - 2)
                        between(q)
                    turn(NW - 1)
                    between(8)
                    values(NW - 2)
                    values(NW - 1)

                def low_rank(name, rows, col, t, free):
                    if free is not None:
                        pe.wait_ge(R_ACT.sem, R_ACT.at(free, p))
                    nc.tensor.matmul(PS[:, 7, :], lora[rows, col:col + P], proj[rows, t, halves(int(name[2]))],
                                     start=True, stop=True).then_inc(R_PE.sem, R_PE.one(name))

                def head_sums(src):
                    for w in range(NW):
                        last = nc.tensor.matmul(PS[:, 7, 2 * w:2 * w + 2], src[:, win(w)],
                                                con[:, C_HO:C_HO + 2], start=True, stop=True)
                    return last

                def spread(half):
                    for w in range(4):
                        for h in range(2):
                            c = 16 + 8 * half + 2 * w + h
                            last = nc.tensor.matmul(PS[HD * h:HD * h + HD, 7, win(w)],
                                                    rSt[:, c:c + 1].broadcast_to([P, HD]), ident,
                                                    start=True, stop=True)
                    return last

                def block_sums(half, mask, src):
                    return nc.tensor.matmul(PS[:, 7, :], con[:, mask:mask + P], src[:, halves(half)],
                                            start=True, stop=True)

                def during_first(q):
                    wa = slice(64, P)
                    if q == "qk":
                        pe.wait_ge(lora_loaded, 16 * (p + 1))
                        pe.wait_ge(R_DVE.sem, R_DVE.at("out", p - 1))
                        low_rank("lw0", wa, 0, T_CQWA, None)
                        low_rank("lw1", wa, 0, T_CQWA, "tw0")
                    if q == 0:
                        low_rank("la0", wa, P, T_CQWA, "tw1")
                        low_rank("la1", wa, P, T_CQWA, "ta0")
                    if q == 1:
                        pe.wait_ge(R_ACT.sem, R_ACT.at("kksq", p))
                        head_sums(rBh).then_inc(R_PE.sem, R_PE.one("kks"))
                    if q == 3:
                        pe.wait_ge(R_POOL.sem, R_POOL.at("pow", p))
                        spread(0).then_inc(R_PE.sem, R_PE.one("kkb0"))
                    if q == 4:
                        pe.wait_ge(R_DVE.sem, R_DVE.at("nkk0", p))
                        spread(1).then_inc(R_PE.sem, R_PE.one("kkb1"))
                    if q == 6:
                        lower(0)
                    if q == 7:
                        lower(1)
                        lower(2)
                    if q == 8:
                        lower(3)

                def lower(n):
                    if n == 0:
                        pe.wait_ge(R_DVE.sem, R_DVE.at("bt", p))
                        pe.wait_ge(R_ACT.sem, R_ACT.at("afirst", p))
                    else:
                        pe.wait_ge(R_DVE.sem, R_DVE.at(f"al{n - 1}", p))
                    rows = slice(HD * (n % 2), HD * (n % 2) + HD)
                    for k in range(4):
                        w = 4 * (n // 2) + k
                        last = nc.tensor.matmul(PS[:, 7, win(k)], rAR[rows, w, 0, :], rB[rows, win(w)],
                                                start=True, stop=True)
                    last.then_inc(R_PE.sem, R_PE.one(f"al{n}"))

                head(0, during_first)
                def scores(w):
                    s, bb = w % 2, 4 * (w % 2)
                    if w == 0:
                        pe.wait_ge(R_POOL.sem, R_POOL.at("rt", p))
                        pe.wait_ge(R_DVE.sem, R_DVE.at("al3", p))
                        pe.wait_ge(R_ACT.sem, R_ACT.at("afirst", p))
                        pe.wait_ge(M_ACT.sem, M_ACT.at("t7", 2 * p))
                        pe.wait_ge(M_DVE.sem, M_DVE.at("o7", 2 * p))
                    if w >= 2:
                        pe.wait_ge(R_DVE.sem, R_DVE.at(f"mt1_{w - 2}", p))
                    for h in range(2):
                        rows = slice(HD * h, HD * h + HD)
                        nc.tensor.matmul(PS[:, bb + h, 0:P], rB[rows, win(w)], rAR[rows, w, 1, :],
                                         start=True, stop=True)
                        last = nc.tensor.matmul(PS[:, bb + h, P:3 * P], rK[rows, win(w)], rAR[rows, w, :, :],
                                                start=True, stop=True)
                    last.then_inc(R_PE.sem, R_PE.one(f"sc{w}"))

                def tokens(w):
                    bb = 4 * (w % 2)
                    if w == 0:
                        pe.wait_ge(R_POOL.sem, R_POOL.at("kh", p))
                        pe.wait_ge(R_ACT.sem, R_ACT.at("vc", p))
                    pe.wait_ge(R_DVE.sem, R_DVE.at(f"sc0_{w}", p))
                    nc.tensor.transpose(PS[:, bb, 0:P], rAR[:, w, 0, :], ident)
                    nc.tensor.transpose(PS[:, bb, P:2 * P], rBh[:, win(w)], ident)
                    nc.tensor.transpose(PS[:, bb, 2 * P:3 * P], rKh[:, win(w)], ident)
                    nc.tensor.transpose(PS[:, bb, 3 * P:4 * P], rT3[:, win(w)], ident).then_inc(
                        R_PE.sem, R_PE.one(f"tok{w}"))

                def a_v(w):
                    s, bb = w % 2, 4 * (w % 2)
                    pe.wait_ge(R_DVE.sem, R_DVE.at(f"sc1_{w}", p))
                    pe.wait_ge(R_ACT.sem, R_ACT.at(f"vz{w}", p))
                    for h in range(2):
                        last = nc.tensor.matmul(PS[:, bb + 1, HD * h:HD * h + HD], rSC[s][:, h, 1, :],
                                                rVZ[s][:, h, HD:P], start=True, stop=True)
                    last.then_inc(R_PE.sem, R_PE.one(f"akv{w}"))

                def double_q(lv, w):
                    s, bb = w % 2, 4 * (w % 2)
                    if lv == 0:
                        pe.wait_ge(xx_loaded[w // 2], 64 * (p + 1))
                        if w >= 2:
                            pe.wait_ge(R_DVE.sem, R_DVE.at(f"st{2 * (w - 2) + 1}", p))
                    else:
                        pe.wait_ge(R_DVE.sem, R_DVE.at(f"z{lv - 1}_{w}", p))
                    for h in range(2):
                        last = nc.tensor.matmul(PS[:, bb + 2, win(h)], rAL[2 * (w // 4) + h][:, w % 4, :], rXX[w][:, 1, h, :],
                                                start=True, stop=True)
                    last.then_inc(R_PE.sem, R_PE.one(f"q{lv}_{w}"))

                def double_z(lv, w):
                    s, bb = w % 2, 4 * (w % 2)
                    pe.wait_ge(R_DVE.sem, R_DVE.at(f"q{lv}_{w}", p))
                    if w >= 2 and lv == 0:
                        pe.wait_ge(R_ACT.sem, R_ACT.at(f"y{w - 2}", p))
                    if w == 1 and lv == 0:
                        pe.wait_ge(R_DVE.sem, R_DVE.at("bv1", p))
                    for h in range(2):
                        if lv < LEVELS - 1:
                            nc.tensor.matmul(PS[:, bb + 3, win(h)], rQ[s][:, h, :], rXX[w][:, 0, h, :],
                                             start=True, stop=True)
                        last = nc.tensor.matmul(PS[:, bb + 3, win(2 + h)], rXX[w][:, 0, h, :], rQ[s][:, h, :],
                                                start=True, stop=True)
                    last.then_inc(R_PE.sem, R_PE.one(f"z{lv}_{w}"))

                def solve(w):
                    s, bb = w % 2, 4 * (w % 2)
                    pe.wait_ge(R_ACT.sem, R_ACT.at(f"akv{w}", p))
                    pe.wait_ge(R_DVE.sem, R_DVE.at(f"z{LEVELS - 1}_{w}", p))
                    for h in range(2):
                        last = nc.tensor.matmul(PS[:, bb + 2, win(h)], rXX[w][:, 1, h, :], rAG[s][:, h, :],
                                                start=True, stop=True)
                    last.then_inc(R_PE.sem, R_PE.one(f"pg{w}"))

                def local(w):
                    s, bb = w % 2, 4 * (w % 2)
                    pe.wait_ge(R_ACT.sem, R_ACT.at(f"pg{w}", p))
                    for h in range(2):
                        nc.tensor.matmul(PS[:, bb + 3, win(h)], rPG[s][:, h, :], rSC[s][:, h, 0, :],
                                         start=True, stop=False)
                        nc.tensor.matmul(PS[:, bb + 3, win(h)], rVZ[s][:, h, :], rSC[s][:, h, 2, :],
                                         start=False, stop=False)
                        last = nc.tensor.matmul(PS[:, bb + 3, win(h)], con[:, C_SEL + P * h:C_SEL + P * h + P],
                                                rAR[:, w, 1, :], start=False, stop=True)
                    last.then_inc(R_PE.sem, R_PE.one(f"ry{w}"))

                def carry(w):
                    s, bb = w % 2, 4 * (w % 2)
                    for c in range(2):
                        rows = slice(CH * c, CH * c + CH)
                        for h in range(2):
                            hc = slice(HD * h, HD * h + HD)
                            nc.tensor.matmul(PS[:, bb + c, hc], rPG[s][rows, h, :], rBK[s][rows, 0, hc],
                                             start=True, stop=False)
                            last = nc.tensor.matmul(PS[:, bb + c, hc], rVZ[s][rows, h, :], rBK[s][rows, 1, hc],
                                                    start=False, stop=True)
                    last.then_inc(R_PE.sem, R_PE.one(f"mn{w}"))

                def state(c):
                    w = c // 2
                    bb = 4 * (w % 2)
                    pe.wait_ge(R_DVE.sem, R_DVE.at(f"mt1_{w}", p))
                    if c >= 1:
                        pe.wait_ge(R_DVE.sem, R_DVE.at(f"st{c - 1}", p))
                    for h in range(2):
                        last = nc.tensor.matmul(PS[0:HD, bb + 2, HD * h:HD * h + HD], rMT[w % 2][:, c % 2, h, :],
                                                rST[:, c, h, :], start=True, stop=True)
                    last.then_inc(R_PE.sem, R_PE.one(f"st{c}"))

                def outputs(c):
                    w = c // 2
                    s, bb = w % 2, 4 * (w % 2)
                    pe.wait_ge(R_ACT.sem, R_ACT.at(f"ry{w}", p))
                    if c >= 1:
                        pe.wait_ge(R_DVE.sem, R_DVE.at(f"st{c - 1}", p))
                    cc = slice(CH * (c % 2), CH * (c % 2) + CH)
                    for h in range(2):
                        last = nc.tensor.matmul(PS[HD * h:HD * h + HD, bb + 3, cc], rST[:, c, h, :],
                                                rRY[s][:, h, cc], start=True, stop=True)
                    last.then_inc(R_PE.sem, R_PE.one(f"y{c}"))

                for g in range(NW // 2):
                    ab = (2 * g, 2 * g + 1)
                    if g == 0:
                        for stage in (scores, tokens, a_v):
                            for w in ab:
                                stage(w)
                        pe.wait_ge(R_DVE.sem, R_DVE.at("al3", p))
                        block_sums(0, C_BO, rY).then_inc(R_PE.sem, R_PE.one("rk0"))
                        pe.wait_ge(R_DVE.sem, R_DVE.at("bv0", p))
                        block_sums(1, C_BO, rY).then_inc(R_PE.sem, R_PE.one("rk1"))
                    for lv in range(LEVELS):
                        for w in ab:
                            double_q(lv, w)
                        for w in ab:
                            double_z(lv, w)
                    for stage in (solve, local, carry):
                        for w in ab:
                            stage(w)
                    for k in range(4):
                        c, n = 4 * g + k, 2 * g + 2 + k % 2
                        if c < NC - 1:
                            state(c)
                        outputs(c)
                        if n < NW:
                            (scores if k < 2 else tokens)(n)
                    if g < NW // 2 - 1:
                        a_v(n - 1)
                        a_v(n)

                pe.wait_ge(R_ACT.sem, R_ACT.at("y7", p))
                pe.wait_ge(R_DVE.sem, R_DVE.at("st14", p))

                def during_second(q):
                    if q == "qk":
                        block_sums(0, C_BM, rY).then_inc(R_PE.sem, R_PE.one("mean0"))
                    if q == 0:
                        pe.wait_ge(R_DVE.sem, R_DVE.at("yc0", p))
                        block_sums(1, C_BM, rY).then_inc(R_PE.sem, R_PE.one("mean1"))
                    if q == 2:
                        pe.wait_ge(R_ACT.sem, R_ACT.at("ysq", p))
                        head_sums(rT1).then_inc(R_PE.sem, R_PE.one("vs"))
                    if q == 4:
                        pe.wait_ge(R_POOL.sem, R_POOL.at("gpow", p))
                        spread(0).then_inc(R_PE.sem, R_PE.one("vb0"))
                    if q == 5:
                        pe.wait_ge(R_DVE.sem, R_DVE.at("yn0", p))
                        spread(1).then_inc(R_PE.sem, R_PE.one("vb1"))
                    if q == 7:
                        pe.wait_ge(R_DVE.sem, R_DVE.at("yn1", p))
                        low_rank("lg0", slice(0, 96), 2 * P, T_GK, None)
                    if q == 8:
                        pe.wait_ge(R_DVE.sem, R_DVE.at("out0", p))
                        low_rank("lg1", slice(0, 96), 2 * P, T_GK, None)

                head(1, during_second)

                pe.wait_ge(MO_DVE.sem, MO_DVE.at("norm", p))
                for w in range(NW):
                    last = nc.tensor.transpose(PS[:, 4 + w // 4, P * (w % 4):P * (w % 4) + P], mO[:, w, :], ident)
                last.then_inc(MO_PE.sem, MO_PE.one("turn"))

            pe.wait_ge(mm_dve, 8)
            for w in range(2):
                last = nc.tensor.matmul(PS[:, 4, w:w + 1], cMs[:, win(w)], con[:, C_ONE:C_ONE + 1], start=True, stop=True)
            last.then_inc(mm_pe, 1)
            pe.wait_ge(mm_dve, 10)
            for w in range(2):
                last = nc.tensor.matmul(PS[:, 7, P * w + 64:P * w + 64 + P], small[:, 36 + w:37 + w].broadcast_to([P, P]),
                                        ident, start=True, stop=True)
            last.then_inc(mm_pe, 1)
            gemm(U_OUT, 8, xn, split_ready(1))

            with pe.Fori(0, 4) as i:
                for k in range(2):
                    pe.wait_ge(mem_split, 2 * i + (k + 1))
                    pe.wait_ge(acc_free, 2 * i + (U_MK + k + 1))
                    pe.wait_ge(mm_dve, 10 + 2 * KT)
                    for kt in range(KT):
                        for a, b in ((0, 0), (0, 1), (1, 0)):
                            last = nc.tensor.matmul(PS[:, 2 * k, 0:MEM], wsp[:, k, kt, a, :], memn[:, kt, b, :],
                                                    start=(kt == 0 and (a, b) == (0, 0)), stop=(kt == KT - 1 and a == 1))
                    last.then_inc(acc_ready, 1)
            norm(1)
            def turn_values(u):
                pe.wait_ge(vt_copied, u + 1)
                for t in range(2):
                    last = nc.tensor.transpose(PS[:, 2 * (u % 2) + 1, win(t)], cVT[u % 2][:, win(t)], ident)
                last.then_inc(vt_turned, 1)

            for u in range(8):
                pe.wait_ge(mem_split, 8 + u + 1)
                pe.wait_ge(acc_free, U_MV + u + 1)
                for kt in range(KT):
                    for a, b in ((0, 0), (0, 1), (1, 0)):
                        last = nc.tensor.matmul(PS[:, 2 * (u % 2), 0:MEM], wsp[:, u % 2, kt, a, :], memn[:, kt, b, :],
                                                start=(kt == 0 and (a, b) == (0, 0)), stop=(kt == KT - 1 and a == 1))
                last.then_inc(acc_ready, 1)
                if u >= 1:
                    turn_values(u - 1)
            turn_values(7)
            gemm(U_Q, 8, xn, split_ready(2))

            pe.wait_ge(acc_free, U_O + 2)
            with pe.Fori(0, CA_HEADS // 2) as i:
                def cscores(g):
                    a, j = g // 4, g % 4
                    if j == 0:
                        pe.wait_ge(ca_stage, 8 * i + 4 * (a + 1))
                    if g >= 2:
                        pe.wait_ge(C_ACT.sem, C_ACT.at(f"e{g - 2}", i))
                    else:
                        pe.wait_ge(C_ACT.sem, C_ACT.at(f"e{g + 6}", i - 1))
                    for w in range(2):
                        for k in range(2):
                            last = nc.tensor.matmul(PS[:, 4 + g % 2, MEM * w:MEM * w + MEM],
                                                    cQh[a][:, k, win(2 * j + w)],
                                                    cK[:, bass.ds(4 * i + (2 * a + k), 1), :].rearrange(
                                                        "p a t -> p (a t)"), start=(k == 0), stop=(k == 1))
                    last.then_inc(C_PE.sem, C_PE.one(f"s{g}"))

                def cturn(g):
                    pe.wait_ge(C_DVE.sem, C_DVE.at(f"p{g}", i))
                    if g >= 2:
                        pe.wait_ge(C_DVE.sem, C_DVE.at(f"c{g - 2}", i))
                    else:
                        pe.wait_ge(C_DVE.sem, C_DVE.at(f"c{g + 6}", i - 1))
                    for k in range(2):
                        for w in range(2):
                            last = nc.tensor.transpose(PS[:, 6 + g % 2, win(2 * k + w)], cP[g % 2][:, w, win(k)], ident)
                    last.then_inc(C_PE.sem, C_PE.one(f"t{g}"))

                def cvalues(o):
                    pe.wait_ge(C_DVE.sem, C_DVE.at(f"c{2 * o + 1}", i))
                    if o >= 2:
                        pe.wait_ge(C_DVE.sem, C_DVE.at(f"l{o - 2}", i))
                    else:
                        pe.wait_ge(C_DVE.sem, C_DVE.at(f"l{o + 2}", i - 1))
                    for m in range(2):
                        for k in range(2):
                            last = nc.tensor.matmul(PS[:, 2 * (o % 2) + m, :], cVh[o // 2][:, k, win(m)],
                                                    cPT[o % 2][:, k, :], start=(k == 0), stop=(k == 1))
                    last.then_inc(C_PE.sem, C_PE.one(f"o{o}"))

                cscores(0)
                for g in range(8):
                    if g < 7:
                        cscores(g + 1)
                    cturn(g)
                    if g in (2, 4, 6):
                        cvalues(g // 2 - 1)
                cvalues(3)

            def ca_ready(kt):
                pe.wait_ge(C_DVE.sem, C_DVE.at("l3", 1))

            gemm(U_O, 8, xn, ca_ready)
            norm(2)

            with pe.Fori(0, 4) as c:
                with pe.Fori(0, 4) as i:
                    for k in range(2):
                        unit(16 * c + 2 * i + (U_MLP + k), k, xn, split_ready(3))
                with pe.Fori(0, 4) as i:
                    for k in range(2):
                        unit(16 * c + 2 * i + (U_MLP + 8 + k), k, hid,
                             lambda kt: pe.wait_ge(hid_ready, 8 * c + kt + 3))
            norm(3)

        @block.scalar
        def _(act):
            for st in (M_ACT, MO_ACT, R_ACT, C_ACT):
                nc.scalar.sem_inc(st.sem, st.n)

            def square(i, src):
                nc.scalar.activation(tmp[:, i % 2, :], src, ACT.Square).then_inc(sq_ready, 1)

            def norm(n):
                act.wait_ge(var_ready, n + 1)
                nc.scalar.activation(small[:, 8:16], small[:, 0:8], ACT.Sqrt).then_inc(std_ready, 1)

            def heads(n):
                for kt in range(KT):
                    act.wait_ge(scaled, KT * n + kt + 1)
                    nc.scalar.copy(xn[:, kt, 0, :], tmp[:, kt % 2, :]).then_inc(head_ready, 1)

            for kt in range(KT):
                act.wait_ge(x_loaded[kt], 16)
                if kt >= 2:
                    act.wait_ge(sq_added, kt - 1)
                square(kt, H[:, kt, :])
            norm(0)
            heads(0)

            act.wait_ge(acc_free, U_OUT + 2)
            act.wait_ge(acc_ready, U_OUT + 2)
            nc.scalar.activation(mQ, proj[:, T_CQ, :], ACT.Square).then_inc(MP_ACT.sem, MP_ACT.one("sq1"))
            nc.scalar.activation(mK[0:HD], proj[0:HD, T_CQWA, :], ACT.Square).then_inc(MP_ACT.sem, MP_ACT.one("sq2"))
            nc.scalar.activation(mP[0], proj[:, T_CKV, :], ACT.Square).then_inc(MP_ACT.sem, MP_ACT.one("sq3"))
            act.wait_ge(MP_DVE.sem, MP_DVE.at("clamp", -1))
            nc.scalar.activation(mSin, mT[0], ACT.Sin).then_inc(MP_ACT.sem, MP_ACT.one("sin"))
            act.wait_ge(MP_DVE.sem, MP_DVE.at("abs", -1))
            nc.scalar.activation(mCos, mT[1], ACT.Sin, bias=con[:, C_PI2:C_PI2 + 1], scale=-1.0).then_inc(
                MP_ACT.sem, MP_ACT.one("cos"))
            act.wait_ge(MP_DVE.sem, MP_DVE.at("var", -1))
            nc.scalar.activation(small[:, 16:32], small[:, 0:16], ACT.Sqrt).then_inc(MP_ACT.sem, MP_ACT.one("std"))
            for w in range(NW):
                act.wait_ge(MP_PE.sem, MP_PE.at(f"v{w}", -1))
                nc.scalar.copy(mV[:, w, :], PS[:, 4 + w % 2, :]).then_inc(MP_ACT.sem, MP_ACT.one(f"v{w}"))

            nc.scalar.activation(proj[64:96, T_CQWA, :], proj[64:96, T_CQWA, :], ACT.Tanh).then_inc(rp_act, 1)
            nc.scalar.activation(proj[0:96, T_GK, :], proj[0:96, T_GK, :], ACT.Tanh, scale=0.5).then_inc(rp_act, 1)

            act.wait_ge(MP_DVE.sem, MP_DVE.at("kr", -1))
            with act.Fori(0, PAIRS) as p:
                half_e = 0.5 * EXPM05

                def par(base):
                    return vech[:, bass.ds(p + base, 1)]

                def halves(k):
                    return slice(HALF * k, HALF * k + HALF)

                def head(hd, between):
                    h = 2 * p + hd
                    act.wait_ge(M_PE.sem, M_PE.at("k", h))
                    nc.scalar.copy(mK[0:HD], two(2)[0:HD]).then_inc(M_ACT.sem, M_ACT.one("k"))
                    between("qk")

                    def turned(q):
                        act.wait_ge(M_PE.sem, M_PE.at(f"t{q}", h))
                        if q >= 2:
                            act.wait_ge(M_PE.sem, M_PE.at(f"o{q - 2}", h))
                        else:
                            act.wait_ge(M_PE.sem, M_PE.at(f"o{q + 6}", h - 1))
                        nc.scalar.copy(mPT[q % 2][:, 0:P * (q + 1)], two(4)[:, 0:P * (q + 1)]).then_inc(
                            M_ACT.sem, M_ACT.one(f"t{q}"))

                    for q in range(NW):
                        n = P * (q + 1)
                        act.wait_ge(M_DVE.sem, M_DVE.at(f"b{q}", h))
                        if q >= 2:
                            act.wait_ge(M_PE.sem, M_PE.at(f"t{q - 2}", h))
                        else:
                            act.wait_ge(M_PE.sem, M_PE.at(f"t{q + 6}", h - 1))
                        nc.scalar.activation(mP[q % 2][:, 0:n], two(2 * (q % 2))[:, 0:n], ACT.Exp,
                                             bias=small[:, 8 + q:9 + q], scale=MLA_SCALE,
                                             accum_out=small[:, 16 + q:17 + q]).then_inc(M_ACT.sem, M_ACT.one(f"e{q}"))
                        if q >= 1:
                            turned(q - 1)
                        between(q)
                    turned(NW - 1)

                def during_first(q):
                    if q == "qk":
                        for k in range(2):
                            act.wait_ge(R_PE.sem, R_PE.at(f"lw{k}", p))
                            nc.scalar.sem_inc(act_turn, 1)
                            nc.scalar.activation(rT1[:, halves(k)], PS[:, 7, :], ACT.Tanh, bias=par(0),
                                                 scale=0.5).then_inc(R_ACT.sem, R_ACT.one(f"tw{k}"))
                    if q == 0:
                        for k in range(2):
                            act.wait_ge(R_PE.sem, R_PE.at(f"la{k}", p))
                            nc.scalar.sem_inc(act_turn, 1)
                            nc.scalar.activation(rK[:, halves(k)], PS[:, 7, :], ACT.Tanh, bias=par(4),
                                                 scale=0.5).then_inc(R_ACT.sem, R_ACT.one(f"ta{k}"))
                        act.wait_ge(R_DVE.sem, R_DVE.at("kk", p))
                        nc.scalar.activation(rBh, rY, ACT.Square).then_inc(R_ACT.sem, R_ACT.one("kksq"))
                        nc.scalar.activation(rT2, rT1, ACT.Exp, bias=con[:, C_EM:C_EM + 1], scale=-half_e).then_inc(
                            R_ACT.sem, R_ACT.one("dec"))
                        nc.scalar.activation(rT3, rT1, ACT.Exp, bias=con[:, C_EP:C_EP + 1], scale=half_e).then_inc(
                            R_ACT.sem, R_ACT.one("dnv"))
                    if q == 5:
                        act.wait_ge(R_DVE.sem, R_DVE.at("nkk1", p))
                        nc.scalar.copy(rAR[:, :, 0, :].rearrange("p w (c t) -> p w c t", c=2)[:, :, :, 0],
                                       rY.rearrange("p (w c t) -> p w c t", w=NW, c=2)[:, :, :, 0]).then_inc(
                            R_ACT.sem, R_ACT.one("afirst"))
                        wt = rW.rearrange("p (c t) -> p c t", c=NC)[:, :, CH - 1]
                        nc.scalar.copy(rWT[:, :, 0], wt[0:HD]).then_inc(R_ACT.sem, R_ACT.one("wt0"))
                        nc.scalar.copy(rWT[:, :, 1], wt[HD:P]).then_inc(R_ACT.sem, R_ACT.one("wt1"))

                head(0, during_first)
                act.wait_ge(R_DVE.sem, R_DVE.at("bt", p))
                nc.scalar.copy(rT3, proj[:, bass.ds(p + T_V, 1), :].rearrange("p a t -> p (a t)")).then_inc(
                    R_ACT.sem, R_ACT.one("vc"))

                def tokens(w):
                    s, bb = w % 2, 4 * (w % 2)
                    tok = PS[:, bb, :].rearrange("p (k h n) -> p k h n", k=4, h=2)
                    act.wait_ge(R_PE.sem, R_PE.at(f"tok{w}", p))
                    nc.scalar.copy(rAG[s][:, :, 0:HD], tok[:, 0]).then_inc(R_ACT.sem, R_ACT.one(f"ag{w}"))
                    nc.scalar.copy(rBK[s].rearrange("p k (h n) -> p k h n", h=2), tok[:, 1:3]).then_inc(
                        R_ACT.sem, R_ACT.one(f"bk{w}"))
                    nc.scalar.copy(rVZ[s][:, :, HD:P], tok[:, 3]).then_inc(R_ACT.sem, R_ACT.one(f"vz{w}"))

                def a_v(w):
                    s, bb = w % 2, 4 * (w % 2)
                    act.wait_ge(R_PE.sem, R_PE.at(f"akv{w}", p))
                    nc.scalar.copy(rAG[s][:, :, HD:P], PS[:, bb + 1, 0:P].rearrange("p (h n) -> p h n", h=2)
                                   ).then_inc(R_ACT.sem, R_ACT.one(f"akv{w}"))

                for g in range(NW // 2):
                    ab = (2 * g, 2 * g + 1)
                    if g == 0:
                        for stage in (tokens, a_v):
                            for w in ab:
                                stage(w)
                    for w in ab:
                        s, bb = w % 2, 4 * (w % 2)
                        act.wait_ge(R_PE.sem, R_PE.at(f"pg{w}", p))
                        nc.scalar.copy(rPG[s].rearrange("p h n -> p (h n)"), PS[:, bb + 2, 0:256]).then_inc(
                            R_ACT.sem, R_ACT.one(f"pg{w}"))
                    for w in ab:
                        s, bb = w % 2, 4 * (w % 2)
                        act.wait_ge(R_PE.sem, R_PE.at(f"ry{w}", p))
                        nc.scalar.copy(rRY[s].rearrange("p h n -> p (h n)"), PS[:, bb + 3, 0:256]).then_inc(
                            R_ACT.sem, R_ACT.one(f"ry{w}"))
                    for w in ab:
                        act.wait_ge(R_PE.sem, R_PE.at(f"y{2 * w + 1}", p))
                        nc.scalar.copy(rY[:, win(w)], PS[:, 4 * (w % 2) + 3, 0:P]).then_inc(
                            R_ACT.sem, R_ACT.one(f"y{w}"))
                    if g < NW // 2 - 1:
                        for stage in (tokens, a_v):
                            for w in ab:
                                stage(w + 2)

                def during_second(q):
                    if q == 1:
                        act.wait_ge(R_DVE.sem, R_DVE.at("yc1", p))
                        nc.scalar.activation(rT1, rY, ACT.Square).then_inc(R_ACT.sem, R_ACT.one("ysq"))

                head(1, during_second)
                act.wait_ge(MO_DVE.sem, MO_DVE.at("var", p))
                nc.scalar.activation(mSt, mSt, ACT.Sqrt).then_inc(MO_ACT.sem, MO_ACT.one("std"))

            for kt in range(KT):
                act.wait_ge(R_DVE.sem, R_DVE.at("out", PAIRS - 1))
                act.wait_ge(MO_DVE.sem, MO_DVE.at("out", PAIRS - 1))
                nc.scalar.copy(xn[:, kt, 0, :], mixed(kt)).then_inc(head_ready, 1)

            act.wait_ge(mem_loaded, 16)
            nc.scalar.activation(cMt, cMem, ACT.Square).then_inc(mm_act, 1)

            def residual_squares(u0, n):
                with act.Fori(0, 4) as i:
                    for k in range(2):
                        act.wait_ge(h_added, 2 * i + (u0 + k + 1))
                        act.wait_ge(sq_added, 2 * i + (KT * n + k - 1))
                        square(k, H[:, bass.ds(2 * i + k, 1), :].rearrange("p a t -> p (a t)"))

            act.wait_ge(mm_dve, 9)
            nc.scalar.activation(small[:, 34:36], small[:, 32:34], ACT.Sqrt).then_inc(mm_act, 1)
            for kt in range(KT):
                act.wait_ge(mm_dve, 10 + kt + 1)
                nc.scalar.copy(memn[:, kt, 0, :], cMt[:, kt, :]).then_inc(mm_act, 1)
            def value_columns(u):
                act.wait_ge(acc_ready, U_MV + u + 3)
                nc.scalar.copy(cVT[u % 2], PS[:, 2 * (u % 2), 0:MEM]).then_inc(vt_copied, 1)

            def value_rows(u):
                act.wait_ge(vt_turned, u + 1)
                nc.scalar.copy(cV[:, :, win(u)], PS[:, 2 * (u % 2) + 1, 0:MEM].rearrange(
                    "p (t n) -> p t n", t=2)).then_inc(acc_free, 1)

            residual_squares(0, 1)
            with act.Fori(0, 4) as i:
                for k in range(2):
                    act.wait_ge(acc_ready, 2 * i + (U_MK + k + 3))
                    nc.scalar.copy(cK[:, bass.ds(2 * i + k, 1), :].rearrange("p a t -> p (a t)"),
                                   PS[:, 2 * k, 0:MEM]).then_inc(acc_free, 1)
            norm(1)
            for kt in range(KT):
                act.wait_ge(scaled, KT + kt + 1)
                nc.scalar.copy(xn[:, kt, 0, :], tmp[:, kt % 2, :]).then_inc(head_ready, 1)
                act.wait_ge(raw_loaded[kt % 2], 16 * ((U_MV + kt) // 2 + 1))
                act.wait_ge(acc_ready, U_MV + kt + 1)
                nc.scalar.copy(wsp[:, kt % 2, :, 0, :], wraw[:, kt % 2, :].rearrange(
                    "p (k n) -> p k n", k=KT)).then_inc(mem_head, 1)
                if kt >= 1:
                    value_columns(kt - 1)
                if kt >= 2:
                    value_rows(kt - 2)
            value_columns(7)
            value_rows(6)
            value_rows(7)
            with act.Fori(0, 4) as i:
                for k in range(2):
                    act.wait_ge(acc_ready, 2 * i + (U_Q + k + 3))
                    nc.scalar.copy(cQ[:, bass.ds(2 * i + k, 1), :].rearrange("p a t -> p (a t)"),
                                   two(2 * k)).then_inc(acc_free, 1)

            with act.Fori(0, CA_HEADS // 2) as i:
                def cheads(o):
                    act.wait_ge(C_PE.sem, C_PE.at(f"o{o}", i))
                    half = HALF * (o % 2)
                    nc.scalar.copy(xn[:, bass.ds(4 * i + 2 * (o // 2), 2), 0, half:half + HALF],
                                   PS[:, 2 * (o % 2):2 * (o % 2) + 2, :]).then_inc(C_ACT.sem, C_ACT.one(f"h{o}"))

                for g in range(8):
                    act.wait_ge(C_DVE.sem, C_DVE.at(f"b{g}", i))
                    if g >= 2:
                        act.wait_ge(C_PE.sem, C_PE.at(f"t{g - 2}", i))
                    else:
                        act.wait_ge(C_PE.sem, C_PE.at(f"t{g + 6}", i - 1))
                    for w in range(2):
                        c = 2 * g + w
                        e = nc.scalar.activation(cP[g % 2][:, w, :], PS[:, 4 + g % 2, MEM * w:MEM * w + MEM], ACT.Exp,
                                                 bias=cBias[:, c:c + 1], scale=CA_SCALE, accum_out=cSum[:, c:c + 1])
                    e.then_inc(C_ACT.sem, C_ACT.one(f"e{g}"))
                    if g in (3, 5, 7):
                        cheads(g // 2 - 1)
                cheads(3)

            residual_squares(8, 2)
            norm(2)
            heads(2)

            def hidden(c):
                with act.Fori(0, 4) as i:
                    for k in range(2):
                        n = 8 * c + 2 * i
                        act.wait_ge(acc_ready, 16 * c + 2 * i + (U_MLP + k + 3))
                        act.wait_ge(hid_ready, n + (k + 1))
                        nc.scalar.activation(tmp[:, k, :], two(2 * k), ACT.Relu).then_inc(relu_ready, 1)
                        act.wait_ge(hsq_ready, n + (k + 1))
                        nc.scalar.copy(hid[:, bass.ds(2 * i + k, 1), 0, :].rearrange("p a t -> p (a t)"),
                                       tmp[:, k, :]).then_inc(hhead_ready, 1)

            with act.Fori(0, 4) as c:
                hidden(c)
            residual_squares(40, 3)
            norm(3)

        @block.vector
        def _(dve):
            nc.vector.sem_inc(acc_free, 2)
            nc.vector.sem_inc(hid_ready, 2)
            for st in (M_DVE, MO_DVE, R_DVE, C_DVE):
                nc.vector.sem_inc(st.sem, st.n)

            def norm(n):
                dve.wait_ge(nsum_ready, n + 1)
                nc.vector.tensor_scalar(small[:, 0:8], PS[:, 4, 0:NW], 1.0 / D, EPS, ALU.mult, ALU.add).then_inc(
                    var_ready, 1)
                dve.wait_ge(std_ready, n + 1)
                nc.vector.reciprocal(small[:, 16:24], small[:, 8:16]).then_inc(rstd_ready, 1)

            def scale_and_split(n, pas, gain, between=lambda kt: None):
                def rest(kt):
                    dve.wait_ge(head_ready, KT * pas + kt + 1)
                    nc.vector.tensor_tensor(xn[:, kt, 1, :], tmp[:, kt % 2, :], xn[:, kt, 0, :].bitcast(F32),
                                            ALU.subtract).then_inc(xn_ready, 1)

                dve.wait_ge(nb_ready, n + 1)
                for kt in range(KT):
                    if kt >= 2:
                        dve.wait_ge(xn_ready, KT * pas + kt - 1)
                    nc.vector.scalar_tensor_tensor(tmp[:, kt % 2, :], H[:, kt, :], vec[:, gain + kt:gain + kt + 1],
                                                   two(5), ALU.mult, ALU.mult).then_inc(scaled, 1)
                    if kt >= 1:
                        rest(kt - 1)
                    between(kt)
                rest(KT - 1)

            for kt in range(KT):
                dve.wait_ge(sq_ready, kt + 1)
                if kt == 0:
                    nc.vector.tensor_copy(ssum[:, :], tmp[:, 0, :]).then_inc(sq_added, 1)
                else:
                    dve.wait_ge(sq_added, kt)
                    nc.vector.tensor_tensor(ssum[:, :], ssum[:, :], tmp[:, kt % 2, :], ALU.add).then_inc(sq_added, 1)
            dve.wait_ge(vec_loaded, 16)
            nc.vector.tensor_scalar(omu[:, :], vec[:, V_MU:V_MU + 16], -1.0, 1.0, ALU.mult, ALU.add).then_inc(vec_made, 1)
            nc.vector.tensor_scalar(vech[:, 0:8], vec[:, V_W0:V_W0 + 8], 0.5, None, ALU.mult).then_inc(vec_made, 1)
            nc.vector.tensor_scalar(vech[:, 8:12], vec[:, V_KA:V_KA + 4], 0.5, None, ALU.mult).then_inc(vec_made, 1)
            norm(0)
            scale_and_split(0, 0, V_MIX)

            dve.wait_ge(vec_made, 3)
            with dve.Fori(0, 8) as i:
                for k in range(2):
                    u = 2 * i + k
                    cur = proj[:, bass.ds(u, 1), :].rearrange("p a t -> p (a t)")
                    rest = proj[:, bass.ds(u, 1), 1:S].rearrange("p a t -> p (a t)")
                    dve.wait_ge(acc_ready, u + 3)
                    nc.vector.tensor_scalar(cur, two(2 * k), omu[:, bass.ds(u, 1)], None, ALU.mult).then_inc(proj_part, 1)
                    dve.wait_ge(proj_part, u + 1)
                    nc.vector.scalar_tensor_tensor(rest, two(2 * k)[:, 0:S - 1], vec[:, bass.ds(u + V_MU, 1)], rest,
                                                   ALU.mult, ALU.add).then_inc(acc_free, 1)

            def mp(ins, name):
                ins.then_inc(MP_DVE.sem, MP_DVE.one(name))

            def after(name):
                dve.wait_ge(MP_DVE.sem, MP_DVE.at(name, -1))

            dve.wait_ge(con_loaded, 16)
            dve.wait_ge(pos_loaded, 16)
            mp(nc.vector.tensor_copy(mT[0], posi), "posf")
            after("posf")
            mp(nc.vector.tensor_scalar(mT[0], mT[0], con[:, C_INV:C_INV + 1], None, ALU.mult), "ang")
            after("ang")
            mp(nc.vector.tensor_scalar(mT[1], mT[0], 1.0 / (2 * math.pi), MAGIC, ALU.mult, ALU.add), "turns")
            after("turns")
            mp(nc.vector.tensor_scalar(mCos, mT[1], -MAGIC, -6.28125, ALU.add, ALU.mult), "m1")
            after("m1")
            mp(nc.vector.tensor_tensor(mT[0], mT[0], mCos, ALU.add), "r1")
            mp(nc.vector.tensor_scalar(mT[1], mT[1], -MAGIC, -(2 * math.pi - 6.28125), ALU.add, ALU.mult), "m2")
            after("m2")
            mp(nc.vector.tensor_tensor(mT[0], mT[0], mT[1], ALU.add), "r2")
            after("r2")
            mp(nc.vector.tensor_scalar(mT[0], mT[0], 3.1415925, -3.1415925, ALU.min, ALU.max), "clamp")
            after("clamp")
            mp(nc.vector.scalar_tensor_tensor(mT[1], mT[0], -1.0, mT[0], ALU.mult, ALU.max), "abs")
            dve.wait_ge(MP_PE.sem, MP_PE.at("sums", -1))
            mp(nc.vector.tensor_scalar(small[:, 0:8], PS[:, 4, 0:8], 1.0 / QR, EPS, ALU.mult, ALU.add), "var1")
            mp(nc.vector.tensor_scalar(small[:, 8:16], PS[:, 4, 8:16], 1.0 / KVR, EPS, ALU.mult, ALU.add), "var")
            dve.wait_ge(MP_ACT.sem, MP_ACT.at("std", -1))
            mp(nc.vector.reciprocal(small[:, 32:48], small[:, 16:32]), "rstd")
            mp(nc.vector.memset(mCS[0:HD], 1.0), "one")
            mp(nc.vector.tensor_copy(mCS[64:96], mCos[64:96]), "csc")
            mp(nc.vector.tensor_scalar(mCS[96:P], mSin[96:P], con[96:P, C_SGN:C_SGN + 1], None, ALU.mult), "css")
            dve.wait_ge(MP_PE.sem, MP_PE.at("e12", -1))
            mp(nc.vector.tensor_tensor(mT[0][HD:P], two(0)[HD:P], mCos[HD:P], ALU.mult), "kr1")
            mp(nc.vector.tensor_tensor(mT[1][HD:P], two(2)[HD:P], mSin[HD:P], ALU.mult), "kr2")
            after("kr2")
            mp(nc.vector.tensor_tensor(mK[HD:P], mT[0][HD:P], mT[1][HD:P], ALU.add), "kr")
            dve.wait_ge(MP_PE.sem, MP_PE.at("bq", -1))
            mp(nc.vector.scalar_tensor_tensor(proj[:, T_CQ, :], proj[:, T_CQ, :], vec[:, V_QN:V_QN + 1], two(5),
                                              ALU.mult, ALU.mult), "cq0")
            mp(nc.vector.scalar_tensor_tensor(proj[0:HD, T_CQWA, :], proj[0:HD, T_CQWA, :],
                                              vec[0:HD, V_QN + 1:V_QN + 2], two(5)[0:HD], ALU.mult, ALU.mult), "cq1")
            dve.wait_ge(MP_PE.sem, MP_PE.at("bkv", -1))
            mp(nc.vector.scalar_tensor_tensor(proj[:, T_CKV, :], proj[:, T_CKV, :], vec[:, V_KVN:V_KVN + 1], two(0),
                                              ALU.mult, ALU.mult), "ckv")

            nc.vector.memset(zeros, 0.0).then_inc(zeros_made, 1)
            dve.wait_ge(MP_DVE.sem, MP_DVE.at("ckv", -1))
            nc.vector.tensor_copy(rST[HD:P], ident[HD:P, HD:P].rearrange("p (a b n) -> p a b n", a=1, b=1)
                                  .broadcast_to([HD, NC, 2, HD])).then_inc(rp_dve, 1)
            nc.vector.memset(rST[0:HD, 0], 0.0).then_inc(rp_dve, 1)
            for s in range(2):
                nc.vector.memset(rVZ[s][:, :, 0:HD], 0.0).then_inc(rp_dve, 1)
            nc.vector.memset(ssum[HD:P, 0:512], 0.0).then_inc(rp_dve, 1)
            dve.wait_ge(rp_act, 2)
            nc.vector.tensor_scalar(proj[0:96, T_GK, :], proj[0:96, T_GK, :], 0.5, 0.5, ALU.mult, ALU.add).then_inc(
                rp_dve, 1)

            dve.wait_ge(zeros_stored, 32)
            with dve.Fori(0, PAIRS) as p:
                def r(ins, name):
                    ins.then_inc(R_DVE.sem, R_DVE.one(name))

                def own(name):
                    dve.wait_ge(R_DVE.sem, R_DVE.at(name, p))

                def of_act(name):
                    dve.wait_ge(R_ACT.sem, R_ACT.at(name, p))

                def of_pe(name):
                    dve.wait_ge(R_PE.sem, R_PE.at(name, p))

                def of_pool(name):
                    dve.wait_ge(R_POOL.sem, R_POOL.at(name, p))

                def tile(base):
                    return proj[:, bass.ds(p + base, 1), :].rearrange("p a t -> p (a t)")

                def half_tile(base, k):
                    return proj[:, bass.ds(p + base, 1), HALF * k:HALF * k + HALF].rearrange("p a t -> p (a t)")

                def par(base):
                    return vec[:, bass.ds(p + base, 1)]

                def chunks(ap):
                    return ap.rearrange("p (c t) -> p c t", c=NC)

                def halves(k):
                    return slice(HALF * k, HALF * k + HALF)

                def head(hd, between):
                    h = 2 * p + hd

                    def m(ins, name):
                        ins.then_inc(M_DVE.sem, M_DVE.one(name))

                    def mown(name):
                        dve.wait_ge(M_DVE.sem, M_DVE.at(name, h))

                    dve.wait_ge(M_PE.sem, M_PE.at("q", h))
                    m(nc.vector.tensor_tensor(mQ, two(0), mCS, ALU.mult), "q")

                    def row_max(q):
                        dve.wait_ge(M_PE.sem, M_PE.at(f"s{q}", h))
                        m(nc.vector.tensor_reduce(small[:, q:q + 1], two(2 * (q % 2))[:, 0:P * (q + 1)], AX_X,
                                                  ALU.max), f"m{q}")
                        mown(f"m{q}")
                        m(nc.vector.tensor_scalar(small[:, 8 + q:9 + q], small[:, q:q + 1], -MLA_SCALE, None,
                                                  ALU.mult), f"b{q}")

                    def divide(q):
                        m(nc.vector.reciprocal(small[:, 24 + q:25 + q], small[:, 16 + q:17 + q]), f"r{q}")
                        dve.wait_ge(M_PE.sem, M_PE.at(f"o{q}", h))
                        mown(f"r{q}")
                        m(nc.vector.tensor_scalar(mO[:, q, HD * hd:HD * hd + HD], PS[:, 6, 0:HD],
                                                  small[:, 24 + q:25 + q], None, ALU.mult), f"o{q}")
                        mown(f"o{q}")
                        o, c = mO[:, q, HD * hd:HD * hd + HD], 2 * q + hd
                        m(nc.vector.tensor_tensor(mOsq, o, o, ALU.mult), f"sq{q}")
                        mown(f"sq{q}")
                        m(nc.vector.tensor_reduce(mSt[:, c:c + 1], mOsq, AX_X, ALU.add), f"ss{q}")

                    row_max(0)
                    between(0)
                    for q in range(1, NW):
                        row_max(q)
                        if q >= 2:
                            divide(q - 2)
                        between(q)
                    between(8)
                    divide(NW - 2)
                    divide(NW - 1)

                of_pe("lw0")
                r(nc.vector.tensor_scalar(rY, tile(T_K), par(V_KK), None, ALU.mult), "kk")

                def during_first(q):
                    if q == 1:
                        r(nc.vector.memset(rKh, 0.0), "zk")
                        of_pe("kks")
                        r(nc.vector.tensor_scalar(rSt[:, 0:16], PS[:, 7, 0:16], 1e-24, None, ALU.max), "kkm")
                        r(nc.vector.memset(rBh, 0.0), "zb")
                    if q == 2:
                        of_act("dnv")
                        r(nc.vector.tensor_tensor(rWi, rT2, rT3, ALU.mult), "nw")
                        own("nw")
                        r(nc.vector.scalar_tensor_tensor(rT3, rWi, 2.0, rT3, ALU.subtract, ALU.mult,
                                                         reverse0=True), "dinv")
                        own("dinv")
                        r(nc.vector.tensor_copy(chunks(rBh)[:, :, 0:1], chunks(rT2)[:, :, 0:1]), "f1")
                        r(nc.vector.tensor_copy(chunks(rKh)[:, :, 0:1], chunks(rT3)[:, :, 0:1]), "f2")
                        own("f2")
                        r(nc.vector.memset(chunks(rT2)[:, :, 0:1], 0.0), "z1")
                        r(nc.vector.memset(chunks(rT3)[:, :, 0:1], 0.0), "z2")
                    if q == 3:
                        own("z2")
                        r(nc.vector.tensor_tensor_scan(rW, rT2, rBh, 0.0, ALU.mult, ALU.add), "W")
                        r(nc.vector.tensor_tensor_scan(rWi, rT3, rKh, 0.0, ALU.mult, ALU.add), "Wi")
                    if q == 4:
                        for k in range(2):
                            of_pe(f"kkb{k}")
                            r(nc.vector.scalar_tensor_tensor(rY[:, halves(k)], rY[:, halves(k)], -1.0, PS[:, 7, :],
                                                             ALU.mult, ALU.mult), f"nkk{k}")
                        own("nkk1")
                        r(nc.vector.tensor_tensor(
                            rAR[:, :, 0, :].rearrange("p w (c t) -> p w c t", c=2)[:, :, :, 1:CH],
                            rY.rearrange("p (w c t) -> p w c t", w=NW, c=2)[:, :, :, 1:CH],
                            rW.rearrange("p (w c t) -> p w c t", w=NW, c=2)[:, :, :, 0:CH - 1], ALU.mult), "at")
                    if q == 5:
                        of_act("ta1")
                        r(nc.vector.tensor_scalar(rT2, rK, -0.5, -0.5, ALU.mult, ALU.add), "na")
                        own("na")
                        r(nc.vector.tensor_tensor(rT3, rT2, rY, ALU.mult), "b")
                        own("b")
                        r(nc.vector.tensor_tensor(rB, rT3, rWi, ALU.mult), "bt")
                        r(nc.vector.tensor_scalar(rT1, rK, -1.0, vech[:, bass.ds(p + 8, 1)], ALU.add, ALU.mult),
                          "am")
                    if q == 6:
                        lower(0)
                        own("am")
                        r(nc.vector.scalar_tensor_tensor(rT1, rT1, 1.0, tile(T_K), ALU.add, ALU.mult), "k2")
                    if q == 7:
                        lower(1)
                        own("k2")
                        r(nc.vector.tensor_tensor(rK, rT1, rWi, ALU.mult), "kt")
                        lower(2)
                        of_act("afirst")
                        r(nc.vector.scalar_tensor_tensor(rY, tile(T_R), par(V_RK), rT1, ALU.mult, ALU.mult), "rk")
                        r(nc.vector.memset(sc_s[:, 2048:2304], 0.0), "x0")
                        own("x0")
                        r(nc.vector.memset(sc_s[:, 2048:2304:BLK + 1], 1.0), "x1")
                    if q == 8:
                        lower(3)

                def lower(n):
                    of_pe(f"al{n}")
                    r(nc.vector.tensor_tensor(
                        rAL[n], PS[:, 7, :].rearrange("p (a n) -> p a n", a=4),
                        con[:, C_ML:C_ML + P].rearrange("p (a n) -> p a n", a=1).broadcast_to([P, 4, P]), ALU.mult),
                        f"al{n}")

                def substitute(columns):
                    for j in columns:
                        shape = [P, BLK - 1 - j, j + 1]
                        below, part = bX[:, j + 1:BLK, 0:j + 1], bT[:, j + 1:BLK, 0:j + 1]
                        r(nc.vector.tensor_tensor(part, bA[:, j + 1:BLK, j:j + 1].broadcast_to(shape),
                                                  bX[:, j:j + 1, 0:j + 1].broadcast_to(shape), ALU.mult), f"xm{j}")
                        own(f"xm{j}")
                        r(nc.vector.tensor_tensor(below, below, part, ALU.add), f"xa{j}")
                        own(f"xa{j}")

                head(0, during_first)
                def masked_scores(w):
                    s, bb = w % 2, 4 * (w % 2)
                    of_pe(f"sc{w}")
                    for hh in range(2):
                        r(nc.vector.tensor_tensor(rSC[s][:, hh].rearrange("p k n -> p (k n)"),
                                                  PS[:, bb + hh, 0:3 * P], con[:, C_MS:C_MS + 3 * P], ALU.mult),
                          f"sc{hh}_{w}")

                for g in range(NW // 2):
                    ab = (2 * g, 2 * g + 1)
                    if g == 0:
                        for w in ab:
                            masked_scores(w)
                            if w == 0:
                                own("x1")
                                dve.wait_ge(a_blocks_loaded, 16 * (p + 1))
                            substitute(SUBST[w])
                    if g == 0:
                        r(nc.vector.tensor_copy(bXT, bX.rearrange("p i n -> p n i")), "xt")
                        for k in range(2):
                            of_pe(f"rk{k}")
                            r(nc.vector.tensor_tensor(rBV[:, halves(k)], PS[:, 7, :], half_tile(T_V, k), ALU.mult),
                              f"bv{k}")
                    for lv in range(LEVELS):
                        for w in ab:
                            s, bb = w % 2, 4 * (w % 2)
                            of_pe(f"q{lv}_{w}")
                            mask = con[:, C_BQ + P * lv:C_BQ + P * lv + P].rearrange("p (a n) -> p a n", a=1)
                            r(nc.vector.tensor_tensor(rQ[s], PS[:, bb + 2, 0:256].rearrange("p (h n) -> p h n", h=2),
                                                      mask.broadcast_to([P, 2, P]), ALU.mult), f"q{lv}_{w}")
                        for w in ab:
                            s, bb = w % 2, 4 * (w % 2)
                            of_pe(f"z{lv}_{w}")
                            lo = 0 if lv < LEVELS - 1 else 256
                            xx = rXX[w].rearrange("p a h n -> p (a h n)")[:, lo:512]
                            r(nc.vector.tensor_tensor(xx, PS[:, bb + 3, lo:512], xx, ALU.add), f"z{lv}_{w}")
                    for w in ab:
                        s, bb = w % 2, 4 * (w % 2)
                        of_pool(f"dg_{w}")
                        of_pe(f"mn{w}")
                        for c in range(2):
                            r(nc.vector.tensor_tensor(rMT[s][:, c].rearrange("p h n -> p (h n)"), PS[:, bb + c, 0:P],
                                                      rDg[s][:, c].rearrange("p h n -> p (h n)"), ALU.add),
                              f"mt{c}_{w}")
                    for k in range(4):
                        c, w = 4 * g + k, 2 * g + k // 2
                        if c < NC - 1:
                            of_pe(f"st{c}")
                            r(nc.vector.tensor_copy(rST[0:HD, c + 1].rearrange("p h n -> p (h n)"),
                                                    PS[0:HD, 4 * (w % 2) + 2, 0:P]), f"st{c}")
                        if k < 2 and g < NW // 2 - 1:
                            masked_scores(2 * g + 2 + k)

                def during_second(q):
                    if q in (0, 1):
                        k = q
                        of_pe(f"mean{k}")
                        r(nc.vector.tensor_tensor(rY[:, halves(k)], rY[:, halves(k)], PS[:, 7, :], ALU.subtract),
                          f"yc{k}")
                    if q == 3:
                        of_pe("vs")
                        r(nc.vector.tensor_scalar(rSt[:, 0:16], PS[:, 7, 0:16], 1.0 / HD, GN_EPS, ALU.mult,
                                                  ALU.add), "var")
                    if q in (5, 6):
                        k = q - 5
                        of_pe(f"vb{k}")
                        r(nc.vector.tensor_tensor(rT2[:, halves(k)], rY[:, halves(k)], PS[:, 7, :], ALU.mult),
                          f"yn{k}")
                    if q == 7:
                        own("yn1")
                        r(nc.vector.tensor_scalar(rT2, rT2, par(V_LW), par(V_LB), ALU.mult, ALU.add), "yl")
                        own("yl")
                        r(nc.vector.tensor_tensor(rT2, rT2, rBV, ALU.add), "yb")
                        own("yb")
                        of_pe("lg0")
                        r(nc.vector.tensor_tensor(half_tile(T_R, 0), rT2[:, halves(0)], PS[:, 7, :], ALU.mult), "out0")

                head(1, during_second)
                of_pe("lg1")
                r(nc.vector.tensor_tensor(half_tile(T_R, 1), rT2[:, halves(1)], PS[:, 7, :], ALU.mult), "out")

                def mo(ins, name):
                    ins.then_inc(MO_DVE.sem, MO_DVE.one(name))
                    dve.wait_ge(MO_DVE.sem, MO_DVE.at(name, p))

                o_all = mO.rearrange("p w (h n) -> p (w h) n", n=HD)
                dve.wait_ge(M_DVE.sem, M_DVE.at("ss7", 2 * p + 1))
                mo(nc.vector.tensor_scalar(mSt, mSt, 1.0 / HD, EPS, ALU.mult, ALU.add), "var")
                dve.wait_ge(MO_ACT.sem, MO_ACT.at("std", p))
                mo(nc.vector.reciprocal(mSt, mSt), "rstd")
                mo(nc.vector.tensor_tensor(o_all, o_all, mSt.rearrange("p (a n) -> p a n", n=1).broadcast_to(
                    [P, 16, HD]), ALU.mult), "norm")
                dve.wait_ge(MO_PE.sem, MO_PE.at("turn", p))
                mo(nc.vector.tensor_scalar(tile(T_K), two(4), par(V_ON), None, ALU.mult), "out")

            for kt in range(KT):
                dve.wait_ge(head_ready, KT + kt + 1)
                nc.vector.tensor_tensor(xn[:, kt, 1, :], mixed(kt), xn[:, kt, 0, :].bitcast(F32),
                                        ALU.subtract).then_inc(xn_ready, 1)

            dve.wait_ge(mm_act, 1)
            nc.vector.tensor_copy(cMs, cMt[:, 0, :]).then_inc(mm_dve, 1)
            for kt in range(1, KT):
                dve.wait_ge(mm_dve, kt)
                nc.vector.tensor_tensor(cMs, cMs, cMt[:, kt, :], ALU.add).then_inc(mm_dve, 1)

            def residual(u0, j0, n):
                nc.vector.memset(ssum[:, :], 0.0).then_inc(ssum_zero, 1)
                dve.wait_ge(ssum_zero, n)
                with dve.Fori(0, 4) as i:
                    for k in range(2):
                        tile = H[:, bass.ds(2 * i + k, 1), :].rearrange("p a t -> p (a t)")
                        dve.wait_ge(acc_ready, 2 * i + (u0 + k + 3))
                        nc.vector.tensor_tensor(tile, two(2 * k), tile, ALU.add).then_inc(h_added, 1)
                        dve.wait_ge(h_added, 2 * i + (j0 + k + 1))
                        nc.vector.sem_inc(acc_free, 1)
                        dve.wait_ge(sq_ready, 2 * i + (KT * n + k + 1))
                        dve.wait_ge(sq_added, 2 * i + (KT * n + k))
                        nc.vector.tensor_tensor(ssum[:, :], ssum[:, :], tmp[:, k, :], ALU.add).then_inc(sq_added, 1)

            dve.wait_ge(mm_pe, 1)
            nc.vector.tensor_scalar(small[:, 32:34], PS[:, 4, 0:2], 1.0 / D, EPS, ALU.mult, ALU.add).then_inc(mm_dve, 1)
            dve.wait_ge(mm_act, 2)
            nc.vector.reciprocal(small[:, 36:38], small[:, 34:36]).then_inc(mm_dve, 1)
            dve.wait_ge(mm_pe, 2)
            for kt in range(KT):
                nc.vector.scalar_tensor_tensor(cMt[:, kt, :], cMem[:, kt, :], vec[:, V_MEM + kt:V_MEM + kt + 1],
                                               PS[:, 7, 64:64 + MEM], ALU.mult, ALU.mult).then_inc(mm_dve, 1)
            for kt in range(KT):
                dve.wait_ge(mm_act, 2 + kt + 1)
                nc.vector.tensor_tensor(memn[:, kt, 1, :], cMt[:, kt, :], memn[:, kt, 0, :].bitcast(F32),
                                        ALU.subtract).then_inc(mm_dve, 1)
            for kt in range(KT):
                dve.wait_ge(x_loaded[kt], 32)
            residual(U_OUT, 0, 1)

            with dve.Fori(0, 4) as i:
                for k in range(2):
                    raw = wraw[:, k, :].rearrange("p (k n) -> p k n", k=KT)
                    dve.wait_ge(raw_loaded[k], 16 * (i + (U_MK // 2 + 1)))
                    dve.wait_ge(acc_ready, 2 * i + (U_MK + k + 1))
                    nc.vector.tensor_copy(wsp[:, k, :, 0, :], raw).then_inc(mem_head, 1)
                    dve.wait_ge(mem_head, 2 * i + (k + 1))
                    nc.vector.tensor_tensor(wsp[:, k, :, 1, :], raw, wsp[:, k, :, 0, :].bitcast(F32),
                                            ALU.subtract).then_inc(mem_split, 1)

            def value_weights(kt):
                raw = wraw[:, kt % 2, :].rearrange("p (k n) -> p k n", k=KT)
                dve.wait_ge(mem_head, 8 + kt + 1)
                nc.vector.tensor_tensor(wsp[:, kt % 2, :, 1, :], raw, wsp[:, kt % 2, :, 0, :].bitcast(F32),
                                        ALU.subtract).then_inc(mem_split, 1)

            norm(1)
            scale_and_split(1, 2, V_CA, value_weights)

            with dve.Fori(0, CA_HEADS // 2) as i:
                def c(ins, name):
                    ins.then_inc(C_DVE.sem, C_DVE.one(name))

                def own(name):
                    dve.wait_ge(C_DVE.sem, C_DVE.at(name, i))

                def crow_max(g):
                    cols = slice(2 * g, 2 * g + 2)
                    dve.wait_ge(C_PE.sem, C_PE.at(f"s{g}", i))
                    c(nc.vector.tensor_reduce(cMax[:, cols], PS[:, 4 + g % 2, :].rearrange("p (w n) -> p w n", w=2),
                                              AX_X, ALU.max), f"m{g}")
                    own(f"m{g}")
                    c(nc.vector.tensor_scalar(cBias[:, cols], cMax[:, cols], -CA_SCALE, None, ALU.mult), f"b{g}")

                def normalise(g):
                    cols = slice(2 * g, 2 * g + 2)
                    dve.wait_ge(C_ACT.sem, C_ACT.at(f"e{g}", i))
                    c(nc.vector.reciprocal(cInv[:, cols], cSum[:, cols]), f"r{g}")
                    own(f"r{g}")
                    c(nc.vector.tensor_tensor(cP[g % 2], cP[g % 2], cInv[:, cols].rearrange(
                        "p (w n) -> p w n", n=1).broadcast_to([P, 2, MEM]), ALU.mult), f"p{g}")

                def copy_cpt(g):
                    dve.wait_ge(C_PE.sem, C_PE.at(f"t{g}", i))
                    j = g % 4
                    c(nc.vector.tensor_copy(cPT[j // 2][:, :, 256 * (j % 2):256 * (j % 2) + 256],
                                            PS[:, 6 + g % 2, :].rearrange("p (k n) -> p k n", k=2)), f"c{g}")

                def crest(o):
                    dve.wait_ge(C_ACT.sem, C_ACT.at(f"h{o}", i))
                    half = HALF * (o % 2)
                    dst = xn[:, bass.ds(4 * i + 2 * (o // 2), 2), :, half:half + HALF]
                    c(nc.vector.tensor_tensor(dst[:, :, 1, :], PS[:, 2 * (o % 2):2 * (o % 2) + 2, :],
                                              dst[:, :, 0, :].bitcast(F32), ALU.subtract), f"l{o}")

                crow_max(0)
                for g in range(8):
                    normalise(g)
                    if g < 7:
                        crow_max(g + 1)
                    if g:
                        copy_cpt(g - 1)
                    if g in (4, 6):
                        crest(g // 2 - 2)
                copy_cpt(7)
                crest(2)
                crest(3)

            residual(U_O, 8, 2)
            norm(2)
            scale_and_split(2, 3, V_MLP)

            def hidden(c):
                with dve.Fori(0, 4) as i:
                    for k in range(2):
                        n = 8 * c + 2 * i
                        dve.wait_ge(relu_ready, n + (k + 1))
                        nc.vector.tensor_tensor(tmp[:, k, :], tmp[:, k, :], tmp[:, k, :], ALU.mult).then_inc(
                            hsq_ready, 1)
                        nc.vector.sem_inc(acc_free, 1)
                        dve.wait_ge(hhead_ready, n + (k + 1))
                        dve.wait_ge(hsq_ready, n + (k + 1))
                        dst = hid[:, bass.ds(2 * i + k, 1), :, :].rearrange("p a b t -> p (a b) t")
                        nc.vector.tensor_tensor(dst[:, 1, :], tmp[:, k, :], dst[:, 0, :].bitcast(F32),
                                                ALU.subtract).then_inc(hid_ready, 1)

            with dve.Fori(0, 3) as c:
                hidden(c)
                with dve.Fori(0, 4) as i:
                    for k in range(2):
                        tile = H[:, bass.ds(2 * i + k, 1), :].rearrange("p a t -> p (a t)")
                        dve.wait_ge(acc_ready, 16 * c + 2 * i + (U_MLP + 8 + k + 3))
                        nc.vector.tensor_tensor(tile, two(2 * k), tile, ALU.add).then_inc(h_added, 1)
                        dve.wait_ge(h_added, 8 * c + 2 * i + (16 + k + 1))
                        nc.vector.sem_inc(acc_free, 1)
            hidden(3)
            residual(UNITS - 8, 40, 3)
            norm(3)
            dve.wait_ge(nb_ready, 4)
            for kt in range(KT):
                nc.vector.scalar_tensor_tensor(proj[:, kt, :], H[:, kt, :], vec[:, V_FIN + kt:V_FIN + kt + 1], two(5),
                                               ALU.mult, ALU.mult).then_inc(out_scaled, 1)

        for st in STEPS:
            assert st.next > 0 and st.next % st.n == 0, st.names


def tiles(w, rows):
    k, n = w.shape
    return w.reshape(k // P, P, n // P, P).transpose(2, 1, 0, 3).reshape(n // P, P, k)


def layout(x, mem, positions, mix_norm, w_in_first, w_in_rest, shift_mu_first, shift_mu_rest,
           mla_q_norm, mla_w_uq, mla_kv_norm, mla_w_ukv, mla_out_norm,
           rwkv_w0, rwkv_w2, rwkv_a0, rwkv_a2, rwkv_g2, rwkv_v0, rwkv_v2,
           rwkv_k_k, rwkv_k_a, rwkv_r_k, rwkv_ln_w, rwkv_ln_b, w_out,
           ca_norm, mem_norm, ca_wq, ca_wkv, ca_wo,
           mlp_norm, mlp_w_up, mlp_w_down, final_norm):
    f32 = np.float32
    rw = 512
    mla = QR + KVR + ROPE
    at = mla + 3 * rw
    cols = np.concatenate([np.arange(0, QR), np.arange(at, at + 64), np.arange(QR, QR + KVR),
                           np.arange(at + 64, at + 160), np.arange(QR + KVR, mla), np.arange(mla, at)])
    w_in = np.asarray(w_in_first)[:, cols]
    mu = np.concatenate([np.zeros(mla, f32), np.asarray(shift_mu_first)])[cols]
    wkv = np.asarray(ca_wkv)[0]
    up, down = np.asarray(mlp_w_up)[0], np.asarray(mlp_w_down)[0]
    units = [tiles(w_in, D), tiles(np.asarray(w_out)[0], D), tiles(wkv[:, :D], D), tiles(wkv[:, D:], D),
             tiles(np.asarray(ca_wq)[0], D), tiles(np.asarray(ca_wo)[0], D)]
    for c in range(4):
        units += [tiles(up[:, D * c:D * c + D], D), tiles(down[D * c:D * c + D], D)]
    vecs = np.zeros((P, NV), f32)

    def put(col, v):
        v = np.asarray(v).reshape(-1, P).T
        vecs[:, col:col + v.shape[1]] = v

    for col, v in ((V_MIX, mix_norm), (V_CA, ca_norm), (V_MLP, mlp_norm), (V_FIN, final_norm), (V_MEM, mem_norm),
                   (V_MU, mu), (V_KVN, mla_kv_norm), (V_ON, mla_out_norm), (V_W0, rwkv_w0), (V_A0, rwkv_a0),
                   (V_KK, rwkv_k_k), (V_KA, rwkv_k_a), (V_RK, rwkv_r_k), (V_LW, rwkv_ln_w), (V_LB, rwkv_ln_b)):
        put(col, v)
    qn = np.asarray(mla_q_norm)[0]
    vecs[:, V_QN] = qn[:P]
    vecs[:QR - P, V_QN + 1] = qn[P:]
    uq = np.asarray(mla_w_uq)[0].reshape(QR, MLA_HEADS, HD + ROPE)
    swap = np.concatenate([np.arange(HD + ROPE), HD + np.arange(ROPE // 2, ROPE), HD + np.arange(ROPE // 2)])
    uq = uq[:, :, swap].transpose(1, 0, 2)
    ukv = np.asarray(mla_w_ukv)[0].reshape(KVR, MLA_HEADS, 2 * HD)
    headw = np.zeros((MLA_HEADS, P, 320), f32)
    headw[:, :, 0:P] = uq[:, :P]
    headw[:, :QR - P, P:2 * P] = uq[:, P:]
    headw[:, :, 2 * P:] = ukv[:, :, :HD].transpose(1, 0, 2)
    headw = headw.reshape(PAIRS, 2, P, 320).transpose(0, 2, 1, 3).reshape(PAIRS, P, 640)
    wv = ukv[:, :, HD:].reshape(KVR, MLA_HEADS * HD)
    lora = np.zeros((PAIRS, P, 384), f32)
    lora[:, 64:96, 0:P] = np.asarray(rwkv_w2)[0].reshape(32, PAIRS, P).transpose(1, 0, 2)
    lora[:, 96:128, P:2 * P] = np.asarray(rwkv_a2)[0].reshape(32, PAIRS, P).transpose(1, 0, 2)
    lora[:, 0:96, 2 * P:] = np.asarray(rwkv_g2)[0].reshape(96, PAIRS, P).transpose(1, 0, 2)
    return {
        "x": np.asarray(x)[0].T.reshape(KT, P, S), "mem": np.asarray(mem)[0].T.reshape(KT, P, MEM),
        "positions": np.asarray(positions), "weights": np.concatenate(units), "vectors": vecs,
        "constants": constants(), "head_weights": headw, "value_weights": wv, "lora": lora,
    }


def kernel(**inputs):
    import concourse.bacc as bacc
    from concourse.bass_utils import run_bass_kernel_spmd

    nc = bacc.Bacc("TRN2", target_bir_lowering=False, num_devices=1)
    arrays, args = {}, []
    for name, a in layout(**inputs).items():
        a = np.ascontiguousarray(a)
        arrays[f"in_{name}_dram"] = a
        args.append(nc.dram_tensor(f"in_{name}_dram", a.shape, mybir.dt.from_np(a.dtype), kind="ExternalInput").ap())
    args.append(nc.dram_tensor("out_0_dram", (KT, P, S), F32, kind="ExternalOutput").ap())
    build(nc, *args)
    r = run_bass_kernel_spmd(nc, [arrays], core_ids=[0])
    return np.ascontiguousarray(r.results[0]["out_0_dram"].reshape(1, D, S).transpose(0, 2, 1))
```
